# Optimizing a Trainium2 kernel written in Bass

```python
import math
import jax, jax.numpy as jnp
from jax import lax
import numpy as np

D_MODEL = 1024
BATCH = 1
SEQ = 256
DEPTH = 2
DEC_BATCH = 8
DEC_SEQ = 8
PAST_LEN = 1024
PAGE_SIZE = 128

N_AB = (DEPTH + 1) // 2
N_C = DEPTH // 2
POOL_WINDOWS = (2, 4, 8, 16)
POOL_GROUPS = len(POOL_WINDOWS)
D_A = D_MODEL // 4
POOL_GC = D_A // POOL_GROUPS
POOL_BUF = max(POOL_WINDOWS) - 1
SB_HEAD_DIM = 64
D_B = D_MODEL - D_A
SB_HEADS = D_B // SB_HEAD_DIM
Q_BLOCK = 128
SB_BIAS_LO = -9.0
SB_BIAS_HI = -6.0
D_AB_IN = D_A + 3 * D_B
D_INNER = 2 * D_MODEL
SSD_HEAD_DIM = 64
SSD_HEADS = D_INNER // SSD_HEAD_DIM
SSD_GROUPS = 4
SSD_STATE = 128
SSD_CONV = 4
SSD_CHUNK = 128
CONV_DIM = D_INNER + 2 * SSD_GROUPS * SSD_STATE
D_SSD_IN = D_INNER + CONV_DIM + SSD_HEADS
PEER_HEADS = 8
N_KEYS = 128
N_EXPERTS = N_KEYS * N_KEYS
PEER_TOPK = 16
D_KEY = 256
D_HALF = D_KEY // 2
TOK_BLOCK = 256
EPS = 1e-6

kernel_name = 'hybrid_pool_stickbreak_ssd_peer_decode_step'

def rmsnorm(x, g):
    xf = x.astype(jnp.float32)
    r = lax.rsqrt(jnp.mean(xf * xf, axis=-1, keepdims=True) + EPS)
    return (xf * r).astype(x.dtype) * g

def modulate(x, g, shift, scale):
    return rmsnorm(x, g) * (1 + scale[:, None, :]) + shift[:, None, :]

def pool_mixer(a, buf, start_pos, pool_w, pool_scale):
    bsz, t, _ = a.shape
    raw = jnp.concatenate([buf.astype(a.dtype), a], axis=1)
    full = raw.astype(jnp.float32)
    cs = jnp.concatenate([jnp.zeros_like(full[:, :1]), jnp.cumsum(full, axis=1)], axis=1)
    pos = start_pos + jnp.arange(t)
    hi = cs[:, POOL_BUF + 1:POOL_BUF + 1 + t]
    means = []
    for g, w in enumerate(POOL_WINDOWS):
        sl = slice(g * POOL_GC, (g + 1) * POOL_GC)
        lo = cs[:, POOL_BUF + 1 - w:POOL_BUF + 1 - w + t, sl]
        cnt = jnp.minimum(pos + 1, w).astype(jnp.float32)[None, :, None]
        means.append((hi[..., sl] - lo) / cnt)
    mean = jnp.stack(means, axis=2)
    diff = (mean - full[:, POOL_BUF:].reshape(bsz, t, POOL_GROUPS, POOL_GC)).astype(a.dtype)
    y = jnp.einsum('btgc,gcd->btgd', diff, pool_w).reshape(bsz, t, D_A) * pool_scale
    return y, raw[:, -POOL_BUF:]

def stick_breaking(q, k, v, q_pos, k_pos, bias):
    bsz, tq, h, dh = q.shape
    qb = min(Q_BLOCK, tq)
    nb = -(-tq // qb)
    pad = nb * qb - tq
    qp = jnp.pad(q, ((0, 0), (0, pad), (0, 0), (0, 0))).reshape(bsz, nb, qb, h, dh)
    qp = jnp.moveaxis(qp, 1, 0)
    pp = jnp.pad(q_pos, (0, pad), constant_values=-1).reshape(nb, qb)
    scale = dh ** -0.5
    bias_f = bias.astype(jnp.float32)[None, :, None, None]

    def block(args):
        qblk, pblk = args
        z = jnp.einsum('bqhd,bkhd->bhqk', qblk, k, preferred_element_type=jnp.float32) * scale + bias_f
        valid = k_pos[None, :] < pblk[:, None]
        log_keep = jnp.where(valid, jax.nn.log_sigmoid(-z), 0.0)
        after = lax.cumsum(log_keep, axis=3, reverse=True) - log_keep
        wts = jnp.where(valid, jnp.exp(jax.nn.log_sigmoid(z) + after), 0.0)
        return jnp.einsum('bhqk,bkhd->bqhd', wts.astype(v.dtype), v)

    out = lax.map(block, (qp, pp))
    return jnp.moveaxis(out, 0, 1).reshape(bsz, nb * qb, h, dh)[:, :tq]

def mixer_ab(h, start_pos, pool_buf, past_k, past_v, w_in, w_out, pool_w, pool_scale, sb_bias):
    bsz, t, _ = h.shape
    proj = h @ w_in
    a = proj[..., :D_A]
    q, k, v = jnp.split(proj[..., D_A:], 3, axis=-1)
    q = q.reshape(bsz, t, SB_HEADS, SB_HEAD_DIM)
    k = k.reshape(bsz, t, SB_HEADS, SB_HEAD_DIM)
    v = v.reshape(bsz, t, SB_HEADS, SB_HEAD_DIM)
    ya, new_buf = pool_mixer(a, pool_buf, start_pos, pool_w, pool_scale)
    q_pos = start_pos + jnp.arange(t)
    if past_k is None:
        k_all, v_all, k_pos = k, v, q_pos
    else:
        k_all = jnp.concatenate([past_k.astype(k.dtype), k], axis=1)
        v_all = jnp.concatenate([past_v.astype(v.dtype), v], axis=1)
        k_pos = jnp.arange(past_k.shape[1] + t)
    yb = stick_breaking(q, k_all, v_all, q_pos, k_pos, sb_bias).reshape(bsz, t, D_B)
    y = jnp.concatenate([ya, yb], axis=-1) @ w_out
    return y, k, v, new_buf

def causal_conv(u, buf, w, b):
    t = u.shape[1]
    full = jnp.concatenate([buf.astype(u.dtype), u], axis=1)
    y = b + sum(full[:, i:i + t] * w[i] for i in range(SSD_CONV))
    return y, full[:, -(SSD_CONV - 1):]

def ssd_scan(x, dt, a, b_in, c_in, h0):
    bsz, t = x.shape[0], x.shape[1]
    cl = min(SSD_CHUNK, t)
    nc = -(-t // cl)
    pad = nc * cl - t
    r = SSD_HEADS // SSD_GROUPS

    def padt(u):
        return jnp.pad(u.astype(jnp.float32), ((0, 0), (0, pad)) + ((0, 0),) * (u.ndim - 2))

    xc = padt(x).reshape(bsz, nc, cl, SSD_GROUPS, r, SSD_HEAD_DIM)
    dtc = padt(dt).reshape(bsz, nc, cl, SSD_GROUPS, r)
    bc = padt(b_in).reshape(bsz, nc, cl, SSD_GROUPS, SSD_STATE)
    cc = padt(c_in).reshape(bsz, nc, cl, SSD_GROUPS, SSD_STATE)
    acs = jnp.cumsum(dtc * a.astype(jnp.float32).reshape(SSD_GROUPS, r), axis=2)
    xdt = xc * dtc[..., None]
    causal = jnp.tril(jnp.ones((cl, cl), dtype=bool))
    seg = acs[:, :, :, None] - acs[:, :, None, :]
    decay = jnp.exp(jnp.where(causal[:, :, None, None], seg, -jnp.inf))
    cb = jnp.einsum('bclgn,bcsgn->bclsg', cc, bc)
    y_diag = jnp.einsum('bclsgr,bcsgrp->bclgrp', cb[..., None] * decay, xdt)
    to_end = jnp.exp(acs[:, :, -1:] - acs)
    chunk_states = jnp.einsum('bclgn,bclgr,bclgrp->bcgrpn', bc, to_end, xdt)
    chunk_decay = jnp.exp(acs[:, :, -1])

    def step(hc, inp):
        st, dec = inp
        return hc * dec[..., None, None] + st, hc

    h_last, h_in = lax.scan(step, h0.reshape(bsz, SSD_GROUPS, r, SSD_HEAD_DIM, SSD_STATE),
                            (jnp.moveaxis(chunk_states, 1, 0), jnp.moveaxis(chunk_decay, 1, 0)))
    h_in = jnp.moveaxis(h_in, 0, 1)
    y_off = jnp.einsum('bclgn,bcgrpn,bclgr->bclgrp', cc, h_in, jnp.exp(acs))
    y = (y_diag + y_off).reshape(bsz, nc * cl, SSD_HEADS, SSD_HEAD_DIM)[:, :t]
    return y, h_last.reshape(bsz, SSD_HEADS, SSD_HEAD_DIM, SSD_STATE)

def mixer_ssd(h, conv_buf, ssm_state, w_in, conv_w, conv_b, dt_bias, a_log, d_skip, norm_g, w_out):
    bsz, t, _ = h.shape
    proj = h @ w_in
    z = proj[..., :D_INNER]
    xbc = proj[..., D_INNER:D_INNER + CONV_DIM]
    dt_raw = proj[..., D_INNER + CONV_DIM:]
    xbc, new_conv = causal_conv(xbc, conv_buf, conv_w, conv_b)
    xbc = jax.nn.silu(xbc)
    xs = xbc[..., :D_INNER].reshape(bsz, t, SSD_HEADS, SSD_HEAD_DIM)
    b_in = xbc[..., D_INNER:D_INNER + SSD_GROUPS * SSD_STATE].reshape(bsz, t, SSD_GROUPS, SSD_STATE)
    c_in = xbc[..., D_INNER + SSD_GROUPS * SSD_STATE:].reshape(bsz, t, SSD_GROUPS, SSD_STATE)
    dt = jax.nn.softplus(dt_raw.astype(jnp.float32) + dt_bias.astype(jnp.float32))
    a = -jnp.exp(a_log.astype(jnp.float32))
    y, h_new = ssd_scan(xs, dt, a, b_in, c_in, ssm_state.astype(jnp.float32))
    y = y + xs.astype(jnp.float32) * d_skip.astype(jnp.float32)[:, None]
    y = y.reshape(bsz, t, D_INNER) * jax.nn.silu(z.astype(jnp.float32))
    y = rmsnorm(y.reshape(bsz, t, SSD_GROUPS, D_INNER // SSD_GROUPS),
                norm_g.reshape(SSD_GROUPS, D_INNER // SSD_GROUPS)).reshape(bsz, t, D_INNER)
    return y.astype(h.dtype) @ w_out, new_conv, h_new.astype(ssm_state.dtype)

def peer_ffn(h, wq, k1, k2, u_tab, v_tab):
    bsz, t, d = h.shape
    n = bsz * t
    nb = -(-n // TOK_BLOCK)
    xt = jnp.pad(h.reshape(n, d), ((0, nb * TOK_BLOCK - n), (0, 0))).reshape(nb, TOK_BLOCK, d)

    def block(xb):
        q = (xb @ wq).reshape(TOK_BLOCK, PEER_HEADS, D_KEY)
        s1 = jnp.einsum('thd,hkd->thk', q[..., :D_HALF], k1, preferred_element_type=jnp.float32)
        s2 = jnp.einsum('thd,hkd->thk', q[..., D_HALF:], k2, preferred_element_type=jnp.float32)
        v1, i1 = lax.top_k(s1, PEER_TOPK)
        v2, i2 = lax.top_k(s2, PEER_TOPK)
        cand = (v1[..., :, None] + v2[..., None, :]).reshape(TOK_BLOCK, PEER_HEADS, PEER_TOPK * PEER_TOPK)
        cidx = (i1[..., :, None] * N_KEYS + i2[..., None, :]).reshape(TOK_BLOCK, PEER_HEADS, PEER_TOPK * PEER_TOPK)
        best, sel = lax.top_k(cand, PEER_TOPK)
        eidx = jnp.take_along_axis(cidx, sel, axis=-1)
        gate = jax.nn.softmax(best, axis=-1)
        act = jax.nn.gelu(jnp.einsum('thkd,td->thk', u_tab[eidx], xb, preferred_element_type=jnp.float32),
                          approximate=False)
        return jnp.einsum('thk,thkd->td', (gate * act).astype(v_tab.dtype), v_tab[eidx])

    return lax.map(block, xt).reshape(nb * TOK_BLOCK, d)[:n].reshape(bsz, t, d)

def trunk(x, c, start_pos, past_k, past_v, pool_bufs, conv_bufs, ssm_states,
          ada_w, ada_b, norm_mix_g, norm_ffn_g, norm_out_g,
          ab_w_in, ab_w_out, pool_w, pool_scale, sb_bias,
          ssd_w_in, ssd_conv_w, ssd_conv_b, ssd_dt_bias, ssd_a_log, ssd_d, ssd_norm_g, ssd_w_out,
          peer_wq, peer_k1, peer_k2, peer_u, peer_v):
    new_k, new_v, new_pool, new_conv, new_ssm = [], [], [], [], []
    for l in range(DEPTH):
        mod = c @ ada_w[l] + ada_b[l]
        sh1, sc1, g1, sh2, sc2, g2 = jnp.split(mod, 6, axis=-1)
        h = modulate(x, norm_mix_g[l], sh1, sc1)
        j = l // 2
        if l % 2 == 0:
            pk = None if past_k is None else past_k[j]
            pv = None if past_v is None else past_v[j]
            y, k, v, nbuf = mixer_ab(h, start_pos, pool_bufs[j], pk, pv,
                                     ab_w_in[j], ab_w_out[j], pool_w[j], pool_scale[j], sb_bias[j])
            new_k.append(k)
            new_v.append(v)
            new_pool.append(nbuf)
        else:
            y, ncv, nss = mixer_ssd(h, conv_bufs[j], ssm_states[j], ssd_w_in[j], ssd_conv_w[j], ssd_conv_b[j],
                                    ssd_dt_bias[j], ssd_a_log[j], ssd_d[j], ssd_norm_g[j], ssd_w_out[j])
            new_conv.append(ncv)
            new_ssm.append(nss)
        x = x + g1[:, None, :] * y
        h = modulate(x, norm_ffn_g[l], sh2, sc2)
        x = x + g2[:, None, :] * peer_ffn(h, peer_wq[l], peer_k1[l], peer_k2[l], peer_u[l], peer_v[l])
    return (rmsnorm(x, norm_out_g), jnp.stack(new_k), jnp.stack(new_v), jnp.stack(new_pool),
            jnp.stack(new_conv), jnp.stack(new_ssm))

def setup_inputs(seed: int = 0) -> dict:
    key = jax.random.key(seed)
    ks = jax.random.split(key, 40)
    f32 = jnp.float32
    n_pages = PAST_LEN // PAGE_SIZE
    n_pool = (5 * DEC_BATCH * n_pages + 3) // 4

    def nrm(k, shape, s):
        return jax.random.normal(k, shape, f32) * s

    dt0 = jnp.exp(jax.random.uniform(ks[0], (N_C, SSD_HEADS), f32, math.log(1e-3), math.log(1e-1)))
    page_table = jax.random.permutation(ks[1], n_pool)[:DEC_BATCH * n_pages].reshape(DEC_BATCH, n_pages).astype(jnp.int32)
    return {
        'x_prompt': nrm(ks[2], (BATCH, SEQ, D_MODEL), 1.0),
        'x_sample': nrm(ks[3], (DEC_BATCH, DEC_SEQ, D_MODEL), 1.0),
        'cache_sb_k': nrm(ks[4], (N_AB, n_pool, PAGE_SIZE, SB_HEADS, SB_HEAD_DIM), 1.0),
        'cache_sb_v': nrm(ks[5], (N_AB, n_pool, PAGE_SIZE, SB_HEADS, SB_HEAD_DIM), 1.0),
        'state_pool': nrm(ks[6], (N_AB, DEC_BATCH, POOL_BUF, D_A), 1.0),
        'state_conv': nrm(ks[7], (N_C, DEC_BATCH, SSD_CONV - 1, CONV_DIM), 1.0),
        'state_ssm': nrm(ks[8], (N_C, DEC_BATCH, SSD_HEADS, SSD_HEAD_DIM, SSD_STATE), 0.5),
        'page_table': page_table,
        'c_prompt': nrm(ks[9], (BATCH, D_MODEL), 1.0),
        'c_sample': nrm(ks[10], (DEC_BATCH, D_MODEL), 1.0),
        'ada_w': nrm(ks[11], (DEPTH, D_MODEL, 6 * D_MODEL), 0.5 * D_MODEL ** -0.5),
        'ada_b': nrm(ks[12], (DEPTH, 6 * D_MODEL), 0.02),
        'norm_mix_g': 1.0 + nrm(ks[13], (DEPTH, D_MODEL), 0.05),
        'norm_ffn_g': 1.0 + nrm(ks[14], (DEPTH, D_MODEL), 0.05),
        'norm_out_g': 1.0 + nrm(ks[15], (D_MODEL,), 0.05),
        'ab_w_in': nrm(ks[16], (N_AB, D_MODEL, D_AB_IN), D_MODEL ** -0.5),
        'ab_w_out': nrm(ks[17], (N_AB, D_A + D_B, D_MODEL), (D_A + D_B) ** -0.5),
        'pool_w': nrm(ks[18], (N_AB, POOL_GROUPS, POOL_GC, POOL_GC), POOL_GC ** -0.5),
        'pool_scale': 1.0 + nrm(ks[19], (N_AB, D_A), 0.1),
        'sb_bias': jax.random.uniform(ks[32], (N_AB, SB_HEADS), f32, SB_BIAS_LO, SB_BIAS_HI),
        'ssd_w_in': nrm(ks[20], (N_C, D_MODEL, D_SSD_IN), D_MODEL ** -0.5),
        'ssd_conv_w': nrm(ks[21], (N_C, SSD_CONV, CONV_DIM), SSD_CONV ** -0.5),
        'ssd_conv_b': nrm(ks[22], (N_C, CONV_DIM), 0.02),
        'ssd_dt_bias': dt0 + jnp.log(-jnp.expm1(-dt0)),
        'ssd_a_log': jnp.log(jax.random.uniform(ks[23], (N_C, SSD_HEADS), f32, 1.0, 16.0)),
        'ssd_d': 1.0 + nrm(ks[24], (N_C, SSD_HEADS), 0.1),
        'ssd_norm_g': 1.0 + nrm(ks[25], (N_C, D_INNER), 0.05),
        'ssd_w_out': nrm(ks[26], (N_C, D_INNER, D_MODEL), D_INNER ** -0.5),
        'peer_wq': nrm(ks[27], (DEPTH, D_MODEL, PEER_HEADS * D_KEY), D_MODEL ** -0.5),
        'peer_k1': nrm(ks[28], (DEPTH, PEER_HEADS, N_KEYS, D_HALF), D_HALF ** -0.5),
        'peer_k2': nrm(ks[29], (DEPTH, PEER_HEADS, N_KEYS, D_HALF), D_HALF ** -0.5),
        'peer_u': nrm(ks[30], (DEPTH, N_EXPERTS, D_MODEL), D_MODEL ** -0.5),
        'peer_v': nrm(ks[31], (DEPTH, N_EXPERTS, D_MODEL), 0.5),
    }

def reference(x_prompt, x_sample, cache_sb_k, cache_sb_v, state_pool, state_conv, state_ssm, page_table,
              c_prompt, c_sample, ada_w, ada_b, norm_mix_g, norm_ffn_g, norm_out_g,
              ab_w_in, ab_w_out, pool_w, pool_scale, sb_bias,
              ssd_w_in, ssd_conv_w, ssd_conv_b, ssd_dt_bias, ssd_a_log, ssd_d, ssd_norm_g, ssd_w_out,
              peer_wq, peer_k1, peer_k2, peer_u, peer_v):
    bsz = x_prompt.shape[0]
    dbsz = x_sample.shape[0]
    pool0 = jnp.zeros((N_AB, bsz, POOL_BUF, D_A), x_prompt.dtype)
    conv0 = jnp.zeros((N_C, bsz, SSD_CONV - 1, CONV_DIM), x_prompt.dtype)
    ssm0 = jnp.zeros((N_C, bsz, SSD_HEADS, SSD_HEAD_DIM, SSD_STATE), jnp.float32)
    y_prompt, k_prompt, v_prompt, pool_prompt, conv_prompt, ssm_prompt = trunk(
        x_prompt, c_prompt, 0, None, None, pool0, conv0, ssm0,
        ada_w, ada_b, norm_mix_g, norm_ffn_g, norm_out_g, ab_w_in, ab_w_out, pool_w, pool_scale, sb_bias,
        ssd_w_in, ssd_conv_w, ssd_conv_b, ssd_dt_bias, ssd_a_log, ssd_d, ssd_norm_g, ssd_w_out,
        peer_wq, peer_k1, peer_k2, peer_u, peer_v)
    n_layers_ab = cache_sb_k.shape[0]
    past_k = cache_sb_k[:, page_table].reshape(n_layers_ab, dbsz, -1, SB_HEADS, SB_HEAD_DIM)
    past_v = cache_sb_v[:, page_table].reshape(n_layers_ab, dbsz, -1, SB_HEADS, SB_HEAD_DIM)
    y_sample, k_sample, v_sample, pool_sample, conv_sample, ssm_sample = trunk(
        x_sample, c_sample, PAST_LEN, past_k, past_v, state_pool, state_conv, state_ssm,
        ada_w, ada_b, norm_mix_g, norm_ffn_g, norm_out_g, ab_w_in, ab_w_out, pool_w, pool_scale, sb_bias,
        ssd_w_in, ssd_conv_w, ssd_conv_b, ssd_dt_bias, ssd_a_log, ssd_d, ssd_norm_g, ssd_w_out,
        peer_wq, peer_k1, peer_k2, peer_u, peer_v)
    return (y_prompt, y_sample, k_prompt, v_prompt, k_sample, v_sample,
            pool_prompt, pool_sample, conv_prompt, conv_sample, ssm_prompt, ssm_sample)


_drawn_inputs = setup_inputs


def setup_inputs(seed=0):
    import zlib

    import numpy as np

    out = dict(_drawn_inputs(seed))
    spreads = {}
    factors = {}
    for name, (base, spread) in spreads.items():
        noise = np.random.default_rng([zlib.crc32(name.encode()), seed]).standard_normal(out[name].shape)
        drawn = base * np.exp(spread * noise) if base else spread * noise
        out[name] = __import__('jax').numpy.asarray(drawn.astype(out[name].dtype))
    for name, factor in factors.items():
        out[name] = (out[name] * factor).astype(out[name].dtype)
    return out
```

```python
from contextlib import ExitStack

import concourse.bass as bass
from concourse import mybir

F32 = mybir.dt.float32
I32 = mybir.dt.int32
U32 = mybir.dt.uint32
ALU = mybir.AluOpType
ACT = mybir.ActivationFunctionType
AX = mybir.AxisListType
ds = bass.ds

P = 128
D = 1024
KC = D // P
TP = 256
NSEQ = 8
SQ = 8
TS = NSEQ * SQ
T = TP + TS
NCOND = 1 + NSEQ
EPS = 1e-6
FAR = -1.0e30

D_A = D // 4
HB = 12
HD = 64
D_B = HB * HD
NBUF = 15
PAGES = 8
PAGE = 128
PAST = PAGES * PAGE
ZK = PAST + SQ

D_IN = 2 * D
SH = 32
SG = 4
SR = SH // SG
NST = 128
XC = D_IN // P
CONV = D_IN + 2 * SG * NST
CC = CONV // P

EH = 8
NK = 128
NX = NK * NK
TOPK = 16
LOWEST = -3.0e38
GRP = 8

TILES = ((0, 128), (128, 128), (256, 64))


class Count:

    def __init__(self, sem):
        self.sem, self.n = sem, 0

    def by(self, ins, k=1):
        ins.then_inc(self.sem, k)
        self.n += k
        return self.n


class Stage:

    def __init__(self, nc, name):
        self.nc, self.name, self.ctx, self.sems = nc, name, ExitStack(), []

    def __enter__(self):
        return self

    def __exit__(self, *a):
        nums = sorted(x.num for x in self.sems)
        while nums:
            n = 1
            while n < len(nums) and nums[n] == nums[0] + n:
                n += 1
            self.nc.gpsimd.sem_clear(range(nums[0], nums[0] + n))
            nums = nums[n:]
        for x in self.sems:
            self.nc.release_semaphore(x)
        return self.ctx.__exit__(*a)

    def sb(self, name, shape, dt=F32):
        return self.ctx.enter_context(self.nc.sbuf_tensor(f"{self.name}_{name}", shape, dt))

    def bank(self, name, width=512):
        return self.ctx.enter_context(self.nc.psum_tensor(f"{self.name}_{name}", [P, width], F32))

    def sem(self, name):
        self.sems.append(self.nc.alloc_semaphore(f"{self.name}_{name}"))
        return self.sems[-1]


def chained(eng, count):
    def link(ins):
        eng.wait_ge(count.sem, count.by(ins))
    return link


def value_of(eng, x):
    return eng.compute_val(x)


def apart(eng, sem):
    eng.wait_ge(sem, 1)


class Mem:
    pass


def stage_setup(nc, m, a):
    with Stage(nc, "setup") as s:
        xrow = s.sb("xrow", [P, 3, D])
        crow = s.sb("crow", [NCOND, D])
        vrow = s.sb("vrow", [P, 3, P])
        hsel = s.sb("hsel", [96, HB, SQ])
        psx = [s.bank(f"psx{i}") for i in range(2)]
        psv = s.bank("psv")
        loaded = s.sem("loaded")
        pooled = Count(s.sem("pool_step"))
        vecd = Count(s.sem("dve_step"))
        masks = s.sem("masks_made")
        xt = s.sem("x_transposed")
        xc = s.sem("x_copied")
        vt = s.sem("vec_transposed")
        vc = s.sem("vec_copied")
        vz = s.sem("vrow_cleared")
        hz = s.sem("hsel_ready")
        with nc.Block() as block:
            @block.sync
            def _(sp):
                sp.dma_start(xrow[:, 0:2, :], a["x_prompt"].rearrange("b (t p) d -> p (b t) d", p=P)).then_inc(loaded, 16)
                sp.dma_start(xrow[0:TS, 2, :], a["x_sample"].rearrange("b t d -> (b t) d")).then_inc(loaded, 16)
                sp.dma_start(crow[0:1, :], a["c_prompt"]).then_inc(loaded, 16)
                sp.dma_start(crow[1:NCOND, :], a["c_sample"]).then_inc(loaded, 16)
                sp.wait_ge(vz, 1)
                sp.dma_start(vrow[0:96, 0, :], a["ada_b"].rearrange("l (c p) -> (l c) p", p=P)).then_inc(loaded, 16)
                sp.dma_start(vrow[96:112, 0, :], a["norm_mix_g"].rearrange("l (c p) -> (l c) p", p=P)).then_inc(loaded, 16)
                sp.dma_start(vrow[112:128, 0, :], a["norm_ffn_g"].rearrange("l (c p) -> (l c) p", p=P)).then_inc(loaded, 16)
                sp.dma_start(vrow[0:8, 1, :], a["norm_out_g"].rearrange("(c p) -> c p", p=P)).then_inc(loaded, 16)
                sp.dma_start(vrow[8:10, 1, :], a["pool_scale"].rearrange("l (c p) -> (l c) p", p=P)).then_inc(loaded, 16)
                sp.dma_start(vrow[10:34, 1, :], a["ssd_conv_b"].rearrange("l (c p) -> (l c) p", p=P)).then_inc(loaded, 16)
                sp.dma_start(vrow[34:50, 1, :], a["ssd_norm_g"].rearrange("l (c p) -> (l c) p", p=P)).then_inc(loaded, 16)
                sp.dma_start(vrow[0:96, 2, :], a["ssd_conv_w"].rearrange("l i (c p) -> (l i c) p", p=P)).then_inc(loaded, 16)

            @block.gpsimd
            def _(pool):
                link = chained(pool, pooled)
                link(pool.memset(m.ident[:], 0.0))
                link(pool.affine_select(out=m.ident[:], in_=m.ident[:], compare_op=ALU.not_equal, fill=1.0,
                                        base=0, pattern=[[-1, P]], channel_multiplier=1))
                pool.nop().then_inc(masks, 1)
                link(pool.memset(m.ones[:], 1.0))
                link(pool.affine_select(out=m.upto[:], in_=m.ones[:], compare_op=ALU.is_ge, fill=0.0,
                                        base=0, pattern=[[1, P]], channel_multiplier=-1))
                link(pool.affine_select(out=m.after[:], in_=m.ones[:], compare_op=ALU.is_gt, fill=0.0,
                                        base=0, pattern=[[-1, P]], channel_multiplier=1))
                for dst, src in ((m.upto_s, m.upto), (m.after_s, m.after), (m.seq_s, m.ones)):
                    v = dst[:].rearrange("p (b j) -> p b j", j=SQ)
                    w = src[0:TS, 0:TS].rearrange("p (b j) -> p b j", j=SQ)
                    link(pool.affine_select(out=v, in_=w, compare_op=ALU.is_ge, fill=0.0,
                                            base=0, pattern=[[-SQ, NSEQ], [0, SQ]], channel_multiplier=1))
                    link(pool.affine_select(out=v, in_=v, compare_op=ALU.is_ge, fill=0.0,
                                            base=SQ - 1, pattern=[[SQ, NSEQ], [0, SQ]], channel_multiplier=-1))
                link(pool.memset(m.far_p[:], 0.0))
                link(pool.affine_select(out=m.far_p[:], in_=m.far_p[:], compare_op=ALU.is_gt, fill=FAR,
                                        base=0, pattern=[[-1, P]], channel_multiplier=1))
                hm = m.headmask[:].rearrange("p (h d) -> p h d", d=HD)
                link(pool.memset(m.headmask[:], 1.0))
                link(pool.affine_select(out=hm, in_=hm, compare_op=ALU.is_ge, fill=0.0,
                                        base=0, pattern=[[-SQ, HB], [0, HD]], channel_multiplier=1))
                link(pool.affine_select(out=hm, in_=hm, compare_op=ALU.is_ge, fill=0.0,
                                        base=SQ - 1, pattern=[[SQ, HB], [0, HD]], channel_multiplier=-1))
                link(pool.memset(hsel[:], 1.0))
                link(pool.affine_select(out=hsel[:], in_=hsel[:], compare_op=ALU.is_gt, fill=0.0,
                                        base=0, pattern=[[-SQ, HB], [-1, SQ]], channel_multiplier=1))
                link(pool.affine_select(out=hsel[:], in_=hsel[:], compare_op=ALU.is_ge, fill=0.0,
                                        base=SQ - 1, pattern=[[SQ, HB], [0, SQ]], channel_multiplier=-1))
                pool.nop().then_inc(hz, 1)
                link(pool.iota(m.iota16[:], pattern=[[1, TOPK]], base=0, channel_multiplier=0,
                               allow_small_or_imprecise_dtypes=True))
                link(pool.iota(m.rowid[:], pattern=[[0, 1]], base=0, channel_multiplier=1,
                               allow_small_or_imprecise_dtypes=True))

            @block.tensor
            def _(pe):
                pe.wait_ge(masks, 1)
                pe.wait_ge(loaded, 16 * 12)
                for g, c in enumerate(range(0, KC, 1)):
                    if g >= 2:
                        pe.wait_ge(xc, g - 1)
                    for t0, n in TILES:
                        t = t0 // P
                        ins = pe.transpose(psx[g % 2][:, t0:t0 + n], xrow[0:n, t, c * P:(c + 1) * P], m.ident[0:n, 0:n])
                    ins.then_inc(xt, 1)
                for c in range(KC):
                    pe.transpose(psv[:, c * NCOND:(c + 1) * NCOND], crow[:, c * P:(c + 1) * P], m.ident[0:NCOND, 0:NCOND])
                for v in range(3):
                    ins = pe.transpose(psv[:, (v + 1) * P:(v + 2) * P], vrow[:, v, :], m.ident[:])
                ins.then_inc(vt, 1)

            @block.vector
            def _(dve):
                dve.memset(vrow[:], 0.0).then_inc(vz, 1)
                dve.wait_ge(masks, 1)
                dve.tensor_tensor(m.fold[:], m.ident[:, 0:TS], m.ident[:, TS:P], ALU.add).then_inc(vecd.sem, 1)
                dve.tensor_reduce(m.qsel[:], m.ident[0:96, 0:96].rearrange("p (h q) -> p q h", q=SQ), AX.X, ALU.add).then_inc(vecd.sem, 1)
                dve.wait_ge(hz, 1)
                link = chained(dve, vecd)
                vecd.n = 2
                link(dve.tensor_reduce(m.far_s[:], hsel[:].rearrange("p h j -> p j h"), AX.X, ALU.add))
                link(dve.tensor_scalar(m.far_s[:], m.far_s[:], 1.0, -FAR, ALU.subtract, ALU.mult))
                for g in range(KC):
                    dve.wait_ge(xt, g + 1)
                    dve.tensor_copy(m.xT[:, g, :], psx[g % 2][:, 0:T]).then_inc(xc, 1)
                dve.wait_ge(vt, 1)
                dve.tensor_copy(m.cT[:].rearrange("p c n -> p (c n)"), psv[:, 0:KC * NCOND]).then_inc(vc, 1)
                dve.tensor_copy(m.vcol[:], psv[:, P:4 * P]).then_inc(vc, 1)


def stage_ada(nc, m, a, layer):
    NB = 12
    w = a["ada_w"][layer].rearrange("(c p) n -> p c n", p=P)
    with Stage(nc, f"ada{layer}") as s:
        wt = [s.sb(f"w{i}", [P, KC, 512]) for i in range(2)]
        row = [s.sb(f"row{i}", [NCOND, 512]) for i in range(2)]
        psr = [s.bank(f"psr{i}") for i in range(2)]
        pst = [s.bank(f"pst{i}") for i in range(2)]
        loaded = [s.sem(f"w_loaded{i}") for i in range(2)]
        made = [s.sem(f"row_made{i}") for i in range(2)]
        copied = [s.sem(f"row_copied{i}") for i in range(2)]
        turned = [s.sem(f"row_turned{i}") for i in range(2)]
        added = [s.sem(f"bias_added{i}") for i in range(2)]
        vecd = Count(s.sem("dve_step"))
        with nc.Block() as block:
            @block.sync
            def _(sp):
                with sp.Fori(0, NB // 2) as i:
                    for k in range(2):
                        sp.wait_ge(made[k], i)
                        sp.dma_start(wt[k][:], w[:, :, ds(i * 1024 + k * 512, 512)]).then_inc(loaded[k], 16)

            @block.tensor
            def _(pe):
                with pe.Fori(0, NB // 2) as i:
                    for k in range(2):
                        pe.wait_ge(loaded[k], i * 16 + 16)
                        pe.wait_ge(copied[k], i)
                        for c in range(KC):
                            ins = pe.matmul(psr[k][0:NCOND, :], m.cT[:, c, :], wt[k][:, c, :], start=(c == 0), stop=(c == KC - 1))
                        ins.then_inc(made[k], 1)
                    for k in range(2):
                        after = value_of(pe, i + 1)
                        apart(pe, loaded[0])
                        pe.wait_ge(copied[k], after)
                        pe.wait_ge(added[k], i)
                        for q in range(4):
                            ins = pe.transpose(pst[k][:, q * NCOND:(q + 1) * NCOND], row[k][:, q * P:(q + 1) * P],
                                               m.ident[0:NCOND, 0:NCOND])
                        ins.then_inc(turned[k], 1)

            @block.scalar
            def _(act):
                with act.Fori(0, NB // 2) as i:
                    for k in range(2):
                        act.wait_ge(made[k], i + 1)
                        act.wait_ge(turned[k], i)
                        act.copy(row[k][:], psr[k][0:NCOND, :]).then_inc(copied[k], 1)

            @block.vector
            def _(dve):
                mod = m.mod[layer][:].rearrange("p c n -> p (c n)")
                with dve.Fori(0, NB // 2) as i:
                    for k in range(2):
                        dve.wait_ge(turned[k], i + 1)
                        dve.tensor_tensor(mod[:, ds(i * (8 * NCOND) + k * 4 * NCOND, 4 * NCOND)].rearrange("p (c n) -> p c n", n=NCOND),
                                          pst[k][:, 0:4 * NCOND].rearrange("p (c n) -> p c n", n=NCOND),
                                          m.vcol[:, ds(i * 8 + (48 * layer + 4 * k), 4)].unsqueeze(2).broadcast_to([P, 4, NCOND]),
                                          ALU.add).then_inc(added[k], 1)
                link = chained(dve, vecd)
                for k in range(2):
                    dve.wait_ge(added[k], NB // 2)
                for part, g0 in ((1, 96), (4, 112)):
                    sc = m.mod[layer][:, part * KC:(part + 1) * KC, :]
                    g = m.vcol[:, g0 + layer * KC:g0 + layer * KC + KC].unsqueeze(2).broadcast_to([P, KC, NCOND])
                    link(dve.tensor_scalar(sc, sc, 1.0, None, ALU.add))
                    link(dve.tensor_tensor(sc, sc, g, ALU.mult))


def stage_norm(nc, m, name, scale, shift):
    with Stage(nc, name) as s:
        sq = s.sb("sq", [P, KC, T])
        var = s.sb("var", [P, T])
        root = s.sb("root", [P, T])
        inv = s.sb("inv", [P, T])
        tmp = s.sb("tmp", [P, T])
        pss = s.bank("pss")
        squared = s.sem("squared")
        summed = s.sem("summed")
        vard = s.sem("var_ready")
        rooted = s.sem("root_ready")
        vecd = Count(s.sem("dve_step"))
        with nc.Block() as block:
            @block.scalar
            def _(act):
                for c in range(KC):
                    act.activation(sq[:, c, :], m.xT[:, c, :], ACT.Square).then_inc(squared, 1)
                act.wait_ge(vard, 1)
                act.activation(root[:], var[:], ACT.Sqrt).then_inc(rooted, 1)

            @block.tensor
            def _(pe):
                for c in range(KC):
                    pe.wait_ge(squared, c + 1)
                    ins = pe.matmul(pss[:, 0:T], m.ones[:], sq[:, c, :], start=(c == 0), stop=(c == KC - 1))
                ins.then_inc(summed, 1)

            @block.vector
            def _(dve):
                link = chained(dve, vecd)
                dve.wait_ge(summed, 1)
                dve.tensor_scalar(var[:], pss[:, 0:T], 1.0 / D, EPS, ALU.mult, ALU.add).then_inc(vard, 1)
                dve.wait_ge(rooted, 1)
                link(dve.reciprocal(inv[:], root[:]))
                link(dve.tensor_tensor(tmp[:], inv[:], inv[:], ALU.mult))
                link(dve.tensor_tensor(tmp[:], tmp[:], var[:], ALU.mult))
                link(dve.tensor_scalar(tmp[:], tmp[:], -0.5, 1.5, ALU.mult, ALU.add))
                link(dve.tensor_tensor(inv[:], inv[:], tmp[:], ALU.mult))
                link(dve.tensor_tensor(m.hT[:], m.xT[:], inv[:].unsqueeze(1).broadcast_to([P, KC, T]), ALU.mult))
                if shift is None:
                    link(dve.tensor_tensor(m.hT[:], m.hT[:], scale.unsqueeze(2).broadcast_to([P, KC, T]), ALU.mult))
                    return
                for c in range(KC):
                    ins = dve.tensor_scalar(m.hT[:, c, 0:TP], m.hT[:, c, 0:TP], scale[:, c, 0:1], shift[:, c, 0:1], ALU.mult, ALU.add)
                vecd.by(ins)
                hs = m.hT[:, :, TP:T].rearrange("p c (b j) -> p c b j", j=SQ)
                link(dve.tensor_tensor(hs, hs, scale[:, :, 1:NCOND].unsqueeze(3).broadcast_to([P, KC, NSEQ, SQ]), ALU.mult))
                link(dve.tensor_tensor(hs, hs, shift[:, :, 1:NCOND].unsqueeze(3).broadcast_to([P, KC, NSEQ, SQ]), ALU.add))


def stage_project(nc, m, name, w, src, out, blocks, kcn=KC, residual=None):
    wv = w.rearrange("(c p) n -> p c n", p=P)
    with Stage(nc, name) as s:
        wt = [s.sb(f"w{i}", [P, kcn, 256]) for i in range(2)]
        tmp = s.sb("tmp", [P, TS])
        ps = [[s.bank(f"ps{i}{j}") for j in range(2)] for i in range(2)]
        loaded = [s.sem(f"w_loaded{i}") for i in range(2)]
        made = [s.sem(f"made{i}") for i in range(2)]
        taken = [s.sem(f"taken{i}") for i in range(2)]
        vecd = s.sem("tmp_ready")
        with nc.Block() as block:
            @block.sync
            def _(sp):
                with sp.Fori(0, blocks // 2) as i:
                    for k in range(2):
                        sp.wait_ge(made[k], i * 2)
                        sp.dma_start(wt[k][:], wv[:, :, ds(i * 512 + k * 256, 256)]).then_inc(loaded[k], 16)

            @block.tensor
            def _(pe):
                with pe.Fori(0, blocks // 2) as i:
                    for k in range(2):
                        pe.wait_ge(loaded[k], i * 16 + 16)
                        pe.wait_ge(taken[k], i * 2)
                        for j in range(2):
                            for c in range(kcn):
                                ins = pe.matmul(ps[k][j][:, 0:T], wt[k][:, c, j * P:(j + 1) * P], src[:, c, :],
                                                start=(c == 0), stop=(c == kcn - 1))
                            ins.then_inc(made[k], 1)

            if residual is None:
                @block.scalar
                def _(act):
                    flat = out.rearrange("p c t -> p (c t)")
                    with act.Fori(0, blocks // 2) as i:
                        for k in range(2):
                            for j in range(2):
                                act.wait_ge(made[k], i * 2 + j + 1)
                                act.copy(flat[:, ds(i * 4 * T + (2 * k + j) * T, T)], ps[k][j][:, 0:T]).then_inc(taken[k], 1)
            else:
                @block.vector
                def _(dve):
                    for i in range(blocks // 2):
                        for k in range(2):
                            for j in range(2):
                                n = 4 * i + 2 * k + j
                                dve.wait_ge(made[k], i * 2 + j + 1)
                                dve.scalar_tensor_tensor(out=m.xT[:, n, 0:TP], in0=ps[k][j][:, 0:TP], scalar=residual[:, n, 0:1],
                                                         in1=m.xT[:, n, 0:TP], op0=ALU.mult, op1=ALU.add)
                                if n:
                                    dve.wait_ge(taken[((n - 1) // 2) % 2], 2 * ((n - 1) // 4) + (n - 1) % 2 + 1)
                                dve.tensor_tensor(tmp[:].rearrange("p (b j) -> p b j", j=SQ),
                                                  ps[k][j][:, TP:T].rearrange("p (b j) -> p b j", j=SQ),
                                                  residual[:, n, 1:NCOND].unsqueeze(2).broadcast_to([P, NSEQ, SQ]), ALU.mult).then_inc(vecd, 1)
                                dve.wait_ge(vecd, n + 1)
                                dve.tensor_tensor(m.xT[:, n, TP:T], m.xT[:, n, TP:T], tmp[:], ALU.add).then_inc(taken[k], 1)


def stage_pool(nc, m, a):
    pr = m.proj
    with Stage(nc, "pool") as s:
        kv = s.sb("kv", [P, 3, 2 * D_B])
        arow = s.sb("arow", [P, 2, D_A])
        buf = s.sb("buf", [NSEQ * NBUF, D_A])
        full_p = s.sb("full_p", [P, 2, NBUF + TP])
        full_s = s.sb("full_s", [P, 2, NSEQ, NBUF + SQ])
        sum_p = [s.sb(f"sum_p{i}", [P, 2, NBUF + TP]) for i in range(4)]
        sum_s = [s.sb(f"sum_s{i}", [P, 2, NSEQ, NBUF + SQ]) for i in range(4)]
        icnt = s.sb("icnt", [P, 2, TP])
        diff = s.sb("diff", [P, 2, T])
        pw = s.sb("pw", [P, 2, P])
        ps = [s.bank(f"ps{i}") for i in range(4)]
        psb = s.bank("psb")
        psy = [s.bank(f"psy{i}") for i in range(2)]
        loaded = s.sem("loaded")
        cleared = s.sem("cleared")
        counted = s.sem("count_written")
        turned = s.sem("turned")
        kept = s.sem("kept")
        bturned = s.sem("buf_turned")
        differ = s.sem("diff_ready")
        mixed = s.sem("mixed")
        scaled = s.sem("scaled")
        stored = s.sem("stored")
        vecd = Count(s.sem("dve_step"))
        groups = [(t, c) for t in range(3) for c in range(8, 20, 4)]
        sp_stores = 0
        with nc.Block() as block:
            @block.sync
            def _(sp):
                sp.wait_ge(cleared, 1)
                sp.dma_start(buf[:], a["state_pool"].rearrange("n b i d -> (n b i) d")).then_inc(loaded, 16)
                for g in range(4):
                    o = 64 * (g % 2)
                    sp.dma_start(pw[o:o + 64, g // 2, o:o + 64], a["pool_w"][0, g]).then_inc(loaded, 16)
                sp.wait_ge(kept, 11)
                for t, (t0, n) in enumerate(TILES):
                    for j, part in enumerate("kv"):
                        dst = a[f"{part}_sample"] if t == 2 else a[f"{part}_prompt"]
                        row0 = 0 if t == 2 else t0
                        sp.dma_start(dst.rearrange("n b t h d -> (n b t) (h d)")[row0:row0 + n, :],
                                     kv[0:n, t, j * D_B:(j + 1) * D_B]).then_inc(stored, 16)
                sp.dma_start(a["pool_prompt"].rearrange("n b i d -> (n b i) d"), arow[P - NBUF:P, 0, :]).then_inc(stored, 16)
                for b in range(NSEQ):
                    sp.dma_start(a["pool_sample"][0, b, NBUF - SQ:NBUF, :], arow[b * SQ:(b + 1) * SQ, 1, :]).then_inc(stored, 16)
                sp.dma_start(a["pool_sample"].rearrange("n b i d -> (n b) i d")[:, 0:NBUF - SQ, :],
                             a["state_pool"].rearrange("n b i d -> (n b) i d")[:, SQ:NBUF, :]).then_inc(stored, 16)
                sp.wait_ge(stored, 16 * 16)

            @block.gpsimd
            def _(pool):
                pool.iota(icnt[:], pattern=[[0, 2], [1, TP]], base=1, channel_multiplier=0,
                          allow_small_or_imprecise_dtypes=True).then_inc(counted, 1)

            @block.tensor
            def _(pe):
                for g, (t, c0) in enumerate(groups):
                    t0, n = TILES[t]
                    if g >= 4:
                        pe.wait_ge(kept, g - 3)
                    for q in range(4):
                        ins = pe.transpose(ps[g % 4][0:n, q * P:(q + 1) * P], pr[:, c0 + q, t0:t0 + n], m.ident[:])
                    ins.then_inc(turned, 1)
                for j, (t0, n) in enumerate(TILES[1:]):
                    g = 9 + j
                    pe.wait_ge(kept, g - 3)
                    for q in range(2):
                        ins = pe.transpose(ps[g % 4][0:n, q * P:(q + 1) * P], pr[:, q, t0:t0 + n], m.ident[:])
                    ins.then_inc(turned, 1)
                pe.wait_ge(loaded, 16 * 5)
                for q in range(2):
                    ins = pe.transpose(psb[:, q * 128:q * 128 + 120], buf[:, q * P:(q + 1) * P], m.ident[0:120, 0:120])
                ins.then_inc(bturned, 1)
                pe.wait_ge(differ, 1)
                for q in range(2):
                    pe.matmul(psy[q][:, 0:T], pw[:, q, :], diff[:, q, :], start=True, stop=True).then_inc(mixed, 1)

            @block.scalar
            def _(act):
                for g, (t, c0) in enumerate(groups):
                    n = TILES[t][1]
                    act.wait_ge(turned, g + 1)
                    act.copy(kv[0:n, t, (c0 - 8) * P:(c0 - 4) * P], ps[g % 4][0:n, :]).then_inc(kept, 1)
                for j, (t0, n) in enumerate(TILES[1:]):
                    act.wait_ge(turned, 10 + j)
                    act.copy(arow[0:n, j, :], ps[(9 + j) % 4][0:n, 0:D_A]).then_inc(kept, 1)
                for q in range(2):
                    act.wait_ge(mixed, q + 1)
                    act.mul(m.yT[:, q, :], psy[q][:, 0:T], m.vcol[:, 136 + q:137 + q]).then_inc(scaled, 1)

            @block.vector
            def _(dve):
                link = chained(dve, vecd)
                dve.memset(pw[:], 0.0).then_inc(cleared, 1)
                link(dve.memset(full_p[:, :, 0:NBUF], 0.0))
                link(dve.tensor_copy(full_p[:, :, NBUF:], pr[:, 0:2, 0:TP]))
                link(dve.tensor_copy(full_s[:, :, :, NBUF:], pr[:, 0:2, TP:T].rearrange("p c (b j) -> p c b j", j=SQ)))
                dve.wait_ge(bturned, 1)
                for q in range(2):
                    link(dve.tensor_copy(full_s[:, q, :, 0:NBUF], psb[:, q * 128:q * 128 + 120].rearrange("p (b i) -> p b i", i=NBUF)))
                at = 0
                src_p, src_s = full_p, full_s
                for lvl in range(4):
                    by = 1 << lvl
                    lo = at + by
                    link(dve.tensor_tensor(sum_p[lvl][:, :, lo:], src_p[:, :, lo:], src_p[:, :, at:NBUF + TP - by], ALU.add))
                    link(dve.tensor_tensor(sum_s[lvl][:, :, :, lo:], src_s[:, :, :, lo:], src_s[:, :, :, at:NBUF + SQ - by], ALU.add))
                    src_p, src_s, at = sum_p[lvl], sum_s[lvl], lo
                dve.wait_ge(counted, 1)
                for g in range(4):
                    o, q, w = 64 * (g % 2), g // 2, 2 << g
                    link(dve.tensor_scalar(icnt[o:o + 64, q, :], icnt[o:o + 64, q, :], float(w), None, ALU.min))
                link(dve.reciprocal(icnt[:], icnt[:]))
                for g in range(4):
                    o, q, w = 64 * (g % 2), g // 2, 2 << g
                    rows = slice(o, o + 64)
                    link(dve.tensor_tensor(diff[rows, q, 0:TP], sum_p[g][rows, q, NBUF:], icnt[rows, q, :], ALU.mult))
                    link(dve.tensor_tensor(diff[rows, q, 0:TP], diff[rows, q, 0:TP], pr[rows, q, 0:TP], ALU.subtract))
                    link(dve.scalar_tensor_tensor(out=diff[rows, q, TP:T].rearrange("p (b j) -> p b j", j=SQ),
                                                  in0=sum_s[g][rows, q, :, NBUF:], scalar=1.0 / w,
                                                  in1=pr[rows, q, TP:T].rearrange("p (b j) -> p b j", j=SQ),
                                                  op0=ALU.mult, op1=ALU.subtract))
                dve.nop().then_inc(differ, 1)


def stage_attend_prompt(nc, m, a):
    W = 3 * P
    pr = m.proj
    NP = HB // 2
    with Stage(nc, "attp") as s:
        bias = s.sb("bias", [P, HB])
        q = s.sb("q", [P, 2, TP])
        v = s.sb("v", [P, 2, P])
        vt = s.sb("vt", [P, TP])
        z = s.sb("z", [P, 2, W])
        e = s.sb("e", [P, 2, W])
        sp_ = s.sb("softplus", [P, 2, W])
        su = s.sb("suffix", [P, 2, W])
        wT = s.sb("wT", [P, 2, W])
        zero = s.sb("zero", [P, TP])
        psz = [s.bank(f"psz{i}") for i in range(2)]
        psw = [s.bank(f"psw{i}") for i in range(2)]
        psv = s.bank("psv")
        pso = [s.bank(f"pso{i}") for i in range(2)]
        loaded = s.sem("bias_loaded")
        staged = s.sem("operands_staged")
        scored = s.sem("scored")
        vturned = s.sem("v_turned")
        vkept = s.sem("v_kept")
        biased = s.sem("biased")
        masked = s.sem("masked")
        logged = s.sem("logged")
        actd = s.sem("act_step")
        softp = s.sem("softplus_ready")
        scanned = s.sem("scanned")
        expo = s.sem("exponent_ready")
        weighed = s.sem("weights_ready")
        wturned = s.sem("weights_turned")
        wkept = s.sem("weights_kept")
        mixed = s.sem("mixed")
        outs = s.sem("outputs_kept")
        zs = s.sem("zero_ready")
        flat = pr[:].rearrange("p c t -> p (c t)")
        yflat = m.yT[:].rearrange("p c t -> p (c t)")
        with nc.Block() as block:
            @block.sync
            def _(sp):
                sp.dma_start(bias[:], a["sb_bias"].broadcast_to([P, HB])).then_inc(loaded, 16)

            @block.tensor
            def _(pe):
                with pe.Fori(0, NP) as i:
                    pe.wait_ge(staged, i * 3 + 3)
                    pe.wait_ge(biased, i * 2)
                    for h in range(2):
                        pe.matmul(psz[h][:, 0:P], q[:, h, 0:P], flat[:, ds(i * T + 8 * T, P)], start=True, stop=True)
                        pe.matmul(psz[h][:, P:W], q[:, h, P:TP], flat[:, ds(i * T + 8 * T, TP)], start=True, stop=True).then_inc(scored, 1)
                    pe.wait_ge(vkept, i)
                    for t in range(2):
                        ins = pe.transpose(psv[:, t * P:(t + 1) * P], vt[:, t * P:(t + 1) * P], m.ident[:])
                    ins.then_inc(vturned, 1)
                    for h in range(2):
                        pe.wait_ge(weighed, i * 2 + h + 1)
                        pe.wait_ge(wkept, i * 2 + h)
                        for b in range(3):
                            ins = pe.transpose(psw[h][:, b * P:(b + 1) * P], z[:, h, b * P:(b + 1) * P], m.ident[:])
                        ins.then_inc(wturned, 1)
                    pe.wait_ge(vkept, i + 1)
                    pe.wait_ge(outs, i * 2)
                    for h in range(2):
                        pe.wait_ge(wkept, i * 2 + h + 1)
                        pe.matmul(pso[h][:, 0:TP], v[:, 0, :], wT[:, h, 0:TP], start=True, stop=False)
                        pe.matmul(pso[h][:, P:TP], v[:, 1, :], wT[:, h, TP:W], start=False, stop=True).then_inc(mixed, 1)

            @block.scalar
            def _(act):
                act.wait_ge(loaded, 16)
                bflat = bias[:]
                with act.Fori(0, NP) as i:
                    act.wait_ge(weighed, i * 2)
                    for h in range(2):
                        act.wait_ge(scored, i * 2 + h + 1)
                        act.wait_ge(wturned, i * 2)
                        act.activation(z[:, h, :], psz[h][:, 0:W], ACT.Identity, bias=bflat[:, ds(i * 2 + h, 1)],
                                       scale=HD ** -0.5).then_inc(biased, 1)
                    act.wait_ge(masked, i + 1)
                    act.wait_ge(softp, i)
                    act.activation(e[:], z[:], ACT.Abs).then_inc(actd, 1)
                    act.wait_ge(actd, i * 2 + 1)
                    act.activation(e[:], e[:], ACT.Exp, scale=-1.0).then_inc(actd, 1)
                    act.wait_ge(actd, i * 2 + 2)
                    act.activation(e[:], e[:], ACT.Ln, bias=1.0).then_inc(logged, 1)
                    for h in range(2):
                        act.wait_ge(expo, i * 2 + h + 1)
                        act.activation(z[:, h, :], z[:, h, :], ACT.Exp).then_inc(weighed, 1)
                    for h in range(2):
                        act.wait_ge(wturned, i * 2 + h + 1)
                        act.wait_ge(mixed, i * 2 + h)
                        act.copy(wT[:, h, :], psw[h][:, 0:W]).then_inc(wkept, 1)

            @block.vector
            def _(dve):
                dve.memset(zero[:], 0.0).then_inc(zs, 1)
                dve.memset(q[:], 0.0).then_inc(zs, 1)
                dve.wait_ge(zs, 2)
                with dve.Fori(0, NP) as i:
                    dve.wait_ge(vturned, i)
                    dve.wait_ge(mixed, i * 2)
                    for h in range(2):
                        r = slice(64 * h, 64 * h + 64)
                        dve.tensor_copy(q[r, h, :], flat[r, ds(i * T + 2 * T, TP)]).then_inc(staged, 1)
                    dve.tensor_copy(vt[:], flat[:, ds(i * T + 14 * T, TP)]).then_inc(staged, 1)
                    dve.wait_ge(vturned, i + 1)
                    dve.tensor_copy(v[:].rearrange("p t d -> p (t d)"), psv[:, 0:TP]).then_inc(vkept, 1)
                    dve.wait_ge(biased, i * 2 + 2)
                    diag = z[:].rearrange("p h (b k) -> p h b k", k=P)[:, :, 0:3:2, :]
                    dve.tensor_tensor(diag, diag, m.far_p[:].unsqueeze(1).unsqueeze(1).broadcast_to([P, 2, 2, P]), ALU.add).then_inc(masked, 1)
                    dve.wait_ge(logged, i + 1)
                    dve.wait_ge(masked, i + 1)
                    dve.scalar_tensor_tensor(out=sp_[:], in0=z[:], scalar=0.0, in1=e[:], op0=ALU.max, op1=ALU.add).then_inc(softp, 1)
                    dve.wait_ge(softp, i + 1)
                    for h in range(2):
                        dve.tensor_tensor_scan(su[:, h, 0:P][:, ::-1], sp_[:, h, 0:P][:, ::-1], zero[:, 0:P], 0.0, ALU.add, ALU.add).then_inc(scanned, 1)
                        dve.tensor_tensor_scan(su[:, h, P:W][:, ::-1], sp_[:, h, P:W][:, ::-1], zero[:], 0.0, ALU.add, ALU.add).then_inc(scanned, 1)
                    for h in range(2):
                        dve.wait_ge(scanned, i * 4 + 2 * h + 2)
                        dve.tensor_tensor(z[:, h, :], z[:, h, :], su[:, h, :], ALU.subtract).then_inc(expo, 1)
                    for h in range(2):
                        dve.wait_ge(mixed, i * 2 + h + 1)
                        r = slice(64 * h, 64 * h + 64)
                        dve.tensor_copy(yflat[r, ds(i * T + 2 * T, TP)], pso[h][r, 0:TP]).then_inc(outs, 1)


def stage_attend_sample(nc, m, a):
    R = HB * SQ
    pr = m.proj
    pos = pr[:].rearrange("p c t -> p (c t)")
    CH = D_B // P
    with Stage(nc, "atts") as s:
        pt_i = s.sb("pt_i", [P, NSEQ * PAGES], I32)
        pt_f = s.sb("pt_f", [P, NSEQ * PAGES])
        rows = s.sb("rows", [P, NSEQ * PAGES], U32)
        kcol = s.sb("kcol", [P, PAGES], U32)
        vcolx = s.sb("vcolx", [P, PAGES], U32)
        bias = s.sb("bias", [R, 1])
        kp = s.sb("kp", [P, PAGES, D_B])
        vp = s.sb("vp", [P, PAGES, D_B])
        kT = s.sb("kT", [P, CH, PAST])
        vnew = s.sb("vnew", [SQ, NSEQ, D_B])
        qb = s.sb("qb", [P, CH * 112])
        z = s.sb("z", [R, ZK])
        e = s.sb("e", [R, ZK])
        sp_ = s.sb("softplus", [R, ZK])
        su = s.sb("suffix", [R, ZK])
        zero = s.sb("zero", [R, ZK])
        wT = s.sb("wT", [P, PAGES * R])
        wTn = s.sb("wTn", [SQ, R])
        om = s.sb("om", [R, D_B])
        psk = [s.bank(f"psk{i}") for i in range(2)]
        psz = [s.bank(f"psz{i}") for i in range(2)]
        psm = s.bank("psm")
        psw = s.bank("psw")
        pso = [s.bank(f"pso{i}") for i in range(2)]
        loaded = s.sem("loaded")
        looked = Count(s.sem("rows_step"))
        kcoled = s.sem("kcol_ready")
        vcoled = s.sem("vcol_ready")
        kin = m.gathered[0:PAGES]
        vin = m.gathered[PAGES:2 * PAGES]
        g0 = m.gathered_by
        m.gathered_by += 16 * NSEQ
        kturn = s.sem("k_turned")
        kkept = s.sem("k_kept_act")
        kkept2 = s.sem("k_kept_dve")
        qset = s.sem("q_set")
        cleared = s.sem("cleared")
        scored = s.sem("scored")
        biased = s.sem("biased")
        masked = s.sem("masked")
        actd = s.sem("act_step")
        logged = s.sem("logged")
        softp = s.sem("softplus_ready")
        scanned = s.sem("scanned")
        expo = s.sem("exponent_ready")
        weighed = s.sem("weights_ready")
        wturn = s.sem("weights_turned")
        wkept = s.sem("weights_kept")
        mixed = s.sem("mixed")
        kept = s.sem("outputs_masked")
        folded = s.sem("outputs_turned")
        done = s.sem("outputs_kept")
        with nc.Block() as block:
            @block.sync
            def _(sp):
                sp.dma_start(pt_i[:], a["page_table"].rearrange("b g -> (b g)").unsqueeze(0).broadcast_to([P, NSEQ * PAGES])).then_inc(loaded, 16)
                sp.dma_start(bias[:], a["sb_bias"].rearrange("n (h o) -> (n h) o", o=1).unsqueeze(1).broadcast_to([HB, SQ, 1])).then_inc(loaded, 16)
                sp.dma_start(vnew[:], a["v_sample"].rearrange("n b t h d -> (n t) b (h d)")).then_inc(loaded, 16)

            @block.gpsimd
            def _(pool):
                kc_ = a["cache_sb_k"].rearrange("n g p h d -> (n g p) (h d)")
                vc_ = a["cache_sb_v"].rearrange("n g p h d -> (n g p) (h d)")
                link = chained(pool, looked)
                pool.wait_ge(loaded, 48)
                link(pool.tensor_copy(pt_f[:], pt_i[:]))
                link(pool.tensor_scalar(pt_f[:], pt_f[:], float(PAGE), m.rowid[:, 0:1], ALU.mult, ALU.add))
                link(pool.tensor_copy(rows[:], pt_f[:]))
                with pool.Fori(0, NSEQ) as b:
                    apart(pool, loaded)
                    for j in range(PAGES):
                        pool.wait_ge(kin[j], b * 16 + g0)
                    pool.tensor_copy(kcol[:], rows[:, ds(b * PAGES, PAGES)]).then_inc(kcoled, 1)
                    after, past = value_of(pool, b + 1), value_of(pool, b * (2 * PAGES))
                    apart(pool, loaded)
                    pool.wait_ge(kcoled, after)
                    pool.wait_ge(kturn, past)
                    for j in range(PAGES):
                        pool.indirect_dma_start(kp[:, j, :], None, kc_, bass.IndirectOffsetOnAxis(ap=kcol[:, j:j + 1], axis=0)).then_inc(kin[j], 16)
                    apart(pool, loaded)
                    for j in range(PAGES):
                        pool.wait_ge(vin[j], b * 16 + g0)
                    pool.tensor_copy(vcolx[:], rows[:, ds(b * PAGES, PAGES)]).then_inc(vcoled, 1)
                    after, past = value_of(pool, b + 1), value_of(pool, b * 2)
                    apart(pool, loaded)
                    pool.wait_ge(vcoled, after)
                    pool.wait_ge(mixed, past)
                    for j in range(PAGES):
                        pool.indirect_dma_start(vp[:, j, :], None, vc_, bass.IndirectOffsetOnAxis(ap=vcolx[:, j:j + 1], axis=0)).then_inc(vin[j], 16)

            def front(eng, b, pe):
                for j in range(PAGES):
                    pe.wait_ge(kin[j], b * 16 + (g0 + 16))
                    pe.wait_ge(kkept, b * PAGES + j)
                    for c in range(4):
                        ins = pe.transpose(psk[0][:, c * P:(c + 1) * P], kp[:, j, c * P:(c + 1) * P], m.ident[:])
                    ins.then_inc(kturn, 1)
                    pe.wait_ge(kkept2, b * PAGES + j)
                    for c in range(4, CH):
                        ins = pe.transpose(psk[1][:, (c - 4) * P:(c - 3) * P], kp[:, j, c * P:(c + 1) * P], m.ident[:])
                    ins.then_inc(kturn, 1)
                pe.wait_ge(kkept, b * PAGES + PAGES)
                pe.wait_ge(kkept2, b * PAGES + PAGES)
                pe.wait_ge(qset, b * 2 + 2)
                pe.wait_ge(biased, b * 3)
                for half in range(2):
                    for c in range(CH):
                        ins = pe.matmul(psz[half][0:R, :], qb[:, c * R:(c + 1) * R], kT[:, c, half * 512:(half + 1) * 512],
                                        start=(c == 0), stop=(c == CH - 1))
                    ins.then_inc(scored, 1)
                pe.wait_ge(done, b)
                pe.wait_ge(wkept, b * 3)
                for c in range(CH):
                    ins = pe.matmul(psm[0:R, 0:SQ], qb[:, c * R:(c + 1) * R], pos[:, ds(b * SQ + ((8 + c) * T + TP), SQ)],
                                    start=(c == 0), stop=(c == CH - 1))
                ins.then_inc(scored, 1)

            def back(pe, b):
                pe.wait_ge(weighed, b + 1)
                for g in range(2):
                    pe.wait_ge(wkept, b * 3 + (2 * g))
                    for j in range(4):
                        ins = pe.transpose(psw[:, j * R:(j + 1) * R], z[:, (4 * g + j) * P:(4 * g + j + 1) * P], m.ident[0:R, 0:R])
                    ins.then_inc(wturn, 1)
                    if g == 0:
                        ins = pe.transpose(psm[0:SQ, P:P + R], z[:, PAST:ZK], m.ident[0:R, 0:R])
                        ins.then_inc(wturn, 1)
                pe.wait_ge(wkept, b * 3 + 3)
                pe.wait_ge(kept, b * 2)
                for half in range(2):
                    cols = slice(half * 384, half * 384 + 384)
                    for j in range(PAGES):
                        if half == 0:
                            pe.wait_ge(vin[j], b * 16 + (g0 + 16))
                        pe.matmul(pso[half][0:R, 0:384], wT[:, j * R:(j + 1) * R], vp[:, j, cols], start=(j == 0), stop=False)
                    pe.matmul(pso[half][0:R, 0:384], wTn[:], vnew[:].rearrange("p b d -> p (b d)")[:, ds(b * D_B + half * 384, 384)],
                              start=False, stop=True).then_inc(mixed, 1)
                pe.wait_ge(kept, b * 2 + 2)
                for c in range(CH):
                    ins = pe.matmul(psm[:, 256 + c * SQ:256 + (c + 1) * SQ], om[:, c * P:(c + 1) * P], m.qsel[:], start=True, stop=True)
                ins.then_inc(folded, 1)

            @block.tensor
            def _(pe):
                pe.wait_ge(loaded, 48)
                front(pe, 0, pe)
                with pe.Fori(1, NSEQ) as b:
                    back(pe, b - 1)
                    front(pe, b, pe)
                back(pe, NSEQ - 1)

            @block.scalar
            def _(act):
                act.wait_ge(loaded, 48)

                def keys(b):
                    for j in range(PAGES):
                        act.wait_ge(kturn, b * (2 * PAGES) + 2 * j + 1)
                        act.wait_ge(scored, b * 3)
                        act.copy(kT[:, 0:4, j * P:(j + 1) * P], psk[0][:].rearrange("p (c k) -> p c k", k=P)).then_inc(kkept, 1)

                def weights(b):
                    act.wait_ge(wturn, b * 3)
                    for half in range(2):
                        act.wait_ge(scored, b * 3 + half + 1)
                        act.activation(z[:, half * 512:(half + 1) * 512], psz[half][0:R, :], ACT.Identity,
                                       bias=bias[:, 0:1], scale=HD ** -0.5).then_inc(biased, 1)
                    act.wait_ge(scored, b * 3 + 3)
                    act.activation(z[:, PAST:ZK], psm[0:R, 0:SQ], ACT.Identity, bias=bias[:, 0:1], scale=HD ** -0.5).then_inc(biased, 1)
                    act.wait_ge(masked, b + 1)
                    act.wait_ge(softp, b)
                    act.wait_ge(biased, b * 3 + 3)
                    act.activation(e[:], z[:], ACT.Abs).then_inc(actd, 1)
                    act.wait_ge(actd, b * 2 + 1)
                    act.activation(e[:], e[:], ACT.Exp, scale=-1.0).then_inc(actd, 1)
                    act.wait_ge(actd, b * 2 + 2)
                    act.activation(e[:], e[:], ACT.Ln, bias=1.0).then_inc(logged, 1)
                    act.wait_ge(expo, b + 1)
                    act.activation(z[:], z[:], ACT.Exp).then_inc(weighed, 1)
                    act.wait_ge(mixed, b * 2)
                    for g in range(2):
                        act.wait_ge(wturn, b * 3 + 1 + 2 * g)
                        act.copy(wT[:, 4 * g * R:4 * (g + 1) * R], psw[:, 0:4 * R]).then_inc(wkept, 1)
                        if g == 0:
                            act.wait_ge(wturn, b * 3 + 2)
                            act.copy(wTn[:], psm[0:SQ, P:P + R]).then_inc(wkept, 1)

                keys(0)
                with act.Fori(0, NSEQ - 1) as b:
                    weights(b)
                    keys(b + 1)
                weights(NSEQ - 1)

            @block.vector
            def _(dve):
                dve.memset(qb[:], 0.0).then_inc(cleared, 1)
                dve.memset(zero[:], 0.0).then_inc(cleared, 1)
                dve.wait_ge(cleared, 2)

                def keys(b):
                    dve.wait_ge(scored, b * 3)
                    for h in range(2):
                        r = slice(64 * h, 64 * h + 64)
                        dve.tensor_copy(qb[r, :].rearrange("p (c x) -> p c x", x=112)[:, :, 8 * h:8 * h + 8],
                                        pos[r, :].rearrange("p (c t) -> p c t", t=T)[:, 2:8, ds(b * SQ + TP, SQ)]).then_inc(qset, 1)
                    for j in range(PAGES):
                        dve.wait_ge(kturn, b * (2 * PAGES) + 2 * j + 2)
                        dve.tensor_copy(kT[:, 4:CH, j * P:(j + 1) * P], psk[1][:, 0:(CH - 4) * P].rearrange("p (c k) -> p c k", k=P)).then_inc(kkept2, 1)

                def weights(b):
                    dve.wait_ge(biased, b * 3 + 3)
                    dve.tensor_tensor(z[:, PAST:ZK], z[:, PAST:ZK], m.far_s[:], ALU.add).then_inc(masked, 1)
                    dve.wait_ge(logged, b + 1)
                    dve.wait_ge(masked, b + 1)
                    dve.scalar_tensor_tensor(out=sp_[:], in0=z[:], scalar=0.0, in1=e[:], op0=ALU.max, op1=ALU.add).then_inc(softp, 1)
                    dve.wait_ge(softp, b + 1)
                    dve.tensor_tensor_scan(su[:, ::-1], sp_[:, ::-1], zero[:], 0.0, ALU.add, ALU.add).then_inc(scanned, 1)
                    dve.wait_ge(scanned, b + 1)
                    dve.tensor_tensor(z[:], z[:], su[:], ALU.subtract).then_inc(expo, 1)

                def outputs(b):
                    for half in range(2):
                        dve.wait_ge(mixed, b * 2 + half + 1)
                        dve.wait_ge(folded, b)
                        cols = slice(half * 384, half * 384 + 384)
                        dve.tensor_tensor(om[:, cols], pso[half][0:R, 0:384], m.headmask[:, cols], ALU.mult).then_inc(kept, 1)
                    dve.wait_ge(folded, b + 1)
                    dve.tensor_copy(m.yT[:, 2:8, ds(b * SQ + TP, SQ)],
                                    psm[:, 256:256 + CH * SQ].rearrange("p (c j) -> p c j", j=SQ)).then_inc(done, 1)

                keys(0)
                with dve.Fori(0, NSEQ - 1) as b:
                    weights(b)
                    outputs(b)
                    keys(b + 1)
                weights(NSEQ - 1)
                outputs(NSEQ - 1)


def stage_conv(nc, m, a):
    pr = m.proj
    NB3 = NSEQ * 3
    NS_ = 3 + NB3
    with Stage(nc, "conv") as s:
        buf = s.sb("buf", [NB3, CONV])
        bufT = s.sb("bufT", [P, CC, NB3])
        full = s.sb("full", [P, CC, NSEQ, 11])
        tmp = s.sb("tmp", [P, CC, NSEQ, SQ])
        last = s.sb("last", [P, CC, NS_])
        lrow = s.sb("lrow", [NS_, CONV])
        wdt = s.sb("wdt", [P, KC, SH])
        dtb = s.sb("dtb", [P, SH])
        alog = s.sb("alog", [P, SH])
        raw = s.sb("raw", [P, 3, SH])
        lg = s.sb("lg", [P, 3, SH])
        psb = [s.bank(f"psb{i}") for i in range(2)]
        psl = [s.bank(f"psl{i}") for i in range(2)]
        psd = s.bank("psd")
        loaded = s.sem("loaded")
        bturned = s.sem("buf_turned")
        bkept = s.sem("buf_kept")
        lasts = s.sem("last_ready")
        lturned = s.sem("last_turned")
        lkept = s.sem("last_kept")
        stored = s.sem("stored")
        dts = s.sem("dt_summed")
        pooled = Count(s.sem("pool_step"))
        vecd = Count(s.sem("dve_step"))
        actd = Count(s.sem("act_step"))
        conv_p = s.sem("conv_prompt_done")
        conv_s = s.sem("conv_sample_done")
        tapped = s.sem("tap_added")
        rawd = s.sem("dt_biased")
        dlog = s.sem("dt_logged")
        cv = m.xbc
        cvf = cv[:].rearrange("p c t -> p (c t)")
        prf = pr[:].rearrange("p c t -> p (c t)")
        with nc.Block() as block:
            @block.sync
            def _(sp):
                sp.dma_start(buf[:], a["state_conv"].rearrange("n b i d -> (n b i) d")).then_inc(loaded, 16)
                sp.dma_start(wdt[:], a["ssd_w_in"][0].rearrange("(c p) n -> p c n", p=P)[:, :, D_IN + CONV:D_IN + CONV + SH]).then_inc(loaded, 16)
                sp.dma_start(dtb[:], a["ssd_dt_bias"].broadcast_to([P, SH])).then_inc(loaded, 16)
                sp.dma_start(alog[:], a["ssd_a_log"].broadcast_to([P, SH])).then_inc(loaded, 16)
                sp.wait_ge(lkept, 6)
                sp.dma_start(a["conv_prompt"].rearrange("n b i d -> (n b i) d"), lrow[0:3, :]).then_inc(stored, 16)
                sp.dma_start(a["conv_sample"].rearrange("n b i d -> (n b i) d"), lrow[3:NS_, :]).then_inc(stored, 16)
                sp.wait_ge(stored, 32)

            @block.tensor
            def _(pe):
                pe.wait_ge(loaded, 64)
                for t, (t0, n) in enumerate(TILES):
                    for c in range(KC):
                        ins = pe.matmul(psd[0:n, t * SH:(t + 1) * SH], m.hT[:, c, t0:t0 + n], wdt[:, c, :], start=(c == 0), stop=(c == KC - 1))
                ins.then_inc(dts, 1)
                for g in range(2):
                    for q in range(12):
                        ins = pe.transpose(psb[g][:, q * NB3:(q + 1) * NB3], buf[:, (12 * g + q) * P:(12 * g + q + 1) * P], m.ident[0:NB3, 0:NB3])
                    ins.then_inc(bturned, 1)
                pe.wait_ge(lasts, 2)
                for g in range(6):
                    if g >= 2:
                        pe.wait_ge(lkept, g - 1)
                    for q in range(4):
                        ins = pe.transpose(psl[g % 2][0:NS_, q * P:(q + 1) * P], last[:, 4 * g + q, :], m.ident[:])
                    ins.then_inc(lturned, 1)

            @block.gpsimd
            def _(pool):
                link = chained(pool, pooled)
                link(pool.tensor_copy(full[:, :, :, 3:11], pr[:, XC:, TP:T].rearrange("p c (b j) -> p c b j", j=SQ)))
                pool.tensor_copy(last[:, :, 0:3], pr[:, XC:, TP - 3:TP]).then_inc(lasts, 1)
                pool.tensor_copy(last[:, :, 3:NS_].rearrange("p c (b i) -> p c b i", i=3),
                                 pr[:, XC:, TP:T].rearrange("p c (b j) -> p c b j", j=SQ)[:, :, :, 5:8]).then_inc(lasts, 1)
                pool.wait_ge(bkept, 2)
                link(pool.tensor_copy(full[:, :, :, 0:3], bufT[:].rearrange("p c (b i) -> p c b i", i=3)))
                out = cv[:, :, TP:T].rearrange("p c (b j) -> p c b j", j=SQ)

                def tap(i):
                    return m.cw[:, i, :].unsqueeze(2).unsqueeze(2).broadcast_to([P, CC, NSEQ, SQ])

                link(pool.tensor_tensor(out, full[:, :, :, 0:8], tap(0), ALU.mult))
                for i in range(1, 4):
                    link(pool.tensor_tensor(tmp[:], full[:, :, :, i:i + 8], tap(i), ALU.mult))
                    link(pool.tensor_tensor(out, out, tmp[:], ALU.add))
                pool.tensor_tensor(out, out, m.vcol[:, 138:162].unsqueeze(2).unsqueeze(2).broadcast_to([P, CC, NSEQ, SQ]),
                                   ALU.add).then_inc(conv_s, 1)

            @block.vector
            def _(dve):
                link = chained(dve, vecd)
                dve.wait_ge(dts, 1)
                dve.wait_ge(loaded, 64)
                for t, (t0, n) in enumerate(TILES):
                    ins = dve.tensor_tensor(raw[0:n, t, :], psd[0:n, t * SH:(t + 1) * SH], dtb[0:n, :], ALU.add)
                    ins.then_inc(rawd, 1)
                with dve.Fori(0, CC) as c:
                    dve.tensor_scalar(cvf[:, ds(c * T, TP)], prf[:, ds(c * T + XC * T, TP)],
                                      m.vcol[:, ds(c + 256 + 72, 1)], m.vcol[:, ds(c + 138, 1)], ALU.mult, ALU.add).then_inc(tapped, 1)
                    for i in range(1, 4):
                        dve.wait_ge(tapped, c * 3 + i)
                        dve.scalar_tensor_tensor(out=cvf[:, ds(c * T + i, TP - i)], in0=prf[:, ds(c * T + XC * T, TP - i)],
                                                 scalar=m.vcol[:, ds(c + 256 + 24 * (3 - i), 1)], in1=cvf[:, ds(c * T + i, TP - i)],
                                                 op0=ALU.mult, op1=ALU.add).then_inc(tapped if i < 3 else conv_p, 1)
                dve.wait_ge(dlog, 1)
                for t, (t0, n) in enumerate(TILES):
                    ins = dve.scalar_tensor_tensor(out=m.dt[0:n, t, :], in0=raw[0:n, t, :], scalar=0.0, in1=lg[0:n, t, :], op0=ALU.max, op1=ALU.add)
                    vecd.by(ins)
                dve.wait_ge(vecd.sem, vecd.n)
                for t, (t0, n) in enumerate(TILES):
                    dve.scalar_tensor_tensor(out=m.dta[0:n, t, :], in0=m.dt[0:n, t, :], scalar=-1.0, in1=alog[0:n, :], op0=ALU.mult, op1=ALU.mult)

            @block.scalar
            def _(act):
                link = chained(act, actd)
                for g in range(2):
                    act.wait_ge(bturned, g + 1)
                    act.copy(bufT[:, 12 * g:12 * (g + 1), :].rearrange("p c n -> p (c n)"), psb[g][:, 0:12 * NB3]).then_inc(bkept, 1)
                act.wait_ge(rawd, 3)
                for t, (t0, n) in enumerate(TILES):
                    actd.by(act.activation(lg[0:n, t, :], raw[0:n, t, :], ACT.Abs))
                act.wait_ge(actd.sem, actd.n)
                for t, (t0, n) in enumerate(TILES):
                    actd.by(act.activation(lg[0:n, t, :], lg[0:n, t, :], ACT.Exp, scale=-1.0))
                actd.by(act.activation(alog[:], alog[:], ACT.Exp))
                act.wait_ge(actd.sem, actd.n)
                for t, (t0, n) in enumerate(TILES):
                    actd.by(act.activation(lg[0:n, t, :], lg[0:n, t, :], ACT.Ln, bias=1.0))
                act.wait_ge(actd.sem, actd.n)
                act.nop().then_inc(dlog, 1)
                for g in range(6):
                    act.wait_ge(lturned, g + 1)
                    act.copy(lrow[:, g * 512:(g + 1) * 512], psl[g % 2][0:NS_, :]).then_inc(lkept, 1)
                act.wait_ge(conv_s, 1)
                act.wait_ge(conv_p, CC)
                act.activation(cv[:], cv[:], ACT.Silu)


def stage_scan(nc, m, a):
    cv = m.xbc
    BC, CCH = XC, XC + SG
    with Stage(nc, "scan") as s:
        bt = m.btok
        eacs = s.sb("eacs", [P, SH])
        toend = s.sb("toend", [P, 4, SH])
        xe = s.sb("xe", [P, 3, D_IN])
        st0 = s.sb("st0", [NST, D_IN])
        stout = s.sb("stout", [P, XC, NST])
        lm = [s.sb(f"lm{i}", [P, 4, P]) for i in range(2)]
        dec = [s.sb(f"dec{i}", [P, 4, P]) for i in range(2)]
        cbm = [s.sb(f"cbm{i}", [P, P]) for i in range(2)]
        yo = s.sb("yo", [P, 512])
        psA = [s.bank(f"psA{i}") for i in range(2)]
        psC = s.bank("psC")
        psY = [s.bank(f"psY{i}") for i in range(2)]
        psO = s.bank("psO")
        psE = s.bank("psE")
        psS = s.bank("psS")
        turned = s.sem("turned")
        kept = s.sem("kept")
        csum = s.sem("decays_summed")
        cexp = s.sem("decays_ready")
        xed = s.sem("xe_ready")
        stsum = s.sem("state0_summed")
        stkept = s.sem("state0_kept")
        cbs = s.sem("cb_made")
        cbk = s.sem("cb_kept")
        lmd = s.sem("lm_ready")
        segd = s.sem("segments_summed")
        decd = s.sem("segments_exp")
        mtd = s.sem("mt_ready")
        yd = s.sem("y_made")
        yod = s.sem("yoff_made")
        yk = s.sem("y_kept")
        ytmp = s.sem("y_tmp")
        fin = s.sem("state_made")
        fink = s.sem("state_kept")
        fins = s.sem("state_stored")
        groups = [(t, g) for t in range(3) for g in range(5)]
        steps = [(t, g, q) for t in range(3) for g in range(SG) for q in range(2)]

        def up(t):
            return (m.upto_s, m.after_s)[0:2] if t == 2 else (m.upto, m.after)

        with nc.Block() as block:
            @block.tensor
            def _(pe):
                pe.matmul(psE[:, 0:SH], m.upto[:], m.dta[:, 1, :], start=True, stop=True)
                pe.matmul(psE[:, SH:2 * SH], m.after[:], m.dta[:, 0, :], start=True, stop=True)
                pe.matmul(psE[:, 2 * SH:3 * SH], m.after[:], m.dta[:, 1, :], start=True, stop=True)
                pe.matmul(psE[0:TS, 3 * SH:4 * SH], m.after_s[:], m.dta[0:TS, 2, :], start=True, stop=True)
                pe.matmul(psE[:, 4 * SH:5 * SH], m.after[:], m.dta[:, 0, :], start=True, stop=False)
                pe.matmul(psE[:, 4 * SH:5 * SH], m.ones[:], m.dta[:, 1, :], start=False, stop=True).then_inc(csum, 1)
                for k, (t, g) in enumerate(groups):
                    t0, n = TILES[t]
                    if k >= 2:
                        pe.wait_ge(kept, k - 1)
                    for q in range(4):
                        ins = pe.transpose(psA[k % 2][0:n, q * P:(q + 1) * P], cv[:, 4 * g + q, t0:t0 + n], m.ident[:])
                    ins.then_inc(turned, 1)
                for g in range(SG):
                    pe.wait_ge(xed, g + 1)
                    pe.wait_ge(stkept, g)
                    pe.matmul(psS[:], bt[:, 0, g * NST:(g + 1) * NST], xe[:, 0, g * 512:(g + 1) * 512], start=True, stop=True).then_inc(stsum, 1)
                pe.wait_ge(kept, len(groups))
                k = 0
                for t in range(3):
                    t0, n = TILES[t]
                    upto, _ = up(t)
                    for g in range(SG):
                        tg = t * SG + g
                        pe.wait_ge(cbk, tg)
                        pe.matmul(psC[0:n, 0:n], cv[:, BC + g, t0:t0 + n], cv[:, CCH + g, t0:t0 + n], start=True, stop=True).then_inc(cbs, 1)
                        if t == 1:
                            pe.wait_ge(ytmp, g)
                            pe.wait_ge(stkept, g + 1)
                            pe.matmul(psO[:], cv[:, CCH + g, t0:t0 + n], st0[:, g * 512:(g + 1) * 512], start=True, stop=True).then_inc(yod, 1)
                        if tg >= 2:
                            pe.wait_ge(yk, tg - 1)
                        for q in range(2):
                            pe.wait_ge(lmd, k + 1)
                            pe.wait_ge(decd, max(k - 1, 0))
                            for r in range(4):
                                ins = pe.matmul(psA[k % 2][0:n, r * P:r * P + n], lm[k % 2][0:n, r, 0:n], upto[0:n, 0:n], start=True, stop=True)
                            ins.then_inc(segd, 1)
                            pe.wait_ge(mtd, k + 1)
                            for r in range(4):
                                h = g * SR + 4 * q + r
                                ins = pe.matmul(psY[tg % 2][0:n, (4 * q + r) * HD:(4 * q + r + 1) * HD], dec[k % 2][0:n, r, 0:n],
                                                m.xdt[0:n, t, h * HD:(h + 1) * HD], start=True, stop=True)
                            ins.then_inc(yd, 1)
                            k += 1
                pe.wait_ge(xed, 3 * SG)
                for c in range(XC):
                    if c >= 2:
                        pe.wait_ge(fink, c - 1)
                    o = 256 * (c % 2)
                    bank = psS if c % 2 else psC
                    pe.wait_ge(cbk, 3 * SG)
                    pe.matmul(bank[:, 0:NST], xe[:, 2, c * P:(c + 1) * P], bt[:, 0, (c // 4) * NST:(c // 4 + 1) * NST], start=True, stop=False)
                    pe.matmul(bank[:, 0:NST], xe[:, 1, c * P:(c + 1) * P], bt[:, 1, (c // 4) * NST:(c // 4 + 1) * NST], start=False, stop=True).then_inc(fin, 1)

            @block.scalar
            def _(act):
                act.wait_ge(csum, 1)
                act.activation(eacs[:], psE[:, 0:SH], ACT.Exp).then_inc(cexp, 1)
                act.activation(toend[:, 0:2, :].rearrange("p t h -> p (t h)"), psE[:, SH:3 * SH], ACT.Exp).then_inc(cexp, 1)
                act.activation(toend[0:TS, 2, :], psE[0:TS, 3 * SH:4 * SH], ACT.Exp).then_inc(cexp, 1)
                act.activation(toend[:, 3, :], psE[:, 4 * SH:5 * SH], ACT.Exp).then_inc(cexp, 1)
                for g in range(SG):
                    act.wait_ge(stsum, g + 1)
                    act.copy(st0[:, g * 512:(g + 1) * 512], psS[:]).then_inc(stkept, 1)
                for k, (t, g, q) in enumerate(steps):
                    n = TILES[t][1]
                    act.wait_ge(segd, k + 1)
                    act.wait_ge(yd, max(k - 1, 0))
                    act.activation(dec[k % 2][0:n, :, 0:n], psA[k % 2][0:n, :].rearrange("p (r l) -> p r l", l=P)[:, :, 0:n], ACT.Exp).then_inc(decd, 1)
                for c in range(XC):
                    act.wait_ge(fin, c + 1)
                    act.copy(stout[:, c, :], (psS if c % 2 else psC)[:, 0:NST]).then_inc(fink, 1)

            @block.gpsimd
            def _(pool):
                for k, (t, g, q) in enumerate(steps):
                    n = TILES[t][1]
                    h = g * SR + 4 * q
                    if k >= 2:
                        pool.wait_ge(segd, k - 1)
                    pool.tensor_tensor(lm[k % 2][0:n, :, 0:n], up(t)[1][0:n, 0:n].unsqueeze(1).broadcast_to([n, 4, n]),
                                       m.dta[0:n, t, h:h + 4].unsqueeze(2).broadcast_to([n, 4, n]), ALU.mult).then_inc(lmd, 1)

            @block.vector
            def _(dve):
                for k, (t, g) in enumerate(groups):
                    t0, n = TILES[t]
                    dve.wait_ge(turned, k + 1)
                    if g < 4:
                        dve.tensor_tensor(m.xdt[0:n, t, g * 512:(g + 1) * 512].rearrange("p (h d) -> p h d", d=HD),
                                          psA[k % 2][0:n, :].rearrange("p (h d) -> p h d", d=HD),
                                          m.dt[0:n, t, g * SR:(g + 1) * SR].unsqueeze(2).broadcast_to([n, SR, HD]), ALU.mult).then_inc(kept, 1)
                    else:
                        dve.tensor_copy(bt[0:n, t, :], psA[k % 2][0:n, :]).then_inc(kept, 1)
                dve.wait_ge(kept, len(groups))
                dve.wait_ge(cexp, 4)

                def scaled(dst, t, e, g, n=P):
                    return dve.tensor_tensor(dst.rearrange("p (h d) -> p h d", d=HD),
                                             m.xdt[0:n, t, g * 512:(g + 1) * 512].rearrange("p (h d) -> p h d", d=HD),
                                             toend[0:n, e, g * SR:(g + 1) * SR].unsqueeze(2).broadcast_to([n, SR, HD]), ALU.mult)

                for g in range(SG):
                    scaled(xe[:, 0, g * 512:(g + 1) * 512], 0, 0, g).then_inc(xed, 1)
                k = 0
                for t in range(3):
                    n = TILES[t][1]
                    upto, _ = up(t)
                    for g in range(SG):
                        tg = t * SG + g
                        dve.wait_ge(cbs, tg + 1)
                        if tg >= 2:
                            dve.wait_ge(mtd, 2 * tg - 2)
                        dve.tensor_tensor(cbm[tg % 2][0:n, 0:n], psC[0:n, 0:n], upto[0:n, 0:n], ALU.mult).then_inc(cbk, 1)
                        if t == 1:
                            dve.wait_ge(yod, g + 1)
                            if g:
                                dve.wait_ge(yk, tg)
                            dve.tensor_tensor(yo[:].rearrange("p (h d) -> p h d", d=HD), psO[:].rearrange("p (h d) -> p h d", d=HD),
                                              eacs[:, g * SR:(g + 1) * SR].unsqueeze(2).broadcast_to([P, SR, HD]), ALU.mult).then_inc(ytmp, 1)
                        dve.wait_ge(cbk, tg + 1)
                        for q in range(2):
                            dve.wait_ge(decd, k + 1)
                            v = dec[k % 2][0:n, :, 0:n]
                            dve.tensor_tensor(v, v, cbm[tg % 2][0:n, 0:n].unsqueeze(1).broadcast_to([n, 4, n]), ALU.mult).then_inc(mtd, 1)
                            k += 1
                        dve.wait_ge(yd, k)
                        dst = m.ytok[0:n, t, g * 512:(g + 1) * 512]
                        if t == 1:
                            dve.wait_ge(ytmp, g + 1)
                            dve.tensor_tensor(dst, psY[tg % 2][0:n, :], yo[:], ALU.add).then_inc(yk, 1)
                        else:
                            dve.tensor_copy(dst, psY[tg % 2][0:n, :]).then_inc(yk, 1)
                for g in range(SG):
                    scaled(xe[:, 1, g * 512:(g + 1) * 512], 1, 1, g).then_inc(xed, 1)
                for g in range(SG):
                    scaled(xe[:, 2, g * 512:(g + 1) * 512], 0, 3, g).then_inc(xed, 1)
                for g in range(SG):
                    scaled(m.xes[:, g * 512:(g + 1) * 512], 2, 2, g, TS)

            @block.sync
            def _(sp):
                sp.wait_ge(fink, XC)
                sp.dma_start(a["ssm_prompt"].rearrange("n b (c h) p s -> (h p) (n b c) s", h=2), stout[:]).then_inc(fins, 16)
                sp.wait_ge(fins, 16)


def stage_state(nc, m, a):
    CCH = XC + SG
    with Stage(nc, "state") as s:
        dx = s.sb("dx", [TS, D_IN])
        ea = s.sb("ea", [P, XC, TS])
        bm = s.sb("bm", [TS, NSEQ, SG * NST])
        h0 = [s.sb(f"h0{i}", [P, XC, NST]) for i in range(2)]
        hT = s.sb("hT", [P, XC * P])
        hd = [s.sb(f"hd{i}", [P, XC, NST]) for i in range(2)]
        psE = [s.bank(f"psE{i}") for i in range(2)]
        psT = [s.bank(f"psT{i}") for i in range(2)]
        psO = s.bank("psO")
        psN = [s.bank(f"psN{i}") for i in range(2)]
        loaded = [s.sem(f"loaded{i}") for i in range(2)]
        spread = s.sem("dx_ready")
        esum = s.sem("ea_summed")
        eexp = s.sem("ea_ready")
        bms = s.sem("bm_ready")
        turned = s.sem("turned")
        kept = s.sem("kept")
        yod = s.sem("yoff_made")
        yk = s.sem("yoff_kept")
        hds = s.sem("decayed")
        newd = s.sem("update_made")
        newk = s.sem("state_ready")
        stored = [s.sem(f"stored{i}") for i in range(2)]
        cvf = m.xbc[:].rearrange("p c t -> p (c t)")
        bmf = bm[:].rearrange("p b n -> p (b n)")
        eaf = ea[:].rearrange("p c t -> p (c t)")
        src = a["state_ssm"].rearrange("n b (c h) p s -> (h p) (n b c) s", h=2)
        dst = a["ssm_sample"].rearrange("n b (c h) p s -> (h p) (n b c) s", h=2)
        with nc.Block() as block:
            @block.sync
            def _(sp):
                for i in range(NSEQ // 2):
                    for k in range(2):
                        if i:
                            sp.wait_ge(hds, 2 * i + k - 1)
                            sp.wait_ge(turned, 8 * i + 4 * k - 4)
                        sp.dma_start(h0[k][:], src[:, (2 * i + k) * XC:(2 * i + k + 1) * XC, :]).then_inc(loaded[k], 16)
                    for k in range(2):
                        sp.wait_ge(newk, 8 * i + 4 * k + 4)
                        sp.dma_start(dst[:, (2 * i + k) * XC:(2 * i + k + 1) * XC, :], hd[k][:]).then_inc(stored[k], 16)
                for k in range(2):
                    sp.wait_ge(stored[k], 16 * (NSEQ // 2))

            @block.gpsimd
            def _(pool):
                pool.tensor_copy(dx[:].rearrange("p (h d) -> p h d", d=HD), m.dta[0:TS, 2, :].unsqueeze(2).broadcast_to([TS, SH, HD])).then_inc(spread, 1)
                pool.tensor_tensor(bm[:], m.btok[0:TS, 2, :].unsqueeze(1).broadcast_to([TS, NSEQ, SG * NST]),
                                   m.seq_s[:, 0:TS:SQ].unsqueeze(2).broadcast_to([TS, NSEQ, SG * NST]), ALU.mult).then_inc(bms, 1)
                pool.wait_ge(eexp, 4)
                with pool.Fori(0, NSEQ // 2) as i:
                    for k in range(2):
                        pool.wait_ge(loaded[k], i * 16 + 16)
                        pool.wait_ge(stored[k], i * 16)
                        pool.tensor_tensor(hd[k][:], h0[k][:],
                                           ea[:, :, ds(i * 2 * SQ + (k * SQ + SQ - 1), 1)].broadcast_to([P, XC, NST]), ALU.mult).then_inc(hds, 1)

            @block.tensor
            def _(pe):
                pe.wait_ge(spread, 1)
                for c in range(XC):
                    if c % 4 == 0 and c >= 8:
                        pe.wait_ge(eexp, c // 4 - 1)
                    ins = pe.matmul(psE[(c // 4) % 2][:, (c % 4) * TS:(c % 4 + 1) * TS], dx[:, c * P:(c + 1) * P], m.upto_s[:], start=True, stop=True)
                    if c % 4 == 3:
                        ins.then_inc(esum, 1)
                pe.wait_ge(bms, 1)
                with pe.Fori(0, NSEQ // 2) as i:
                    for k in range(2):
                        pe.wait_ge(loaded[k], i * 16 + 16)
                        for g in range(4):
                            pe.wait_ge(kept, i * 8 + max(4 * k + g - 1, 0)) if (k or g) else pe.wait_ge(kept, i * 8)
                            for q in range(4):
                                ins = pe.transpose(psT[g % 2][:, q * P:(q + 1) * P], h0[k][:, 4 * g + q, :], m.ident[:])
                            ins.then_inc(turned, 1)
                        pe.wait_ge(kept, i * 8 + 4 * k + 4)
                        pe.wait_ge(yk, i * 2 + k)
                        for c in range(XC):
                            ins = pe.matmul(psO[:, c * SQ:(c + 1) * SQ], hT[:, c * P:(c + 1) * P],
                                            cvf[:, ds(i * 2 * SQ + ((CCH + c // 4) * T + TP + k * SQ), SQ)], start=True, stop=True)
                        ins.then_inc(yod, 1)
                        for g in range(4):
                            if g >= 2 or k:
                                pe.wait_ge(newk, i * 8 + 4 * k + g - 1)
                            else:
                                pe.wait_ge(newk, i * 8)
                            for q in range(4):
                                ins = pe.matmul(psN[g % 2][:, q * NST:(q + 1) * NST], m.xes[:, (4 * g + q) * P:(4 * g + q + 1) * P],
                                                bmf[:, ds(i * 2 * SG * NST + (k * SG * NST + g * NST), NST)], start=True, stop=True)
                            ins.then_inc(newd, 1)

            @block.scalar
            def _(act):
                for c in range(4):
                    act.wait_ge(esum, c + 1)
                    act.activation(ea[:, 4 * c:4 * c + 4, :].rearrange("p c t -> p (c t)"), psE[c % 2][:, 0:4 * TS], ACT.Exp).then_inc(eexp, 1)
                with act.Fori(0, NSEQ // 2) as i:
                    for k in range(2):
                        act.wait_ge(yod, i * 2 + k)
                        for g in range(4):
                            act.wait_ge(turned, i * 8 + 4 * k + g + 1)
                            act.copy(hT[:, g * 512:(g + 1) * 512], psT[g % 2][:]).then_inc(kept, 1)

            @block.vector
            def _(dve):
                dve.wait_ge(eexp, 4)
                with dve.Fori(0, NSEQ // 2) as i:
                    for k in range(2):
                        dve.wait_ge(yod, i * 2 + k + 1)
                        dve.tensor_tensor(m.yoff[:, :, ds(i * 2 * SQ + k * SQ, SQ)], psO[:, 0:XC * SQ].rearrange("p (c j) -> p c j", j=SQ),
                                          ea[:, :, ds(i * 2 * SQ + k * SQ, SQ)], ALU.mult).then_inc(yk, 1)
                        dve.wait_ge(hds, i * 2 + k + 1)
                        for g in range(4):
                            dve.wait_ge(newd, i * 8 + 4 * k + g + 1)
                            v = hd[k][:, 4 * g:4 * g + 4, :]
                            dve.tensor_tensor(v, v, psN[g % 2][:].rearrange("p (c n) -> p c n", n=NST), ALU.add).then_inc(newk, 1)


def stage_gate(nc, m, a):
    y, z = m.yT2, m.proj
    with Stage(nc, "gate") as s:
        drow = s.sb("drow", [P, SH])
        dcol = s.sb("dcol", [P, XC])
        sq = s.sb("sq", [P, 4, T])
        var = s.sb("var", [P, SG, T])
        root = s.sb("root", [P, SG, T])
        inv = s.sb("inv", [P, SG, T])
        tmp = s.sb("tmp", [P, SG, T])
        psT = [s.bank(f"psT{i}") for i in range(2)]
        psS = [s.bank(f"psS{i}") for i in range(SG)]
        loaded = s.sem("loaded")
        turned = s.sem("turned")
        kept = s.sem("kept")
        zs = s.sem("z_gated")
        ysd = s.sem("y_ready")
        squared = s.sem("squared")
        summed = s.sem("summed")
        vard = s.sem("var_ready")
        rooted = s.sem("root_ready")
        vecd = Count(s.sem("dve_step"))
        with nc.Block() as block:
            @block.sync
            def _(sp):
                sp.dma_start(drow[:], a["ssd_d"].broadcast_to([P, SH])).then_inc(loaded, 16)

            @block.tensor
            def _(pe):
                for c in range(XC):
                    if c >= 2:
                        pe.wait_ge(kept, c - 1)
                    for t, (t0, n) in enumerate(TILES):
                        ins = pe.transpose(psT[c % 2][:, t0:t0 + n], m.ytok[0:n, t, c * P:(c + 1) * P], m.ident[0:n, 0:n])
                    ins.then_inc(turned, 1)
                for c in range(XC):
                    pe.wait_ge(squared, c + 1)
                    pe.matmul(psS[c // 4][:, 0:T], m.ones[:], sq[:, c % 4, :], start=(c % 4 == 0), stop=(c % 4 == 3)).then_inc(summed, 1)

            @block.scalar
            def _(act):
                act.activation(z[:, 0:XC, :], z[:, 0:XC, :], ACT.Silu).then_inc(zs, 1)
                for c in range(XC):
                    act.wait_ge(ysd, c + 1)
                    if c >= 4:
                        act.wait_ge(summed, c - 3)
                    act.activation(sq[:, c % 4, :], y[:, c, :], ACT.Square).then_inc(squared, 1)
                act.wait_ge(vard, SG)
                act.activation(root[:], var[:], ACT.Sqrt).then_inc(rooted, 1)

            @block.vector
            def _(dve):
                link = chained(dve, vecd)
                dve.wait_ge(loaded, 16)
                for h in range(2):
                    r = slice(64 * h, 64 * h + 64)
                    link(dve.tensor_copy(dcol[r, :], drow[r, h::2]))
                for c in range(XC):
                    dve.wait_ge(turned, c + 1)
                    ins = dve.scalar_tensor_tensor(out=y[:, c, :], in0=m.xbc[:, c, :], scalar=dcol[:, c:c + 1], in1=psT[c % 2][:, 0:T],
                                                   op0=ALU.mult, op1=ALU.add)
                    ins.then_inc(kept, 1)
                dve.wait_ge(kept, XC)
                link(dve.tensor_tensor(y[:, :, TP:T], y[:, :, TP:T], m.yoff[:], ALU.add))
                dve.wait_ge(zs, 1)
                for c in range(XC):
                    dve.tensor_tensor(y[:, c, :], y[:, c, :], z[:, c, :], ALU.mult).then_inc(ysd, 1)
                for g in range(SG):
                    dve.wait_ge(summed, 4 * g + 4)
                    dve.tensor_scalar(var[:, g, :], psS[g][:, 0:T], 1.0 / (D_IN // SG), EPS, ALU.mult, ALU.add).then_inc(vard, 1)
                dve.wait_ge(vard, SG)
                dve.wait_ge(rooted, 1)
                link(dve.reciprocal(inv[:], root[:]))
                link(dve.tensor_tensor(tmp[:], inv[:], inv[:], ALU.mult))
                link(dve.tensor_tensor(tmp[:], tmp[:], var[:], ALU.mult))
                link(dve.tensor_scalar(tmp[:], tmp[:], -0.5, 1.5, ALU.mult, ALU.add))
                link(dve.tensor_tensor(inv[:], inv[:], tmp[:], ALU.mult))
                dve.wait_ge(ysd, XC)
                dve.wait_ge(squared, XC)
                for c in range(XC):
                    dve.scalar_tensor_tensor(out=y[:, c, :], in0=y[:, c, :], scalar=m.vcol[:, 162 + c:163 + c], in1=inv[:, c // 4, :],
                                             op0=ALU.mult, op1=ALU.mult)


def stage_select(nc, m, a, layer):
    q = m.proj
    with Stage(nc, f"sel{layer}") as s:
        krow = s.sb("krow", [P, 2, EH, P])
        kT = s.sb("kT", [P, 2 * EH, P])
        hdup = s.sb("hdup", [P, KC, P])
        qz = s.sb("qz", [P, 2 * EH, P])
        sc = s.sb("sc", [P, 2 * EH, NK])
        sc2 = s.sb("sc2", [P, 2 * EH, NK])
        top = s.sb("top", [P, 2 * EH, TOPK])
        topi = s.sb("topi", [P, 2 * EH, TOPK], U32)
        topf = s.sb("topf", [P, 2 * EH, TOPK])
        cand = s.sb("cand", [P, EH, TOPK * TOPK])
        cand2 = s.sb("cand2", [P, EH, TOPK * TOPK])
        best = s.sb("best", [P, EH, TOPK])
        pick = s.sb("pick", [P, EH, TOPK], U32)
        part = s.sb("part", [P, 2, EH * TOPK], U32)
        partf = s.sb("partf", [P, 2, EH * TOPK])
        found = s.sb("found", [P, 2, EH * TOPK])
        tot = s.sb("tot", [P, EH])
        ps = [s.bank(f"ps{i}") for i in range(4)]
        loaded = s.sem("loaded")
        dup = s.sem("dup_ready")
        kturn = s.sem("k_turned")
        kkept = s.sem("k_kept")
        scored = s.sem("scored")
        skept = s.sem("scores_kept")
        free = s.sem("scores_used")
        less = s.sem("best_shifted")
        expd = s.sem("best_exp")
        vecd = Count(s.sem("dve_step"))
        with nc.Block() as block:
            @block.sync
            def _(sp):
                for j, k in enumerate(("peer_k1", "peer_k2")):
                    sp.dma_start(krow[:, j, :, :], a[k][layer].rearrange("h k d -> k h d")).then_inc(loaded, 16)

            @block.tensor
            def _(pe):
                u = 0
                pe.wait_ge(loaded, 32)
                for g in range(4):
                    for i in range(4):
                        hs = 4 * g + i
                        ins = pe.transpose(ps[g][:, i * P:(i + 1) * P], krow[:, hs % 2, hs // 2, :], m.ident[:])
                    ins.then_inc(kturn, 1)
                pe.wait_ge(dup, 3)
                for t in range(3):
                    for g in range(2):
                        pe.wait_ge(kkept, 2 * t + g + 1)
                        for i in range(4):
                            c = 4 * g + i
                            src = hdup[:, c, :] if t == 2 else m.hT[:, c, t * P:(t + 1) * P]
                            ins = pe.transpose(ps[(2 * t + g) % 4][:, i * P:(i + 1) * P], src, m.ident[:])
                        ins.then_inc(kturn, 1)
                pe.wait_ge(kkept, 10)
                n = 0
                for t in range(3):
                    for g in range(4 if t < 2 else 2):
                        if n >= 4:
                            pe.wait_ge(skept, n - 3)
                        for i in range(4):
                            hs = 4 * g + i
                            o = ps[n % 4][:, i * P:(i + 1) * P]
                            if t < 2:
                                ins = pe.matmul(o, q[:, hs, t * P:(t + 1) * P], kT[:, hs, :], start=True, stop=True)
                            else:
                                pe.matmul(o, qz[:, hs, :], kT[:, hs, :], start=True, stop=False)
                                ins = pe.matmul(o, qz[:, hs + EH, :], kT[:, hs + EH, :], start=False, stop=True)
                        ins.then_inc(scored, 1)
                        n += 1

            @block.scalar
            def _(act):
                for g in range(4):
                    act.wait_ge(kturn, g + 1)
                    act.copy(kT[:, 4 * g:4 * g + 4, :].rearrange("p c k -> p (c k)"), ps[g][:]).then_inc(kkept, 1)
                for t in range(3):
                    for g in range(2):
                        act.wait_ge(kturn, 5 + 2 * t + g)
                        act.copy(m.htok[:, t, g * 512:(g + 1) * 512], ps[(2 * t + g) % 4][:]).then_inc(kkept, 1)
                n = 0
                for t in range(3):
                    H = EH if t < 2 else EH // 2
                    act.wait_ge(free, t)
                    for g in range(4 if t < 2 else 2):
                        act.wait_ge(scored, n + 1)
                        act.copy(sc[:, 4 * g:4 * g + 4, :].rearrange("p c k -> p (c k)"), ps[n % 4][:]).then_inc(skept, 1)
                        n += 1
                    act.wait_ge(less, t + 1)
                    act.activation(best[:, 0:H, :], best[:, 0:H, :], ACT.Exp).then_inc(expd, 1)

            @block.vector
            def _(dve):
                link = chained(dve, vecd)

                def all_done():
                    dve.wait_ge(vecd.sem, vecd.n)

                link(dve.memset(qz[:], 0.0))
                dve.tensor_copy(hdup[:].rearrange("p c (r t) -> p c r t", r=2),
                                m.hT[:, :, TP:T].unsqueeze(2).broadcast_to([P, KC, 2, TS])).then_inc(dup, 1)
                dve.tensor_copy(qz[:, 0:EH, 0:TS], q[:, 0:EH, TP:T]).then_inc(dup, 1)
                dve.tensor_copy(qz[:, EH:2 * EH, TS:P], q[:, EH:2 * EH, TP:T]).then_inc(dup, 1)

                def top16(val, idx, src, src2, n):
                    for half, at in ((0, src), (1, src2)):
                        o = slice(8 * half, 8 * half + 8)
                        for g in range(n):
                            vecd.by(dve.max(val[:, g, o], at[:, g, :]))
                        all_done()
                        for g in range(n):
                            vecd.by(dve.max_index(idx[:, g, o], val[:, g, o], at[:, g, :]))
                            if half == 0:
                                vecd.by(dve.match_replace(src2[:, g, :], val[:, g, o], src[:, g, :], LOWEST))
                        all_done()

                n = 0
                for t in range(3):
                    H = EH if t < 2 else EH // 2
                    n += 4 if t < 2 else 2
                    dve.wait_ge(skept, n)
                    top16(top, topi, sc, sc2, 2 * H)
                    dve.nop().then_inc(free, 1)
                    vecd.by(dve.tensor_copy(topf[:, 0:2 * H, :], topi[:, 0:2 * H, :]))
                    pair = top[:, 0:2 * H, :].rearrange("p (h s) k -> p h s k", s=2)
                    link(dve.tensor_tensor(cand[:, 0:H, :].rearrange("p h (x y) -> p h x y", y=TOPK),
                                           pair[:, :, 0, :].unsqueeze(3).broadcast_to([P, H, TOPK, TOPK]),
                                           pair[:, :, 1, :].unsqueeze(2).broadcast_to([P, H, TOPK, TOPK]), ALU.add))
                    top16(best, pick, cand, cand2, H)
                    top1 = tot[:, 0:H]
                    link(dve.tensor_copy(top1, best[:, 0:H, 0]))
                    link(dve.tensor_tensor(best[:, 0:H, :], best[:, 0:H, :], top1.unsqueeze(2).broadcast_to([P, H, TOPK]), ALU.subtract))
                    dve.nop().then_inc(less, 1)
                    pk = pick[:, 0:H, :].rearrange("p h k -> p (h k)")
                    w = H * TOPK
                    link(dve.tensor_scalar(part[:, 0, 0:w], pk, 4, None, ALU.logical_shift_right))
                    link(dve.tensor_scalar(part[:, 1, 0:w], pk, 15, None, ALU.bitwise_and))
                    link(dve.tensor_copy(partf[:, :, 0:w], part[:, :, 0:w]))
                    tpair = topf[:, 0:2 * H, :].rearrange("p (h s) k -> p h s k", s=2)
                    for side in range(2):
                        hot = cand[:, 0:H, :].rearrange("p h (k x) -> p h k x", x=TOPK)
                        link(dve.tensor_tensor(hot, partf[:, side, 0:w].rearrange("p (h k) -> p h k", k=TOPK).unsqueeze(3).broadcast_to([P, H, TOPK, TOPK]),
                                               m.iota16[:].unsqueeze(1).unsqueeze(1).broadcast_to([P, H, TOPK, TOPK]), ALU.is_equal))
                        link(dve.tensor_tensor(hot, hot, tpair[:, :, side, :].unsqueeze(2).broadcast_to([P, H, TOPK, TOPK]), ALU.mult))
                        link(dve.tensor_reduce(found[:, side, 0:w].rearrange("p (h k) -> p h k", k=TOPK), hot, AX.X, ALU.add))
                    link(dve.scalar_tensor_tensor(out=found[:, 0, 0:w], in0=found[:, 0, 0:w], scalar=float(NK), in1=found[:, 1, 0:w],
                                                  op0=ALU.mult, op1=ALU.add))
                    link(dve.tensor_scalar(m.expert[:, t, 0:w], found[:, 0, 0:w], float(layer * NX), None, ALU.add))
                    dve.wait_ge(expd, t + 1)
                    link(dve.tensor_reduce(top1, best[:, 0:H, :], AX.X, ALU.add))
                    link(dve.reciprocal(top1, top1))
                    link(dve.tensor_tensor(m.gate[:, t, 0:w].rearrange("p (h k) -> p h k", k=TOPK), best[:, 0:H, :],
                                           top1.unsqueeze(2).broadcast_to([P, H, TOPK]), ALU.mult))


def stage_experts(nc, m, a, layer):
    utab, vtab = (a[n].rearrange("l e d -> (l e) d") for n in ("peer_u", "peer_v"))
    g2 = m.mod[layer][:, 5 * KC:6 * KC, :]
    groups = (16, 16, 8)
    base = (0, 16, 32)
    with Stage(nc, f"exp{layer}") as s:
        ur = [s.sb(f"ur{k}", [P, D]) for k in range(GRP)]
        vr = [s.sb(f"vr{k}", [P, D]) for k in range(GRP)]
        ucol = s.sb("ucol", [P, GRP], U32)
        vcolx = s.sb("vcolx", [P, GRP], U32)
        dots = s.sb("dots", [P, GRP])
        act8 = s.sb("act8", [P, GRP])
        w8 = s.sb("w8", [P, GRP])
        diag = [s.sb(f"diag{k}", [P, P]) for k in range(GRP)]
        zero = s.sb("zero", [P, P])
        otok = s.sb("otok", [P, D])
        tmp = s.sb("tmp", [P, KC, TS])
        acc = [[s.bank(f"acc{i}{j}") for j in range(2)] for i in range(2)]
        psT = [s.bank(f"psT{i}") for i in range(2)]
        zeroed = s.sem("zero_ready")
        ucoled = s.sem("ucol_ready")
        vcoled = s.sem("vcol_ready")
        uin = m.gathered[0:GRP]
        vin = m.gathered[GRP:2 * GRP]
        g0 = m.gathered_by
        m.gathered_by += 16 * sum(groups)
        dotted = s.sem("dotted")
        acted = s.sem("gelu_ready")
        weighed = s.sem("weights_ready")
        diagd = s.sem("diag_ready")
        mixed = s.sem("mixed")
        summed = s.sem("tile_summed")
        okept = s.sem("tile_kept")
        oturned = s.sem("tile_turned")
        added = s.sem("tile_added")
        tmpd = s.sem("tmp_ready")
        gate = m.gate[:].rearrange("p t k -> p (t k)")
        with nc.Block() as block:
            @block.gpsimd
            def _(pool):
                for t in range(3):
                    with pool.Fori(base[t], base[t] + groups[t]) as i:
                        apart(pool, zeroed)
                        for k in range(GRP):
                            pool.wait_ge(uin[k], i * 16 + g0)
                        pool.tensor_copy(ucol[:], m.expert[:].rearrange("p t k -> p (t k)")[:, ds(i * GRP, GRP)]).then_inc(ucoled, 1)
                        after, past = value_of(pool, i + 1), value_of(pool, i * GRP)
                        apart(pool, zeroed)
                        pool.wait_ge(ucoled, after)
                        pool.wait_ge(dotted, past)
                        for k in range(GRP):
                            pool.indirect_dma_start(ur[k][:], None, utab, bass.IndirectOffsetOnAxis(ap=ucol[:, k:k + 1], axis=0)).then_inc(uin[k], 16)
                        apart(pool, zeroed)
                        for k in range(GRP):
                            pool.wait_ge(vin[k], i * 16 + g0)
                        pool.tensor_copy(vcolx[:], m.expert[:].rearrange("p t k -> p (t k)")[:, ds(i * GRP, GRP)]).then_inc(vcoled, 1)
                        after, past = value_of(pool, i + 1), value_of(pool, i * GRP)
                        apart(pool, zeroed)
                        pool.wait_ge(vcoled, after)
                        pool.wait_ge(mixed, past)
                        for k in range(GRP):
                            pool.indirect_dma_start(vr[k][:], None, vtab, bass.IndirectOffsetOnAxis(ap=vcolx[:, k:k + 1], axis=0)).then_inc(vin[k], 16)

            @block.tensor
            def _(pe):
                pe.wait_ge(zeroed, 1)
                for t in range(3):
                    b = t % 2
                    if t == 2:
                        pe.wait_ge(okept, 2)
                    for j in range(2):
                        pe.matmul(acc[b][j][:], zero[:], m.htok[:, 0, 0:512], start=True, stop=False, skip_group_check=True)
                    with pe.Fori(base[t], base[t] + groups[t]) as i:
                        for k in range(GRP):
                            pe.wait_ge(diagd, i * GRP + (k + 1))
                            pe.wait_ge(vin[k], i * 16 + (g0 + 16))
                            pe.matmul(acc[b][0][:], diag[k][:], vr[k][:, 0:512], start=False, stop=False, skip_group_check=True)
                            pe.matmul(acc[b][1][:], diag[k][:], vr[k][:, 512:D], start=False, stop=False, skip_group_check=True).then_inc(mixed, 1)
                    for j in range(2):
                        pe.matmul(acc[b][j][:], zero[:], m.htok[:, 0, 0:512], start=False, stop=True, skip_group_check=True).then_inc(summed, 1)
                    pe.wait_ge(okept, 2 * t + 2)
                    pe.wait_ge(added, t)
                    for c in range(KC):
                        if t < 2:
                            ins = pe.transpose(psT[c // 4][:, (c % 4) * P:(c % 4 + 1) * P], otok[:, c * P:(c + 1) * P], m.ident[:])
                        else:
                            ins = pe.matmul(psT[0][:, c * TS:(c + 1) * TS], otok[:, c * P:(c + 1) * P], m.fold[:], start=True, stop=True)
                    ins.then_inc(oturned, 1)

            @block.scalar
            def _(act):
                for t in range(3):
                    with act.Fori(base[t], base[t] + groups[t]) as i:
                        act.wait_ge(dotted, i * GRP + GRP)
                        act.wait_ge(weighed, i)
                        act.activation(act8[:], dots[:], ACT.Gelu).then_inc(acted, 1)
                        act.wait_ge(weighed, i + 1)
                        for k in range(GRP):
                            act.wait_ge(mixed, i * GRP)
                            act.mul(diag[k][:], m.ident[:], w8[:, k:k + 1]).then_inc(diagd, 1)
                    for j in range(2):
                        act.wait_ge(summed, 2 * t + j + 1)
                        act.wait_ge(oturned, t)
                        act.copy(otok[:, j * 512:(j + 1) * 512], acc[t % 2][j][:]).then_inc(okept, 1)

            @block.vector
            def _(dve):
                dve.memset(zero[:], 0.0).then_inc(zeroed, 1)
                for t in range(3):
                    with dve.Fori(base[t], base[t] + groups[t]) as i:
                        dve.wait_ge(acted, i)
                        for k in range(GRP):
                            dve.wait_ge(uin[k], i * 16 + (g0 + 16))
                            dve.tensor_tensor_reduce(ur[k][:], ur[k][:], m.htok[:, t, :], 1.0, 0.0, ALU.mult, ALU.add,
                                                     dots[:, k:k + 1]).then_inc(dotted, 1)
                        dve.wait_ge(acted, i + 1)
                        dve.wait_ge(diagd, i * GRP)
                        dve.tensor_tensor(w8[:], act8[:], gate[:, ds(i * GRP, GRP)], ALU.mult).then_inc(weighed, 1)
                    dve.wait_ge(oturned, t + 1)
                    if t < 2:
                        for c in range(KC):
                            x = m.xT[:, c, t * P:(t + 1) * P]
                            ins = dve.scalar_tensor_tensor(out=x, in0=psT[c // 4][:, (c % 4) * P:(c % 4 + 1) * P], scalar=g2[:, c, 0:1],
                                                           in1=x, op0=ALU.mult, op1=ALU.add)
                        ins.then_inc(added, 1)
                    else:
                        dve.tensor_tensor(tmp[:].rearrange("p c (b j) -> p c b j", j=SQ),
                                          psT[0][:].rearrange("p (c b j) -> p c b j", c=KC, j=SQ),
                                          g2[:, :, 1:NCOND].unsqueeze(3).broadcast_to([P, KC, NSEQ, SQ]), ALU.mult).then_inc(tmpd, 1)
                        dve.wait_ge(tmpd, 1)
                        dve.tensor_tensor(m.xT[:, :, TP:T], m.xT[:, :, TP:T], tmp[:], ALU.add).then_inc(added, 1)


def stage_out(nc, m, a):
    with Stage(nc, "out") as s:
        rows = s.sb("rows", [P, 3, D])
        ps = [s.bank(f"ps{i}") for i in range(4)]
        turned = s.sem("turned")
        kept = s.sem("kept")
        stored = s.sem("stored")
        with nc.Block() as block:
            @block.tensor
            def _(pe):
                k = 0
                for t, (t0, n) in enumerate(TILES):
                    for g in range(2):
                        if k >= 4:
                            pe.wait_ge(kept, k - 3)
                        for q in range(4):
                            ins = pe.transpose(ps[k % 4][0:n, q * P:(q + 1) * P], m.hT[:, 4 * g + q, t0:t0 + n], m.ident[:])
                        ins.then_inc(turned, 1)
                        k += 1

            @block.scalar
            def _(act):
                for k in range(6):
                    t, g = k // 2, k % 2
                    n = TILES[t][1]
                    act.wait_ge(turned, k + 1)
                    act.copy(rows[0:n, t, g * 512:(g + 1) * 512], ps[k % 4][0:n, :]).then_inc(kept, 1)

            @block.sync
            def _(sp):
                yp = a["y_prompt"].rearrange("b t d -> (b t) d")
                for t, (t0, n) in enumerate(TILES):
                    sp.wait_ge(kept, 2 * t + 2)
                    dst = a["y_sample"].rearrange("b t d -> (b t) d") if t == 2 else yp[t0:t0 + n, :]
                    sp.dma_start(dst, rows[0:n, t, :]).then_inc(stored, 16)
                sp.wait_ge(stored, 48)


def peer(nc, m, a, layer):
    mod = m.mod[layer]
    stage_norm(nc, m, f"norm_ffn{layer}", mod[:, 4 * KC:5 * KC, :], mod[:, 3 * KC:4 * KC, :])
    stage_project(nc, m, f"peer_q{layer}", a["peer_wq"][layer], m.hT, m.proj[:], 8)
    stage_select(nc, m, a, layer)
    stage_experts(nc, m, a, layer)


def build(nc, a, upto=99):
    m = Mem()
    with ExitStack() as ctx:
        def sb(c, name, shape, dt=F32):
            return c.enter_context(nc.sbuf_tensor(name, shape, dt))

        m.ident = sb(ctx, "ident", [P, P])
        m.ones = sb(ctx, "ones", [P, P])
        m.upto = sb(ctx, "upto", [P, P])
        m.after = sb(ctx, "after", [P, P])
        m.upto_s = sb(ctx, "upto_s", [TS, TS])
        m.after_s = sb(ctx, "after_s", [TS, TS])
        m.seq_s = sb(ctx, "seq_s", [TS, TS])
        m.far_p = sb(ctx, "far_p", [P, P])
        m.far_s = sb(ctx, "far_s", [96, SQ])
        m.headmask = sb(ctx, "headmask", [96, D_B])
        m.qsel = sb(ctx, "qsel", [96, SQ])
        m.fold = sb(ctx, "fold", [P, TS])
        m.iota16 = sb(ctx, "iota16", [P, TOPK])
        m.rowid = sb(ctx, "rowid", [P, 1])
        m.vcol = sb(ctx, "vcol", [P, 3 * P])
        m.cw = m.vcol[:, 256:256 + 96].rearrange("p (i c) -> p i c", c=CC)
        m.xT = sb(ctx, "xT", [P, KC, T])
        m.hT = sb(ctx, "hT", [P, KC, T])
        m.cT = sb(ctx, "cT", [P, KC, NCOND])
        m.mod = [sb(ctx, f"mod{l}", [P, 6 * KC, NCOND]) for l in range(2)]

        m.gathered_by = 0
        m.gathered = [nc.alloc_semaphore(f"gathered{i}") for i in range(16)]

        stage_setup(nc, m, a)
        stage_ada(nc, m, a, 0)
        stage_ada(nc, m, a, 1)
        mod = m.mod[0]
        stage_norm(nc, m, "norm_mix0", mod[:, KC:2 * KC, :], mod[:, 0:KC, :])
        with ExitStack() as c:
            m.proj = sb(c, "proj_ab", [P, 20, T])
            m.yT = sb(c, "y_ab", [P, KC, T])
            stage_project(nc, m, "ab_in", a["ab_w_in"][0], m.hT, m.proj[:], 10)
            stage_pool(nc, m, a)
            if upto >= 1:
                stage_attend_prompt(nc, m, a)
                stage_attend_sample(nc, m, a)
                stage_project(nc, m, "ab_out", a["ab_w_out"][0], m.yT, None, 4, residual=mod[:, 2 * KC:3 * KC, :])
        if upto >= 2:
            with ExitStack() as c:
                m.proj = sb(c, "peer_q0", [P, 2 * EH, T])
                m.htok = sb(c, "htok0", [P, 3, D])
                m.expert = sb(c, "expert0", [P, 3, P], U32)
                m.gate = sb(c, "gate0", [P, 3, P])
                peer(nc, m, a, 0)
        mod = m.mod[1]
        if upto >= 3:
            stage_norm(nc, m, "norm_mix1", mod[:, KC:2 * KC, :], mod[:, 0:KC, :])
            with ExitStack() as c:
                m.dt = sb(c, "dt", [P, 3, SH])
                m.dta = sb(c, "dta", [P, 3, SH])
                m.proj = sb(c, "proj_ssd", [P, XC + CC, T])
                m.xbc = sb(c, "xbc", [P, CC, T])
                stage_project(nc, m, "ssd_in", a["ssd_w_in"][0], m.hT, m.proj[:], 20)
                stage_conv(nc, m, a)
                m.ytok = m.proj[:].rearrange("p c t -> p (c t)")[:, XC * T:XC * T + 3 * D_IN].rearrange("p (t n) -> p t n", t=3)
                with ExitStack() as c2:
                    m.btok = sb(c2, "btok", [P, 3, SG * NST])
                    m.xes = sb(c2, "xes", [TS, D_IN])
                    m.yoff = sb(c2, "yoff", [P, XC, TS])
                    with ExitStack() as c3:
                        m.xdt = sb(c3, "xdt", [P, 3, D_IN])
                        stage_scan(nc, m, a)
                    stage_state(nc, m, a)
                    m.yT2 = m.xbc_y = sb(c2, "y_ssd", [P, XC, T])
                    stage_gate(nc, m, a)
                    stage_project(nc, m, "ssd_out", a["ssd_w_out"][0], m.yT2, None, 4, kcn=XC, residual=mod[:, 2 * KC:3 * KC, :])
        if upto >= 4:
            with ExitStack() as c:
                m.proj = sb(c, "peer_q1", [P, 2 * EH, T])
                m.htok = sb(c, "htok1", [P, 3, D])
                m.expert = sb(c, "expert1", [P, 3, P], U32)
                m.gate = sb(c, "gate1", [P, 3, P])
                peer(nc, m, a, 1)
        stage_norm(nc, m, "norm_out", m.vcol[:, 128:136], None)
        stage_out(nc, m, a)


INS = ["x_prompt", "x_sample", "cache_sb_k", "cache_sb_v", "state_pool", "state_conv", "state_ssm", "page_table",
       "c_prompt", "c_sample", "ada_w", "ada_b", "norm_mix_g", "norm_ffn_g", "norm_out_g", "ab_w_in", "ab_w_out",
       "pool_w", "pool_scale", "sb_bias", "ssd_w_in", "ssd_conv_w", "ssd_conv_b", "ssd_dt_bias", "ssd_a_log", "ssd_d",
       "ssd_norm_g", "ssd_w_out", "peer_wq", "peer_k1", "peer_k2", "peer_u", "peer_v"]
OUTS = [("y_prompt", (1, TP, D)), ("y_sample", (NSEQ, SQ, D)),
        ("k_prompt", (1, 1, TP, HB, HD)), ("v_prompt", (1, 1, TP, HB, HD)),
        ("k_sample", (1, NSEQ, SQ, HB, HD)), ("v_sample", (1, NSEQ, SQ, HB, HD)),
        ("pool_prompt", (1, 1, NBUF, D_A)), ("pool_sample", (1, NSEQ, NBUF, D_A)),
        ("conv_prompt", (1, 1, 3, CONV)), ("conv_sample", (1, NSEQ, 3, CONV)),
        ("ssm_prompt", (1, 1, SH, 64, NST)), ("ssm_sample", (1, NSEQ, SH, 64, NST))]


def kernel(**inputs):
    import numpy as np
    import concourse.bacc as bacc
    from concourse.bass_utils import run_bass_kernel_spmd

    nc = bacc.Bacc("TRN2", target_bir_lowering=False, num_devices=1)
    arrays, aps = {}, {}
    for name in INS:
        x = np.ascontiguousarray(inputs[name])
        arrays[f"in_{name}_dram"] = x
        aps[name] = nc.dram_tensor(f"in_{name}_dram", x.shape, mybir.dt.from_np(x.dtype), kind="ExternalInput").ap()
    for name, shape in OUTS:
        aps[name] = nc.dram_tensor(f"out_{name}_dram", shape, F32, kind="ExternalOutput").ap()
    build(nc, aps)
    r = run_bass_kernel_spmd(nc, [arrays], core_ids=[0])
    return tuple(r.results[0][f"out_{name}_dram"] for name, _ in OUTS)
```

```python
from contextlib import ExitStack

import concourse.bass as bass
from concourse import mybir

F32 = mybir.dt.float32
I32 = mybir.dt.int32
U32 = mybir.dt.uint32
ALU = mybir.AluOpType
ACT = mybir.ActivationFunctionType
AX = mybir.AxisListType
ds = bass.ds

P = 128
D = 1024
KC = D // P
TP = 256
NSEQ = 8
SQ = 8
TS = NSEQ * SQ
T = TP + TS
NCOND = 1 + NSEQ
EPS = 1e-6
FAR = -1.0e30

D_A = D // 4
HB = 12
HD = 64
D_B = HB * HD
NBUF = 15
PAGES = 8
PAGE = 128
PAST = PAGES * PAGE
ZK = PAST + SQ

D_IN = 2 * D
SH = 32
SG = 4
SR = SH // SG
NST = 128
XC = D_IN // P
CONV = D_IN + 2 * SG * NST
CC = CONV // P

EH = 8
NK = 128
NX = NK * NK
TOPK = 16
LOWEST = -3.0e38
GRP = 8
OPEN = 1

TILES = ((0, 128), (128, 128), (256, 64))


class Count:

    def __init__(self, sem):
        self.sem, self.n = sem, 0

    def by(self, ins, k=1):
        ins.then_inc(self.sem, k)
        self.n += k
        return self.n


class Stage:

    def __init__(self, nc, name):
        self.nc, self.name, self.ctx, self.sems = nc, name, ExitStack(), []

    def __enter__(self):
        return self

    def __exit__(self, *a):
        nums = sorted(x.num for x in self.sems)
        while nums:
            n = 1
            while n < len(nums) and nums[n] == nums[0] + n:
                n += 1
            self.nc.gpsimd.sem_clear(range(nums[0], nums[0] + n))
            nums = nums[n:]
        for x in self.sems:
            self.nc.release_semaphore(x)
        return self.ctx.__exit__(*a)

    def sb(self, name, shape, dt=F32):
        return self.ctx.enter_context(self.nc.sbuf_tensor(f"{self.name}_{name}", shape, dt))

    def bank(self, name, width=512):
        return self.ctx.enter_context(self.nc.psum_tensor(f"{self.name}_{name}", [P, width], F32))

    def sem(self, name, opened=False):
        self.sems.append(self.nc.alloc_semaphore(f"{self.name}_{name}"))
        if opened:
            self.nc.sync.nop().then_inc(self.sems[-1], OPEN)
        return self.sems[-1]


def chained(eng, count):
    def link(ins):
        eng.wait_ge(count.sem, count.by(ins))
    return link


def value_of(eng, x):
    return x if isinstance(x, int) else eng.compute_val(x)


def apart(eng, sem):
    eng.wait_ge(sem, 1)


class Steps:

    def __init__(self, eng, sem, first, passed):
        self.eng, self.sem, self.first, self.passed, self.n = eng, sem, first, passed, 0

    def then(self, *instructions):
        for ins in instructions:
            ins.then_inc(self.sem, 1)
            self.n += 1
        done = value_of(self.eng, self.first + self.n)
        apart(self.eng, self.passed)
        self.eng.wait_ge(self.sem, done)


class Mem:
    pass


def stage_setup(nc, m, a):
    with Stage(nc, "setup") as s:
        xrow = s.sb("xrow", [P, 3, D])
        crow = s.sb("crow", [NCOND, D])
        vrow = s.sb("vrow", [P, 3, P])
        hsel = s.sb("hsel", [96, HB, SQ])
        psx = [s.bank(f"psx{i}") for i in range(2)]
        psv = s.bank("psv")
        loaded = s.sem("loaded")
        pooled = Count(s.sem("pool_step"))
        vecd = Count(s.sem("dve_step"))
        masks = s.sem("masks_made")
        xt = s.sem("x_transposed")
        xc = s.sem("x_copied")
        vt = s.sem("vec_transposed")
        vc = s.sem("vec_copied")
        vz = s.sem("vrow_cleared")
        hz = s.sem("hsel_ready")
        with nc.Block() as block:
            @block.sync
            def _(sp):
                sp.dma_start(xrow[:, 0:2, :], a["x_prompt"].rearrange("b (t p) d -> p (b t) d", p=P)).then_inc(loaded, 16)
                sp.dma_start(xrow[0:TS, 2, :], a["x_sample"].rearrange("b t d -> (b t) d")).then_inc(loaded, 16)
                sp.dma_start(crow[0:1, :], a["c_prompt"]).then_inc(loaded, 16)
                sp.dma_start(crow[1:NCOND, :], a["c_sample"]).then_inc(loaded, 16)
                sp.wait_ge(vz, 1)
                sp.dma_start(vrow[0:96, 0, :], a["ada_b"].rearrange("l (c p) -> (l c) p", p=P)).then_inc(loaded, 16)
                sp.dma_start(vrow[96:112, 0, :], a["norm_mix_g"].rearrange("l (c p) -> (l c) p", p=P)).then_inc(loaded, 16)
                sp.dma_start(vrow[112:128, 0, :], a["norm_ffn_g"].rearrange("l (c p) -> (l c) p", p=P)).then_inc(loaded, 16)
                sp.dma_start(vrow[0:8, 1, :], a["norm_out_g"].rearrange("(c p) -> c p", p=P)).then_inc(loaded, 16)
                sp.dma_start(vrow[8:10, 1, :], a["pool_scale"].rearrange("l (c p) -> (l c) p", p=P)).then_inc(loaded, 16)
                sp.dma_start(vrow[10:34, 1, :], a["ssd_conv_b"].rearrange("l (c p) -> (l c) p", p=P)).then_inc(loaded, 16)
                sp.dma_start(vrow[34:50, 1, :], a["ssd_norm_g"].rearrange("l (c p) -> (l c) p", p=P)).then_inc(loaded, 16)
                sp.dma_start(vrow[0:96, 2, :], a["ssd_conv_w"].rearrange("l i (c p) -> (l i c) p", p=P)).then_inc(loaded, 16)

            @block.gpsimd
            def _(pool):
                link = chained(pool, pooled)
                link(pool.memset(m.ident[:], 0.0))
                link(pool.affine_select(out=m.ident[:], in_=m.ident[:], compare_op=ALU.not_equal, fill=1.0,
                                        base=0, pattern=[[-1, P]], channel_multiplier=1))
                pool.nop().then_inc(masks, 1)
                link(pool.memset(m.ones[:], 1.0))
                link(pool.affine_select(out=m.upto[:], in_=m.ones[:], compare_op=ALU.is_ge, fill=0.0,
                                        base=0, pattern=[[1, P]], channel_multiplier=-1))
                link(pool.affine_select(out=m.after[:], in_=m.ones[:], compare_op=ALU.is_gt, fill=0.0,
                                        base=0, pattern=[[-1, P]], channel_multiplier=1))
                for dst, src in ((m.upto_s, m.upto), (m.after_s, m.after), (m.seq_s, m.ones)):
                    v = dst[:].rearrange("p (b j) -> p b j", j=SQ)
                    w = src[0:TS, 0:TS].rearrange("p (b j) -> p b j", j=SQ)
                    link(pool.affine_select(out=v, in_=w, compare_op=ALU.is_ge, fill=0.0,
                                            base=0, pattern=[[-SQ, NSEQ], [0, SQ]], channel_multiplier=1))
                    link(pool.affine_select(out=v, in_=v, compare_op=ALU.is_ge, fill=0.0,
                                            base=SQ - 1, pattern=[[SQ, NSEQ], [0, SQ]], channel_multiplier=-1))
                link(pool.memset(m.far_p[:], 0.0))
                link(pool.affine_select(out=m.far_p[:], in_=m.far_p[:], compare_op=ALU.is_gt, fill=FAR,
                                        base=0, pattern=[[-1, P]], channel_multiplier=1))
                hm = m.headmask[:].rearrange("p (h d) -> p h d", d=HD)
                link(pool.memset(m.headmask[:], 1.0))
                link(pool.affine_select(out=hm, in_=hm, compare_op=ALU.is_ge, fill=0.0,
                                        base=0, pattern=[[-SQ, HB], [0, HD]], channel_multiplier=1))
                link(pool.affine_select(out=hm, in_=hm, compare_op=ALU.is_ge, fill=0.0,
                                        base=SQ - 1, pattern=[[SQ, HB], [0, HD]], channel_multiplier=-1))
                link(pool.memset(hsel[:], 1.0))
                link(pool.affine_select(out=hsel[:], in_=hsel[:], compare_op=ALU.is_gt, fill=0.0,
                                        base=0, pattern=[[-SQ, HB], [-1, SQ]], channel_multiplier=1))
                link(pool.affine_select(out=hsel[:], in_=hsel[:], compare_op=ALU.is_ge, fill=0.0,
                                        base=SQ - 1, pattern=[[SQ, HB], [0, SQ]], channel_multiplier=-1))
                pool.nop().then_inc(hz, 1)
                link(pool.iota(m.iota16[:], pattern=[[1, TOPK]], base=0, channel_multiplier=0,
                               allow_small_or_imprecise_dtypes=True))
                link(pool.iota(m.rowid[:], pattern=[[0, 1]], base=0, channel_multiplier=1,
                               allow_small_or_imprecise_dtypes=True))

            @block.tensor
            def _(pe):
                pe.wait_ge(masks, 1)
                pe.wait_ge(loaded, 16 * 12)
                for g, c in enumerate(range(0, KC, 1)):
                    if g >= 2:
                        pe.wait_ge(xc, g - 1)
                    for t0, n in TILES:
                        t = t0 // P
                        ins = pe.transpose(psx[g % 2][:, t0:t0 + n], xrow[0:n, t, c * P:(c + 1) * P], m.ident[0:n, 0:n])
                    ins.then_inc(xt, 1)
                for c in range(KC):
                    pe.transpose(psv[:, c * NCOND:(c + 1) * NCOND], crow[:, c * P:(c + 1) * P], m.ident[0:NCOND, 0:NCOND])
                for v in range(3):
                    ins = pe.transpose(psv[:, (v + 1) * P:(v + 2) * P], vrow[:, v, :], m.ident[:])
                ins.then_inc(vt, 1)

            @block.vector
            def _(dve):
                dve.memset(vrow[:], 0.0).then_inc(vz, 1)
                dve.wait_ge(masks, 1)
                dve.tensor_tensor(m.fold[:], m.ident[:, 0:TS], m.ident[:, TS:P], ALU.add).then_inc(vecd.sem, 1)
                dve.tensor_reduce(m.qsel[:], m.ident[0:96, 0:96].rearrange("p (h q) -> p q h", q=SQ), AX.X, ALU.add).then_inc(vecd.sem, 1)
                dve.wait_ge(hz, 1)
                link = chained(dve, vecd)
                vecd.n = 2
                link(dve.tensor_reduce(m.far_s[:], hsel[:].rearrange("p h j -> p j h"), AX.X, ALU.add))
                link(dve.tensor_scalar(m.far_s[:], m.far_s[:], 1.0, -FAR, ALU.subtract, ALU.mult))
                for g in range(KC):
                    dve.wait_ge(xt, g + 1)
                    dve.tensor_copy(m.xT[:, g, :], psx[g % 2][:, 0:T]).then_inc(xc, 1)
                dve.wait_ge(vt, 1)
                dve.tensor_copy(m.cT[:].rearrange("p c n -> p (c n)"), psv[:, 0:KC * NCOND]).then_inc(vc, 1)
                dve.tensor_copy(m.vcol[:], psv[:, P:4 * P]).then_inc(vc, 1)


class Ada:
    STEPS = 6

    def __init__(self, s, m, a, layer, psr, pst):
        self.m, self.layer, self.psr, self.pst = m, layer, psr, pst
        self.w = a["ada_w"][layer].rearrange("(c p) n -> p c n", p=P)
        self.wt = [s.sb(f"w{i}", [P, KC, 512]) for i in range(2)]
        self.row = [s.sb(f"row{i}", [NCOND, 512]) for i in range(2)]
        self.loaded = [s.sem(f"w_loaded{i}") for i in range(2)]
        self.made = [s.sem(f"row_made{i}", opened=True) for i in range(2)]
        self.copied = [s.sem(f"row_copied{i}", opened=True) for i in range(2)]
        self.turned = [s.sem(f"row_turned{i}", opened=True) for i in range(2)]
        self.added = [s.sem(f"bias_added{i}", opened=True) for i in range(2)]
        self.stepped = Count(s.sem("scale_step"))

    def load(self, sp, i, k):
        sp.wait_ge(self.made[k], OPEN + i)
        sp.dma_start(self.wt[k][:], self.w[:, :, ds(i * 1024 + k * 512, 512)]).then_inc(self.loaded[k], 16)

    def make(self, pe, i, k):
        bank = self.psr[k % len(self.psr)]
        pe.wait_ge(self.loaded[k], i * 16 + 16)
        if len(self.psr) == 2:
            pe.wait_ge(self.copied[k], OPEN + i)
        else:
            pe.wait_ge(self.copied[1 - k], OPEN + i + k)
        for c in range(KC):
            ins = pe.matmul(bank[0:NCOND, :], self.m.cT[:, c, :], self.wt[k][:, c, :], start=(c == 0), stop=(c == KC - 1))
        ins.then_inc(self.made[k], 1)

    def turn(self, pe, i, k):
        bank = self.pst[k % len(self.pst)]
        there = value_of(pe, OPEN + i + 1)
        free = value_of(pe, OPEN + i + (k if len(self.pst) == 1 else 0))
        apart(pe, self.loaded[0])
        pe.wait_ge(self.copied[k], there)
        pe.wait_ge(self.added[k if len(self.pst) == 2 else 1 - k], free)
        for q in range(4):
            ins = pe.transpose(bank[:, q * NCOND:(q + 1) * NCOND], self.row[k][:, q * P:(q + 1) * P],
                               self.m.ident[0:NCOND, 0:NCOND])
        ins.then_inc(self.turned[k], 1)

    def copy(self, act, i, k):
        act.wait_ge(self.made[k], OPEN + i + 1)
        act.wait_ge(self.turned[k], OPEN + i)
        act.copy(self.row[k][:], self.psr[k % len(self.psr)][0:NCOND, :]).then_inc(self.copied[k], 1)

    def add(self, dve, i, k):
        mod = self.m.mod[self.layer][:].rearrange("p c n -> p (c n)")
        dve.wait_ge(self.turned[k], OPEN + i + 1)
        dve.tensor_tensor(mod[:, ds(i * (8 * NCOND) + k * 4 * NCOND, 4 * NCOND)].rearrange("p (c n) -> p c n", n=NCOND),
                          self.pst[k % len(self.pst)][:, 0:4 * NCOND].rearrange("p (c n) -> p c n", n=NCOND),
                          self.m.vcol[:, ds(i * 8 + (48 * self.layer + 4 * k), 4)].unsqueeze(2).broadcast_to([P, 4, NCOND]),
                          ALU.add).then_inc(self.added[k], 1)

    def scales(self, dve):
        link = chained(dve, self.stepped)
        for k in range(2):
            dve.wait_ge(self.added[k], OPEN + self.STEPS)
        for part, g0 in ((1, 96), (4, 112)):
            sc = self.m.mod[self.layer][:, part * KC:(part + 1) * KC, :]
            g = self.m.vcol[:, g0 + self.layer * KC:g0 + self.layer * KC + KC].unsqueeze(2).broadcast_to([P, KC, NCOND])
            link(dve.tensor_scalar(sc, sc, 1.0, None, ALU.add))
            link(dve.tensor_tensor(sc, sc, g, ALU.mult))


def stage_ada(nc, m, a, layer):
    with Stage(nc, f"ada{layer}") as s:
        ada = Ada(s, m, a, layer, [s.bank(f"psr{i}") for i in range(2)], [s.bank(f"pst{i}") for i in range(2)])
        with nc.Block() as block:
            @block.sync
            def _(sp):
                with sp.Fori(0, Ada.STEPS) as i:
                    for k in range(2):
                        ada.load(sp, i, k)

            @block.tensor
            def _(pe):
                with pe.Fori(0, Ada.STEPS) as i:
                    for k in range(2):
                        ada.make(pe, i, k)
                    for k in range(2):
                        ada.turn(pe, i, k)

            @block.scalar
            def _(act):
                with act.Fori(0, Ada.STEPS) as i:
                    for k in range(2):
                        ada.copy(act, i, k)

            @block.vector
            def _(dve):
                with dve.Fori(0, Ada.STEPS) as i:
                    for k in range(2):
                        ada.add(dve, i, k)
                ada.scales(dve)


def stage_norm(nc, m, name, scale, shift):
    with Stage(nc, name) as s:
        sq = s.sb("sq", [P, KC, T])
        var = s.sb("var", [P, T])
        root = s.sb("root", [P, T])
        inv = s.sb("inv", [P, T])
        tmp = s.sb("tmp", [P, T])
        pss = s.bank("pss")
        squared = s.sem("squared")
        summed = s.sem("summed")
        vard = s.sem("var_ready")
        rooted = s.sem("root_ready")
        vecd = Count(s.sem("dve_step"))
        with nc.Block() as block:
            @block.scalar
            def _(act):
                for c in range(KC):
                    act.activation(sq[:, c, :], m.xT[:, c, :], ACT.Square).then_inc(squared, 1)
                act.wait_ge(vard, 1)
                act.activation(root[:], var[:], ACT.Sqrt).then_inc(rooted, 1)

            @block.tensor
            def _(pe):
                for c in range(KC):
                    pe.wait_ge(squared, c + 1)
                    ins = pe.matmul(pss[:, 0:T], m.ones[:], sq[:, c, :], start=(c == 0), stop=(c == KC - 1))
                ins.then_inc(summed, 1)

            @block.vector
            def _(dve):
                link = chained(dve, vecd)
                dve.wait_ge(summed, 1)
                dve.tensor_scalar(var[:], pss[:, 0:T], 1.0 / D, EPS, ALU.mult, ALU.add).then_inc(vard, 1)
                dve.wait_ge(rooted, 1)
                link(dve.reciprocal(inv[:], root[:]))
                link(dve.tensor_tensor(tmp[:], inv[:], inv[:], ALU.mult))
                link(dve.tensor_tensor(tmp[:], tmp[:], var[:], ALU.mult))
                link(dve.tensor_scalar(tmp[:], tmp[:], -0.5, 1.5, ALU.mult, ALU.add))
                link(dve.tensor_tensor(inv[:], inv[:], tmp[:], ALU.mult))
                link(dve.tensor_tensor(m.hT[:], m.xT[:], inv[:].unsqueeze(1).broadcast_to([P, KC, T]), ALU.mult))
                if shift is None:
                    link(dve.tensor_tensor(m.hT[:], m.hT[:], scale.unsqueeze(2).broadcast_to([P, KC, T]), ALU.mult))
                    return
                for c in range(KC):
                    ins = dve.tensor_scalar(m.hT[:, c, 0:TP], m.hT[:, c, 0:TP], scale[:, c, 0:1], shift[:, c, 0:1], ALU.mult, ALU.add)
                vecd.by(ins)
                hs = m.hT[:, :, TP:T].rearrange("p c (b j) -> p c b j", j=SQ)
                link(dve.tensor_tensor(hs, hs, scale[:, :, 1:NCOND].unsqueeze(3).broadcast_to([P, KC, NSEQ, SQ]), ALU.mult))
                link(dve.tensor_tensor(hs, hs, shift[:, :, 1:NCOND].unsqueeze(3).broadcast_to([P, KC, NSEQ, SQ]), ALU.add))


def stage_project(nc, m, name, w, src, out, blocks, kcn=KC, residual=None):
    wv = w.rearrange("(c p) n -> p c n", p=P)
    with Stage(nc, name) as s:
        wt = [s.sb(f"w{i}", [P, kcn, 256]) for i in range(2)]
        tmp = s.sb("tmp", [P, TS])
        ps = [[s.bank(f"ps{i}{j}") for j in range(2)] for i in range(2)]
        loaded = [s.sem(f"w_loaded{i}") for i in range(2)]
        made = [s.sem(f"made{i}", opened=True) for i in range(2)]
        taken = [s.sem(f"taken{i}", opened=True) for i in range(2)]
        vecd = s.sem("tmp_ready")
        with nc.Block() as block:
            @block.sync
            def _(sp):
                with sp.Fori(0, blocks // 2) as i:
                    for k in range(2):
                        sp.wait_ge(made[k], OPEN + i * 2)
                        sp.dma_start(wt[k][:], wv[:, :, ds(i * 512 + k * 256, 256)]).then_inc(loaded[k], 16)

            @block.tensor
            def _(pe):
                with pe.Fori(0, blocks // 2) as i:
                    for k in range(2):
                        pe.wait_ge(loaded[k], i * 16 + 16)
                        pe.wait_ge(taken[k], OPEN + i * 2)
                        for j in range(2):
                            for c in range(kcn):
                                ins = pe.matmul(ps[k][j][:, 0:T], wt[k][:, c, j * P:(j + 1) * P], src[:, c, :],
                                                start=(c == 0), stop=(c == kcn - 1))
                            ins.then_inc(made[k], 1)

            if residual is None:
                @block.scalar
                def _(act):
                    flat = out.rearrange("p c t -> p (c t)")
                    with act.Fori(0, blocks // 2) as i:
                        for k in range(2):
                            for j in range(2):
                                act.wait_ge(made[k], OPEN + i * 2 + j + 1)
                                act.copy(flat[:, ds(i * 4 * T + (2 * k + j) * T, T)], ps[k][j][:, 0:T]).then_inc(taken[k], 1)
            else:
                @block.vector
                def _(dve):
                    for i in range(blocks // 2):
                        for k in range(2):
                            for j in range(2):
                                n = 4 * i + 2 * k + j
                                dve.wait_ge(made[k], OPEN + i * 2 + j + 1)
                                dve.scalar_tensor_tensor(out=m.xT[:, n, 0:TP], in0=ps[k][j][:, 0:TP], scalar=residual[:, n, 0:1],
                                                         in1=m.xT[:, n, 0:TP], op0=ALU.mult, op1=ALU.add)
                                if n:
                                    dve.wait_ge(taken[((n - 1) // 2) % 2], OPEN + 2 * ((n - 1) // 4) + (n - 1) % 2 + 1)
                                dve.tensor_tensor(tmp[:].rearrange("p (b j) -> p b j", j=SQ),
                                                  ps[k][j][:, TP:T].rearrange("p (b j) -> p b j", j=SQ),
                                                  residual[:, n, 1:NCOND].unsqueeze(2).broadcast_to([P, NSEQ, SQ]), ALU.mult).then_inc(vecd, 1)
                                dve.wait_ge(vecd, n + 1)
                                dve.tensor_tensor(m.xT[:, n, TP:T], m.xT[:, n, TP:T], tmp[:], ALU.add).then_inc(taken[k], 1)


def stage_pool(nc, m, a):
    pr = m.proj
    with Stage(nc, "pool") as s:
        kv = s.sb("kv", [P, 3, 2 * D_B])
        arow = s.sb("arow", [P, 2, D_A])
        buf = s.sb("buf", [NSEQ * NBUF, D_A])
        full_p = s.sb("full_p", [P, 2, NBUF + TP])
        full_s = s.sb("full_s", [P, 2, NSEQ, NBUF + SQ])
        sum_p = [s.sb(f"sum_p{i}", [P, 2, NBUF + TP]) for i in range(4)]
        sum_s = [s.sb(f"sum_s{i}", [P, 2, NSEQ, NBUF + SQ]) for i in range(4)]
        icnt = s.sb("icnt", [P, 2, TP])
        diff = s.sb("diff", [P, 2, T])
        pw = s.sb("pw", [P, 2, P])
        ps = [s.bank(f"ps{i}") for i in range(4)]
        psb = s.bank("psb")
        psy = [s.bank(f"psy{i}") for i in range(2)]
        loaded = s.sem("loaded")
        cleared = s.sem("cleared")
        counted = s.sem("count_written")
        turned = s.sem("turned")
        kept = s.sem("kept")
        bturned = s.sem("buf_turned")
        differ = s.sem("diff_ready")
        mixed = s.sem("mixed")
        scaled = s.sem("scaled")
        stored = s.sem("stored")
        vecd = Count(s.sem("dve_step"))
        groups = [(t, c) for t in range(3) for c in range(8, 20, 4)]
        sp_stores = 0
        with nc.Block() as block:
            @block.sync
            def _(sp):
                sp.wait_ge(cleared, 1)
                sp.dma_start(buf[:], a["state_pool"].rearrange("n b i d -> (n b i) d")).then_inc(loaded, 16)
                for g in range(4):
                    o = 64 * (g % 2)
                    sp.dma_start(pw[o:o + 64, g // 2, o:o + 64], a["pool_w"][0, g]).then_inc(loaded, 16)
                sp.wait_ge(kept, 11)
                for t, (t0, n) in enumerate(TILES):
                    for j, part in enumerate("kv"):
                        dst = a[f"{part}_sample"] if t == 2 else a[f"{part}_prompt"]
                        row0 = 0 if t == 2 else t0
                        sp.dma_start(dst.rearrange("n b t h d -> (n b t) (h d)")[row0:row0 + n, :],
                                     kv[0:n, t, j * D_B:(j + 1) * D_B]).then_inc(stored, 16)
                sp.dma_start(a["pool_prompt"].rearrange("n b i d -> (n b i) d"), arow[P - NBUF:P, 0, :]).then_inc(stored, 16)
                for b in range(NSEQ):
                    sp.dma_start(a["pool_sample"][0, b, NBUF - SQ:NBUF, :], arow[b * SQ:(b + 1) * SQ, 1, :]).then_inc(stored, 16)
                sp.dma_start(a["pool_sample"].rearrange("n b i d -> (n b) i d")[:, 0:NBUF - SQ, :],
                             a["state_pool"].rearrange("n b i d -> (n b) i d")[:, SQ:NBUF, :]).then_inc(stored, 16)
                sp.wait_ge(stored, 16 * 16)

            @block.gpsimd
            def _(pool):
                pool.iota(icnt[:], pattern=[[0, 2], [1, TP]], base=1, channel_multiplier=0,
                          allow_small_or_imprecise_dtypes=True).then_inc(counted, 1)

            @block.tensor
            def _(pe):
                for g, (t, c0) in enumerate(groups):
                    t0, n = TILES[t]
                    if g >= 4:
                        pe.wait_ge(kept, g - 3)
                    for q in range(4):
                        ins = pe.transpose(ps[g % 4][0:n, q * P:(q + 1) * P], pr[:, c0 + q, t0:t0 + n], m.ident[:])
                    ins.then_inc(turned, 1)
                for j, (t0, n) in enumerate(TILES[1:]):
                    g = 9 + j
                    pe.wait_ge(kept, g - 3)
                    for q in range(2):
                        ins = pe.transpose(ps[g % 4][0:n, q * P:(q + 1) * P], pr[:, q, t0:t0 + n], m.ident[:])
                    ins.then_inc(turned, 1)
                pe.wait_ge(loaded, 16 * 5)
                for q in range(2):
                    ins = pe.transpose(psb[:, q * 128:q * 128 + 120], buf[:, q * P:(q + 1) * P], m.ident[0:120, 0:120])
                ins.then_inc(bturned, 1)
                pe.wait_ge(differ, 1)
                for q in range(2):
                    pe.matmul(psy[q][:, 0:T], pw[:, q, :], diff[:, q, :], start=True, stop=True).then_inc(mixed, 1)

            @block.scalar
            def _(act):
                for g, (t, c0) in enumerate(groups):
                    n = TILES[t][1]
                    act.wait_ge(turned, g + 1)
                    act.copy(kv[0:n, t, (c0 - 8) * P:(c0 - 4) * P], ps[g % 4][0:n, :]).then_inc(kept, 1)
                for j, (t0, n) in enumerate(TILES[1:]):
                    act.wait_ge(turned, 10 + j)
                    act.copy(arow[0:n, j, :], ps[(9 + j) % 4][0:n, 0:D_A]).then_inc(kept, 1)
                for q in range(2):
                    act.wait_ge(mixed, q + 1)
                    act.mul(m.yT[:, q, :], psy[q][:, 0:T], m.vcol[:, 136 + q:137 + q]).then_inc(scaled, 1)

            @block.vector
            def _(dve):
                link = chained(dve, vecd)
                dve.memset(pw[:], 0.0).then_inc(cleared, 1)
                link(dve.memset(full_p[:, :, 0:NBUF], 0.0))
                link(dve.tensor_copy(full_p[:, :, NBUF:], pr[:, 0:2, 0:TP]))
                link(dve.tensor_copy(full_s[:, :, :, NBUF:], pr[:, 0:2, TP:T].rearrange("p c (b j) -> p c b j", j=SQ)))
                dve.wait_ge(bturned, 1)
                for q in range(2):
                    link(dve.tensor_copy(full_s[:, q, :, 0:NBUF], psb[:, q * 128:q * 128 + 120].rearrange("p (b i) -> p b i", i=NBUF)))
                at = 0
                src_p, src_s = full_p, full_s
                for lvl in range(4):
                    by = 1 << lvl
                    lo = at + by
                    link(dve.tensor_tensor(sum_p[lvl][:, :, lo:], src_p[:, :, lo:], src_p[:, :, at:NBUF + TP - by], ALU.add))
                    link(dve.tensor_tensor(sum_s[lvl][:, :, :, lo:], src_s[:, :, :, lo:], src_s[:, :, :, at:NBUF + SQ - by], ALU.add))
                    src_p, src_s, at = sum_p[lvl], sum_s[lvl], lo
                dve.wait_ge(counted, 1)
                for g in range(4):
                    o, q, w = 64 * (g % 2), g // 2, 2 << g
                    link(dve.tensor_scalar(icnt[o:o + 64, q, :], icnt[o:o + 64, q, :], float(w), None, ALU.min))
                link(dve.reciprocal(icnt[:], icnt[:]))
                for g in range(4):
                    o, q, w = 64 * (g % 2), g // 2, 2 << g
                    rows = slice(o, o + 64)
                    link(dve.tensor_tensor(diff[rows, q, 0:TP], sum_p[g][rows, q, NBUF:], icnt[rows, q, :], ALU.mult))
                    link(dve.tensor_tensor(diff[rows, q, 0:TP], diff[rows, q, 0:TP], pr[rows, q, 0:TP], ALU.subtract))
                    link(dve.scalar_tensor_tensor(out=diff[rows, q, TP:T].rearrange("p (b j) -> p b j", j=SQ),
                                                  in0=sum_s[g][rows, q, :, NBUF:], scalar=1.0 / w,
                                                  in1=pr[rows, q, TP:T].rearrange("p (b j) -> p b j", j=SQ),
                                                  op0=ALU.mult, op1=ALU.subtract))
                dve.nop().then_inc(differ, 1)


def stage_attend_prompt(nc, m, a):
    W = 3 * P
    pr = m.proj
    NP = HB // 2
    with Stage(nc, "attp") as s:
        bias = s.sb("bias", [P, HB])
        q = s.sb("q", [P, 2, TP])
        v = s.sb("v", [P, 2, P])
        vt = s.sb("vt", [P, TP])
        z = s.sb("z", [P, 2, W])
        e = s.sb("e", [P, 2, W])
        sp_ = s.sb("softplus", [P, 2, W])
        su = s.sb("suffix", [P, 2, W])
        wT = s.sb("wT", [P, 2, W])
        zero = s.sb("zero", [P, TP])
        psz = [s.bank(f"psz{i}") for i in range(2)]
        psw = [s.bank(f"psw{i}") for i in range(2)]
        psv = s.bank("psv")
        pso = s.bank("pso")
        ada = Ada(s, m, a, 1, [s.bank("psr")], [s.bank("pst")])
        assert Ada.STEPS == NP
        loaded = s.sem("bias_loaded")
        staged = s.sem("operands_staged")
        scored = s.sem("scored")
        vturned = s.sem("v_turned", opened=True)
        vkept = s.sem("v_kept", opened=True)
        biased = s.sem("biased", opened=True)
        masked = s.sem("masked")
        logged = s.sem("logged")
        actd = s.sem("act_step")
        softp = s.sem("softplus_ready", opened=True)
        scanned = s.sem("scanned")
        expo = s.sem("exponent_ready")
        weighed = s.sem("weights_ready", opened=True)
        wturned = s.sem("weights_turned", opened=True)
        wkept = s.sem("weights_kept", opened=True)
        mixed = s.sem("mixed", opened=True)
        outs = s.sem("outputs_kept", opened=True)
        zs = s.sem("zero_ready")
        flat = pr[:].rearrange("p c t -> p (c t)")
        yflat = m.yT[:].rearrange("p c t -> p (c t)")
        with nc.Block() as block:
            @block.sync
            def _(sp):
                sp.dma_start(bias[:], a["sb_bias"].broadcast_to([P, HB])).then_inc(loaded, 16)
                with sp.Fori(0, NP) as i:
                    for k in range(2):
                        ada.load(sp, i, k)

            @block.tensor
            def _(pe):
                with pe.Fori(0, NP) as i:
                    pe.wait_ge(staged, i * 3 + 3)
                    pe.wait_ge(biased, OPEN + i * 2)
                    for h in range(2):
                        pe.matmul(psz[h][:, 0:P], q[:, h, 0:P], flat[:, ds(i * T + 8 * T, P)], start=True, stop=True)
                        pe.matmul(psz[h][:, P:W], q[:, h, P:TP], flat[:, ds(i * T + 8 * T, TP)], start=True, stop=True).then_inc(scored, 1)
                    pe.wait_ge(vkept, OPEN + i)
                    for t in range(2):
                        ins = pe.transpose(psv[:, t * P:(t + 1) * P], vt[:, t * P:(t + 1) * P], m.ident[:])
                    ins.then_inc(vturned, 1)
                    ada.make(pe, i, 0)
                    ada.make(pe, i, 1)
                    ada.turn(pe, i, 0)
                    for h in range(2):
                        pe.wait_ge(weighed, OPEN + i * 2 + h + 1)
                        pe.wait_ge(wkept, OPEN + i * 2 + h)
                        for b in range(3):
                            ins = pe.transpose(psw[h][:, b * P:(b + 1) * P], z[:, h, b * P:(b + 1) * P], m.ident[:])
                        ins.then_inc(wturned, 1)
                    pe.wait_ge(vkept, OPEN + i + 1)
                    pe.wait_ge(outs, OPEN + i * 2)
                    for h in range(2):
                        pe.wait_ge(wkept, OPEN + i * 2 + h + 1)
                        pe.matmul(pso[:, h * TP:(h + 1) * TP], v[:, 0, :], wT[:, h, 0:TP], start=True, stop=False)
                        pe.matmul(pso[:, h * TP + P:(h + 1) * TP], v[:, 1, :], wT[:, h, TP:W], start=False, stop=True).then_inc(mixed, 1)
                    ada.turn(pe, i, 1)

            @block.scalar
            def _(act):
                act.wait_ge(loaded, 16)
                bflat = bias[:]
                with act.Fori(0, NP) as i:
                    act.wait_ge(weighed, OPEN + i * 2)
                    for h in range(2):
                        act.wait_ge(scored, i * 2 + h + 1)
                        act.wait_ge(wturned, OPEN + i * 2)
                        act.activation(z[:, h, :], psz[h][:, 0:W], ACT.Identity, bias=bflat[:, ds(i * 2 + h, 1)],
                                       scale=HD ** -0.5).then_inc(biased, 1)
                    act.wait_ge(masked, i + 1)
                    act.wait_ge(softp, OPEN + i)
                    act.activation(e[:], z[:], ACT.Abs).then_inc(actd, 1)
                    act.wait_ge(actd, i * 2 + 1)
                    act.activation(e[:], e[:], ACT.Exp, scale=-1.0).then_inc(actd, 1)
                    act.wait_ge(actd, i * 2 + 2)
                    act.activation(e[:], e[:], ACT.Ln, bias=1.0).then_inc(logged, 1)
                    ada.copy(act, i, 0)
                    for h in range(2):
                        act.wait_ge(expo, i * 2 + h + 1)
                        act.activation(z[:, h, :], z[:, h, :], ACT.Exp).then_inc(weighed, 1)
                    ada.copy(act, i, 1)
                    for h in range(2):
                        act.wait_ge(wturned, OPEN + i * 2 + h + 1)
                        act.wait_ge(mixed, OPEN + i * 2 + h)
                        act.copy(wT[:, h, :], psw[h][:, 0:W]).then_inc(wkept, 1)

            @block.vector
            def _(dve):
                dve.memset(zero[:], 0.0).then_inc(zs, 1)
                dve.memset(q[:], 0.0).then_inc(zs, 1)
                dve.wait_ge(zs, 2)
                with dve.Fori(0, NP) as i:
                    dve.wait_ge(vturned, OPEN + i)
                    dve.wait_ge(mixed, OPEN + i * 2)
                    for h in range(2):
                        r = slice(64 * h, 64 * h + 64)
                        dve.tensor_copy(q[r, h, :], flat[r, ds(i * T + 2 * T, TP)]).then_inc(staged, 1)
                    dve.tensor_copy(vt[:], flat[:, ds(i * T + 14 * T, TP)]).then_inc(staged, 1)
                    dve.wait_ge(vturned, OPEN + i + 1)
                    dve.tensor_copy(v[:].rearrange("p t d -> p (t d)"), psv[:, 0:TP]).then_inc(vkept, 1)
                    dve.wait_ge(biased, OPEN + i * 2 + 2)
                    diag = z[:].rearrange("p h (b k) -> p h b k", k=P)[:, :, 0:3:2, :]
                    dve.tensor_tensor(diag, diag, m.far_p[:].unsqueeze(1).unsqueeze(1).broadcast_to([P, 2, 2, P]), ALU.add).then_inc(masked, 1)
                    dve.wait_ge(logged, i + 1)
                    dve.wait_ge(masked, i + 1)
                    dve.scalar_tensor_tensor(out=sp_[:], in0=z[:], scalar=0.0, in1=e[:], op0=ALU.max, op1=ALU.add).then_inc(softp, 1)
                    dve.wait_ge(softp, OPEN + i + 1)
                    for h in range(2):
                        dve.tensor_tensor_scan(su[:, h, 0:P][:, ::-1], sp_[:, h, 0:P][:, ::-1], zero[:, 0:P], 0.0, ALU.add, ALU.add).then_inc(scanned, 1)
                        dve.tensor_tensor_scan(su[:, h, P:W][:, ::-1], sp_[:, h, P:W][:, ::-1], zero[:], 0.0, ALU.add, ALU.add).then_inc(scanned, 1)
                    for h in range(2):
                        dve.wait_ge(scanned, i * 4 + 2 * h + 2)
                        dve.tensor_tensor(z[:, h, :], z[:, h, :], su[:, h, :], ALU.subtract).then_inc(expo, 1)
                    ada.add(dve, i, 0)
                    dve.wait_ge(mixed, OPEN + i * 2 + 2)
                    for h in range(2):
                        r = slice(64 * h, 64 * h + 64)
                        dve.tensor_copy(yflat[r, ds(i * T + 2 * T, TP)], pso[r, h * TP:(h + 1) * TP]).then_inc(outs, 1)
                    ada.add(dve, i, 1)
                ada.scales(dve)


def stage_attend_sample(nc, m, a):
    R = HB * SQ
    pr = m.proj
    pos = pr[:].rearrange("p c t -> p (c t)")
    CH = D_B // P
    with Stage(nc, "atts") as s:
        pt_i = s.sb("pt_i", [P, NSEQ * PAGES], I32)
        pt_f = s.sb("pt_f", [P, NSEQ * PAGES])
        rows = s.sb("rows", [P, NSEQ * PAGES], U32)
        kcol = s.sb("kcol", [P, PAGES], U32)
        vcolx = s.sb("vcolx", [P, PAGES], U32)
        bias = s.sb("bias", [R, 1])
        kp = s.sb("kp", [P, PAGES, D_B])
        vp = s.sb("vp", [P, PAGES, D_B])
        kT = s.sb("kT", [P, CH, PAST])
        vnew = s.sb("vnew", [SQ, NSEQ, D_B])
        qb = s.sb("qb", [P, CH * 112])
        z = s.sb("z", [R, ZK])
        e = s.sb("e", [R, ZK])
        sp_ = s.sb("softplus", [R, ZK])
        su = s.sb("suffix", [R, ZK])
        zero = s.sb("zero", [R, ZK])
        wT = s.sb("wT", [P, PAGES * R])
        wTn = s.sb("wTn", [SQ, R])
        om = s.sb("om", [R, D_B])
        psk = [s.bank(f"psk{i}") for i in range(2)]
        psz = [s.bank(f"psz{i}") for i in range(2)]
        psm = s.bank("psm")
        psw = s.bank("psw")
        pso = [s.bank(f"pso{i}") for i in range(2)]
        loaded = s.sem("loaded")
        looked = Count(s.sem("rows_step"))
        kcoled = s.sem("kcol_ready")
        vcoled = s.sem("vcol_ready")
        kin = m.gathered[0:PAGES]
        vin = m.gathered[PAGES:2 * PAGES]
        g0 = m.gathered_by
        m.gathered_by += 16 * NSEQ
        kturn = s.sem("k_turned", opened=True)
        kkept = s.sem("k_kept_act", opened=True)
        kkept2 = s.sem("k_kept_dve", opened=True)
        qset = s.sem("q_set")
        cleared = s.sem("cleared")
        scored = s.sem("scored", opened=True)
        biased = s.sem("biased", opened=True)
        masked = s.sem("masked")
        actd = s.sem("act_step")
        logged = s.sem("logged")
        softp = s.sem("softplus_ready", opened=True)
        scanned = s.sem("scanned")
        expo = s.sem("exponent_ready")
        weighed = s.sem("weights_ready")
        wturn = s.sem("weights_turned", opened=True)
        wkept = s.sem("weights_kept", opened=True)
        mixed = s.sem("mixed", opened=True)
        kept = s.sem("outputs_masked", opened=True)
        folded = s.sem("outputs_turned", opened=True)
        done = s.sem("outputs_kept", opened=True)
        with nc.Block() as block:
            @block.sync
            def _(sp):
                sp.dma_start(pt_i[:], a["page_table"].rearrange("b g -> (b g)").unsqueeze(0).broadcast_to([P, NSEQ * PAGES])).then_inc(loaded, 16)
                sp.dma_start(bias[:], a["sb_bias"].rearrange("n (h o) -> (n h) o", o=1).unsqueeze(1).broadcast_to([HB, SQ, 1])).then_inc(loaded, 16)
                sp.dma_start(vnew[:], a["v_sample"].rearrange("n b t h d -> (n t) b (h d)")).then_inc(loaded, 16)

            @block.gpsimd
            def _(pool):
                kc_ = a["cache_sb_k"].rearrange("n g p h d -> (n g p) (h d)")
                vc_ = a["cache_sb_v"].rearrange("n g p h d -> (n g p) (h d)")
                link = chained(pool, looked)
                pool.wait_ge(loaded, 48)
                link(pool.tensor_copy(pt_f[:], pt_i[:]))
                link(pool.tensor_scalar(pt_f[:], pt_f[:], float(PAGE), m.rowid[:, 0:1], ALU.mult, ALU.add))
                link(pool.tensor_copy(rows[:], pt_f[:]))

                def fetch(b, col, coled, land, table, pages, used, per):
                    first = isinstance(b, int) and b == 0
                    if not first:
                        past = value_of(pool, (b - 1) * 16 + (g0 + 16))
                        apart(pool, loaded)
                        for j in range(PAGES):
                            pool.wait_ge(land[j], past)
                    pool.tensor_copy(col[:], rows[:, ds(b * PAGES, PAGES)]).then_inc(coled, 1)
                    after, past = value_of(pool, b + 1), value_of(pool, b * per + OPEN)
                    apart(pool, loaded)
                    pool.wait_ge(coled, after)
                    pool.wait_ge(used, past)
                    for j in range(PAGES):
                        pool.indirect_dma_start(pages[:, j, :], None, table, bass.IndirectOffsetOnAxis(ap=col[:, j:j + 1], axis=0)).then_inc(land[j], 16)

                def keys(b):
                    fetch(b, kcol, kcoled, kin, kc_, kp, kturn, 2 * PAGES)

                def values(b):
                    fetch(b, vcolx, vcoled, vin, vc_, vp, mixed, 2)

                keys(0)
                keys(1)
                values(0)
                with pool.Fori(2, NSEQ) as b:
                    keys(b)
                    values(b - 1)
                values(NSEQ - 1)

            def front(pe, b):
                for j in range(PAGES):
                    pe.wait_ge(kin[j], b * 16 + (g0 + 16))
                    pe.wait_ge(kkept, OPEN + b * PAGES + j)
                    for c in range(CH // 2):
                        ins = pe.transpose(psk[0][:, c * P:(c + 1) * P], kp[:, j, c * P:(c + 1) * P], m.ident[:])
                    ins.then_inc(kturn, 1)
                    pe.wait_ge(kkept2, OPEN + b * PAGES + j)
                    for c in range(CH // 2, CH):
                        ins = pe.transpose(psk[1][:, (c - CH // 2) * P:(c - CH // 2 + 1) * P], kp[:, j, c * P:(c + 1) * P], m.ident[:])
                    ins.then_inc(kturn, 1)
                pe.wait_ge(kkept, OPEN + b * PAGES + PAGES)
                pe.wait_ge(kkept2, OPEN + b * PAGES + PAGES)
                pe.wait_ge(qset, b * 2 + 2)
                pe.wait_ge(biased, OPEN + b * 3)
                for half in range(2):
                    for c in range(CH):
                        ins = pe.matmul(psz[half][0:R, :], qb[:, c * R:(c + 1) * R], kT[:, c, half * 512:(half + 1) * 512],
                                        start=(c == 0), stop=(c == CH - 1))
                    ins.then_inc(scored, 1)
                for c in range(CH):
                    ins = pe.matmul(psm[0:R, 0:SQ], qb[:, c * R:(c + 1) * R], pos[:, ds(b * SQ + ((8 + c) * T + TP), SQ)],
                                    start=(c == 0), stop=(c == CH - 1))
                ins.then_inc(scored, 1)

            def back(pe, b):
                pe.wait_ge(weighed, b + 1)
                for g in range(2):
                    pe.wait_ge(wkept, OPEN + b * 3 + (2 * g))
                    for j in range(4):
                        ins = pe.transpose(psw[:, j * R:(j + 1) * R], z[:, (4 * g + j) * P:(4 * g + j + 1) * P], m.ident[0:R, 0:R])
                    if g == 0:
                        ins = pe.transpose(psw[0:SQ, 4 * R:5 * R], z[:, PAST:ZK], m.ident[0:R, 0:R])
                    ins.then_inc(wturn, 1)
                pe.wait_ge(wkept, OPEN + b * 3 + 3)
                pe.wait_ge(done, OPEN + b)
                for half in range(2):
                    cols = slice(half * 384, half * 384 + 384)
                    for j in range(PAGES):
                        if half == 0:
                            pe.wait_ge(vin[j], b * 16 + (g0 + 16))
                        pe.matmul(pso[half][0:R, 0:384], wT[:, j * R:(j + 1) * R], vp[:, j, cols], start=(j == 0), stop=False)
                    pe.matmul(pso[half][0:R, 0:384], wTn[:], vnew[:].rearrange("p b d -> p (b d)")[:, ds(b * D_B + half * 384, 384)],
                              start=False, stop=True).then_inc(mixed, 1)
                pe.wait_ge(kept, OPEN + b * 2 + 2)
                for c in range(CH):
                    ins = pe.matmul(pso[1][:, 384 + c * SQ:384 + (c + 1) * SQ], om[:, c * P:(c + 1) * P], m.qsel[:], start=True, stop=True)
                ins.then_inc(folded, 1)

            @block.tensor
            def _(pe):
                pe.wait_ge(loaded, 48)
                front(pe, 0)
                with pe.Fori(1, NSEQ) as b:
                    front(pe, b)
                    back(pe, b - 1)
                back(pe, NSEQ - 1)

            @block.scalar
            def _(act):
                act.wait_ge(loaded, 48)

                def keys(b):
                    for j in range(PAGES):
                        act.wait_ge(kturn, OPEN + b * (2 * PAGES) + 2 * j + 1)
                        act.wait_ge(scored, OPEN + b * 3)
                        act.copy(kT[:, 0:CH // 2, j * P:(j + 1) * P], psk[0][:, 0:CH // 2 * P].rearrange("p (c k) -> p c k", k=P)).then_inc(kkept, 1)

                def logits(b):
                    act.wait_ge(wturn, OPEN + b * 2)
                    for half in range(2):
                        act.wait_ge(scored, OPEN + b * 3 + half + 1)
                        act.activation(z[:, half * 512:(half + 1) * 512], psz[half][0:R, :], ACT.Identity,
                                       bias=bias[:, 0:1], scale=HD ** -0.5).then_inc(biased, 1)
                    act.wait_ge(scored, OPEN + b * 3 + 3)
                    act.activation(z[:, PAST:ZK], psm[0:R, 0:SQ], ACT.Identity, bias=bias[:, 0:1], scale=HD ** -0.5).then_inc(biased, 1)
                    act.wait_ge(masked, b + 1)
                    act.wait_ge(softp, OPEN + b)
                    act.wait_ge(biased, OPEN + b * 3 + 3)
                    act.activation(e[:], z[:], ACT.Abs).then_inc(actd, 1)
                    act.wait_ge(actd, b * 2 + 1)
                    act.activation(e[:], e[:], ACT.Exp, scale=-1.0).then_inc(actd, 1)
                    act.wait_ge(actd, b * 2 + 2)
                    act.activation(e[:], e[:], ACT.Ln, bias=1.0).then_inc(logged, 1)

                def weights(b):
                    act.wait_ge(expo, b + 1)
                    act.activation(z[:], z[:], ACT.Exp).then_inc(weighed, 1)
                    act.wait_ge(mixed, OPEN + b * 2)
                    for g in range(2):
                        act.wait_ge(wturn, OPEN + b * 2 + 1 + g)
                        act.copy(wT[:, 4 * g * R:4 * (g + 1) * R], psw[:, 0:4 * R]).then_inc(wkept, 1)
                        if g == 0:
                            act.copy(wTn[:], psw[0:SQ, 4 * R:5 * R]).then_inc(wkept, 1)

                keys(0)
                with act.Fori(0, NSEQ - 1) as b:
                    logits(b)
                    keys(b + 1)
                    weights(b)
                logits(NSEQ - 1)
                weights(NSEQ - 1)

            @block.vector
            def _(dve):
                dve.memset(qb[:], 0.0).then_inc(cleared, 1)
                dve.memset(zero[:], 0.0).then_inc(cleared, 1)
                dve.wait_ge(cleared, 2)

                def keys(b):
                    dve.wait_ge(scored, OPEN + b * 3)
                    for h in range(2):
                        r = slice(64 * h, 64 * h + 64)
                        dve.tensor_copy(qb[r, :].rearrange("p (c x) -> p c x", x=112)[:, :, 8 * h:8 * h + 8],
                                        pos[r, :].rearrange("p (c t) -> p c t", t=T)[:, 2:8, ds(b * SQ + TP, SQ)]).then_inc(qset, 1)
                    for j in range(PAGES):
                        dve.wait_ge(kturn, OPEN + b * (2 * PAGES) + 2 * j + 2)
                        dve.tensor_copy(kT[:, CH // 2:CH, j * P:(j + 1) * P], psk[1][:, 0:CH // 2 * P].rearrange("p (c k) -> p c k", k=P)).then_inc(kkept2, 1)

                def mask(b):
                    dve.wait_ge(biased, OPEN + b * 3 + 3)
                    dve.tensor_tensor(z[:, PAST:ZK], z[:, PAST:ZK], m.far_s[:], ALU.add).then_inc(masked, 1)

                def weights(b):
                    dve.wait_ge(logged, b + 1)
                    dve.wait_ge(masked, b + 1)
                    dve.scalar_tensor_tensor(out=sp_[:], in0=z[:], scalar=0.0, in1=e[:], op0=ALU.max, op1=ALU.add).then_inc(softp, 1)
                    dve.wait_ge(softp, OPEN + b + 1)
                    dve.tensor_tensor_scan(su[:, ::-1], sp_[:, ::-1], zero[:], 0.0, ALU.add, ALU.add).then_inc(scanned, 1)
                    dve.wait_ge(scanned, b + 1)
                    dve.tensor_tensor(z[:], z[:], su[:], ALU.subtract).then_inc(expo, 1)

                def outputs(b):
                    for half in range(2):
                        dve.wait_ge(mixed, OPEN + b * 2 + half + 1)
                        dve.wait_ge(folded, OPEN + b)
                        cols = slice(half * 384, half * 384 + 384)
                        dve.tensor_tensor(om[:, cols], pso[half][0:R, 0:384], m.headmask[:, cols], ALU.mult).then_inc(kept, 1)
                    dve.wait_ge(folded, OPEN + b + 1)
                    dve.tensor_copy(m.yT[:, 2:8, ds(b * SQ + TP, SQ)],
                                    pso[1][:, 384:384 + CH * SQ].rearrange("p (c j) -> p c j", j=SQ)).then_inc(done, 1)

                keys(0)
                mask(0)
                weights(0)
                with dve.Fori(0, NSEQ - 1) as b:
                    keys(b + 1)
                    mask(b + 1)
                    weights(b + 1)
                    outputs(b)
                outputs(NSEQ - 1)


def stage_conv(nc, m, a):
    pr = m.proj
    NB3 = NSEQ * 3
    NS_ = 3 + NB3
    with Stage(nc, "conv") as s:
        buf = s.sb("buf", [NB3, CONV])
        bufT = s.sb("bufT", [P, CC, NB3])
        full = s.sb("full", [P, CC, NSEQ, 11])
        tmp = s.sb("tmp", [P, CC, NSEQ, SQ])
        last = s.sb("last", [P, CC, NS_])
        lrow = s.sb("lrow", [NS_, CONV])
        wdt = s.sb("wdt", [P, KC, SH])
        dtb = s.sb("dtb", [P, SH])
        alog = s.sb("alog", [P, SH])
        raw = s.sb("raw", [P, 3, SH])
        lg = s.sb("lg", [P, 3, SH])
        psb = [s.bank(f"psb{i}") for i in range(2)]
        psl = [s.bank(f"psl{i}") for i in range(2)]
        psd = s.bank("psd")
        loaded = s.sem("loaded")
        bturned = s.sem("buf_turned")
        bkept = s.sem("buf_kept")
        lasts = s.sem("last_ready")
        lturned = s.sem("last_turned")
        lkept = s.sem("last_kept")
        stored = s.sem("stored")
        dts = s.sem("dt_summed")
        pooled = Count(s.sem("pool_step"))
        vecd = Count(s.sem("dve_step"))
        actd = Count(s.sem("act_step"))
        conv_p = s.sem("conv_prompt_done")
        conv_s = s.sem("conv_sample_done")
        tapped = s.sem("tap_added")
        rawd = s.sem("dt_biased")
        dlog = s.sem("dt_logged")
        cv = m.xbc
        cvf = cv[:].rearrange("p c t -> p (c t)")
        prf = pr[:].rearrange("p c t -> p (c t)")
        with nc.Block() as block:
            @block.sync
            def _(sp):
                sp.dma_start(buf[:], a["state_conv"].rearrange("n b i d -> (n b i) d")).then_inc(loaded, 16)
                sp.dma_start(wdt[:], a["ssd_w_in"][0].rearrange("(c p) n -> p c n", p=P)[:, :, D_IN + CONV:D_IN + CONV + SH]).then_inc(loaded, 16)
                sp.dma_start(dtb[:], a["ssd_dt_bias"].broadcast_to([P, SH])).then_inc(loaded, 16)
                sp.dma_start(alog[:], a["ssd_a_log"].broadcast_to([P, SH])).then_inc(loaded, 16)
                sp.wait_ge(lkept, 6)
                sp.dma_start(a["conv_prompt"].rearrange("n b i d -> (n b i) d"), lrow[0:3, :]).then_inc(stored, 16)
                sp.dma_start(a["conv_sample"].rearrange("n b i d -> (n b i) d"), lrow[3:NS_, :]).then_inc(stored, 16)
                sp.wait_ge(stored, 32)

            @block.tensor
            def _(pe):
                pe.wait_ge(loaded, 64)
                for t, (t0, n) in enumerate(TILES):
                    for c in range(KC):
                        ins = pe.matmul(psd[0:n, t * SH:(t + 1) * SH], m.hT[:, c, t0:t0 + n], wdt[:, c, :], start=(c == 0), stop=(c == KC - 1))
                ins.then_inc(dts, 1)
                for g in range(2):
                    for q in range(12):
                        ins = pe.transpose(psb[g][:, q * NB3:(q + 1) * NB3], buf[:, (12 * g + q) * P:(12 * g + q + 1) * P], m.ident[0:NB3, 0:NB3])
                    ins.then_inc(bturned, 1)
                pe.wait_ge(lasts, 2)
                for g in range(6):
                    if g >= 2:
                        pe.wait_ge(lkept, g - 1)
                    for q in range(4):
                        ins = pe.transpose(psl[g % 2][0:NS_, q * P:(q + 1) * P], last[:, 4 * g + q, :], m.ident[:])
                    ins.then_inc(lturned, 1)

            @block.gpsimd
            def _(pool):
                link = chained(pool, pooled)
                link(pool.tensor_copy(full[:, :, :, 3:11], pr[:, XC:, TP:T].rearrange("p c (b j) -> p c b j", j=SQ)))
                pool.tensor_copy(last[:, :, 0:3], pr[:, XC:, TP - 3:TP]).then_inc(lasts, 1)
                pool.tensor_copy(last[:, :, 3:NS_].rearrange("p c (b i) -> p c b i", i=3),
                                 pr[:, XC:, TP:T].rearrange("p c (b j) -> p c b j", j=SQ)[:, :, :, 5:8]).then_inc(lasts, 1)
                pool.wait_ge(bkept, 2)
                link(pool.tensor_copy(full[:, :, :, 0:3], bufT[:].rearrange("p c (b i) -> p c b i", i=3)))
                out = cv[:, :, TP:T].rearrange("p c (b j) -> p c b j", j=SQ)

                def tap(i):
                    return m.cw[:, i, :].unsqueeze(2).unsqueeze(2).broadcast_to([P, CC, NSEQ, SQ])

                link(pool.tensor_tensor(out, full[:, :, :, 0:8], tap(0), ALU.mult))
                for i in range(1, 4):
                    link(pool.tensor_tensor(tmp[:], full[:, :, :, i:i + 8], tap(i), ALU.mult))
                    link(pool.tensor_tensor(out, out, tmp[:], ALU.add))
                pool.tensor_tensor(out, out, m.vcol[:, 138:162].unsqueeze(2).unsqueeze(2).broadcast_to([P, CC, NSEQ, SQ]),
                                   ALU.add).then_inc(conv_s, 1)

            @block.vector
            def _(dve):
                link = chained(dve, vecd)
                dve.wait_ge(dts, 1)
                dve.wait_ge(loaded, 64)
                for t, (t0, n) in enumerate(TILES):
                    ins = dve.tensor_tensor(raw[0:n, t, :], psd[0:n, t * SH:(t + 1) * SH], dtb[0:n, :], ALU.add)
                    ins.then_inc(rawd, 1)
                with dve.Fori(0, CC) as c:
                    dve.tensor_scalar(cvf[:, ds(c * T, TP)], prf[:, ds(c * T + XC * T, TP)],
                                      m.vcol[:, ds(c + 256 + 72, 1)], m.vcol[:, ds(c + 138, 1)], ALU.mult, ALU.add).then_inc(tapped, 1)
                    for i in range(1, 4):
                        dve.wait_ge(tapped, c * 3 + i)
                        dve.scalar_tensor_tensor(out=cvf[:, ds(c * T + i, TP - i)], in0=prf[:, ds(c * T + XC * T, TP - i)],
                                                 scalar=m.vcol[:, ds(c + 256 + 24 * (3 - i), 1)], in1=cvf[:, ds(c * T + i, TP - i)],
                                                 op0=ALU.mult, op1=ALU.add).then_inc(tapped if i < 3 else conv_p, 1)
                dve.wait_ge(dlog, 1)
                for t, (t0, n) in enumerate(TILES):
                    ins = dve.scalar_tensor_tensor(out=m.dt[0:n, t, :], in0=raw[0:n, t, :], scalar=0.0, in1=lg[0:n, t, :], op0=ALU.max, op1=ALU.add)
                    vecd.by(ins)
                dve.wait_ge(vecd.sem, vecd.n)
                for t, (t0, n) in enumerate(TILES):
                    dve.scalar_tensor_tensor(out=m.dta[0:n, t, :], in0=m.dt[0:n, t, :], scalar=-1.0, in1=alog[0:n, :], op0=ALU.mult, op1=ALU.mult)

            @block.scalar
            def _(act):
                link = chained(act, actd)
                for g in range(2):
                    act.wait_ge(bturned, g + 1)
                    act.copy(bufT[:, 12 * g:12 * (g + 1), :].rearrange("p c n -> p (c n)"), psb[g][:, 0:12 * NB3]).then_inc(bkept, 1)
                act.wait_ge(rawd, 3)
                for t, (t0, n) in enumerate(TILES):
                    actd.by(act.activation(lg[0:n, t, :], raw[0:n, t, :], ACT.Abs))
                act.wait_ge(actd.sem, actd.n)
                for t, (t0, n) in enumerate(TILES):
                    actd.by(act.activation(lg[0:n, t, :], lg[0:n, t, :], ACT.Exp, scale=-1.0))
                actd.by(act.activation(alog[:], alog[:], ACT.Exp))
                act.wait_ge(actd.sem, actd.n)
                for t, (t0, n) in enumerate(TILES):
                    actd.by(act.activation(lg[0:n, t, :], lg[0:n, t, :], ACT.Ln, bias=1.0))
                act.wait_ge(actd.sem, actd.n)
                act.nop().then_inc(dlog, 1)
                for g in range(6):
                    act.wait_ge(lturned, g + 1)
                    act.copy(lrow[:, g * 512:(g + 1) * 512], psl[g % 2][0:NS_, :]).then_inc(lkept, 1)
                act.wait_ge(conv_s, 1)
                act.wait_ge(conv_p, CC)
                act.activation(cv[:], cv[:], ACT.Silu)


def stage_scan(nc, m, a):
    cv = m.xbc
    BC, CCH = XC, XC + SG
    with Stage(nc, "scan") as s:
        bt = m.btok
        eacs = s.sb("eacs", [P, SH])
        toend = s.sb("toend", [P, 4, SH])
        xe = s.sb("xe", [P, 3, D_IN])
        st0 = s.sb("st0", [NST, D_IN])
        stout = s.sb("stout", [P, XC, NST])
        lm = [s.sb(f"lm{i}", [P, 4, P]) for i in range(2)]
        dec = [s.sb(f"dec{i}", [P, 4, P]) for i in range(2)]
        cbm = [s.sb(f"cbm{i}", [P, P]) for i in range(2)]
        psA = [s.bank(f"psA{i}") for i in range(2)]
        psC = s.bank("psC")
        psY = [s.bank(f"psY{i}") for i in range(2)]
        psO = s.bank("psO")
        psE = s.bank("psE")
        psS = s.bank("psS")
        turned = s.sem("turned")
        kept = s.sem("kept")
        csum = s.sem("decays_summed")
        cexp = s.sem("decays_ready")
        xed = s.sem("xe_ready")
        stsum = s.sem("state0_summed")
        stkept = s.sem("state0_kept")
        cbs = s.sem("cb_made")
        cbk = s.sem("cb_kept")
        lmd = s.sem("lm_ready")
        segd = s.sem("segments_summed")
        decd = s.sem("segments_exp")
        mtd = s.sem("mt_ready")
        yd = s.sem("y_made")
        yod = s.sem("yoff_made")
        yk = s.sem("y_kept")
        ytmp = s.sem("y_tmp")
        fin = s.sem("state_made")
        fink = s.sem("state_kept")
        fins = s.sem("state_stored")
        groups = [(t, g) for t in range(3) for g in range(5)]
        steps = [(t, g, q) for t in range(3) for g in range(SG) for q in range(2)]

        def up(t):
            return (m.upto_s, m.after_s)[0:2] if t == 2 else (m.upto, m.after)

        with nc.Block() as block:
            @block.tensor
            def _(pe):
                pe.matmul(psE[:, 0:SH], m.upto[:], m.dta[:, 1, :], start=True, stop=True)
                pe.matmul(psE[:, SH:2 * SH], m.after[:], m.dta[:, 0, :], start=True, stop=True)
                pe.matmul(psE[:, 2 * SH:3 * SH], m.after[:], m.dta[:, 1, :], start=True, stop=True)
                pe.matmul(psE[0:TS, 3 * SH:4 * SH], m.after_s[:], m.dta[0:TS, 2, :], start=True, stop=True)
                pe.matmul(psE[:, 4 * SH:5 * SH], m.after[:], m.dta[:, 0, :], start=True, stop=False)
                pe.matmul(psE[:, 4 * SH:5 * SH], m.ones[:], m.dta[:, 1, :], start=False, stop=True).then_inc(csum, 1)
                for k, (t, g) in enumerate(groups):
                    t0, n = TILES[t]
                    if k >= 2:
                        pe.wait_ge(kept, k - 1)
                    for q in range(4):
                        ins = pe.transpose(psA[k % 2][0:n, q * P:(q + 1) * P], cv[:, 4 * g + q, t0:t0 + n], m.ident[:])
                    ins.then_inc(turned, 1)
                for g in range(SG):
                    pe.wait_ge(xed, g + 1)
                    pe.wait_ge(stkept, g)
                    pe.matmul(psS[:], bt[:, 0, g * NST:(g + 1) * NST], xe[:, 0, g * 512:(g + 1) * 512], start=True, stop=True).then_inc(stsum, 1)
                pe.wait_ge(kept, len(groups))

                def opening(k):
                    t, g, q = steps[k]
                    t0, n = TILES[t]
                    if q == 0:
                        if t or g:
                            pe.wait_ge(cbk, t * SG + g)
                        pe.matmul(psC[0:n, 0:n], cv[:, BC + g, t0:t0 + n], cv[:, CCH + g, t0:t0 + n], start=True, stop=True).then_inc(cbs, 1)
                        if t == 1:
                            if g:
                                pe.wait_ge(ytmp, g)
                            pe.wait_ge(stkept, g + 1)
                            pe.matmul(psO[:], cv[:, CCH + g, t0:t0 + n], st0[:, g * 512:(g + 1) * 512], start=True, stop=True).then_inc(yod, 1)
                    pe.wait_ge(lmd, k + 1)
                    if k >= 2:
                        pe.wait_ge(decd, k - 1)
                    for r in range(4):
                        ins = pe.matmul(psA[k % 2][0:n, r * P:r * P + n], lm[k % 2][0:n, r, 0:n], up(t)[0][0:n, 0:n], start=True, stop=True)
                    ins.then_inc(segd, 1)

                opening(0)
                for k, (t, g, q) in enumerate(steps):
                    if k + 1 < len(steps):
                        opening(k + 1)
                    n, tg = TILES[t][1], t * SG + g
                    if q == 0 and tg >= 2:
                        pe.wait_ge(yk, tg - 1)
                    pe.wait_ge(mtd, k + 1)
                    for r in range(4):
                        h = g * SR + 4 * q + r
                        ins = pe.matmul(psY[tg % 2][0:n, (4 * q + r) * HD:(4 * q + r + 1) * HD], dec[k % 2][0:n, r, 0:n],
                                        m.xdt[0:n, t, h * HD:(h + 1) * HD], start=True, stop=True)
                    ins.then_inc(yd, 1)
                pe.wait_ge(xed, 3 * SG)
                for c in range(XC):
                    if c >= 2:
                        pe.wait_ge(fink, c - 1)
                    o = 256 * (c % 2)
                    bank = psS if c % 2 else psC
                    pe.wait_ge(cbk, 3 * SG)
                    pe.matmul(bank[:, 0:NST], xe[:, 2, c * P:(c + 1) * P], bt[:, 0, (c // 4) * NST:(c // 4 + 1) * NST], start=True, stop=False)
                    pe.matmul(bank[:, 0:NST], xe[:, 1, c * P:(c + 1) * P], bt[:, 1, (c // 4) * NST:(c // 4 + 1) * NST], start=False, stop=True).then_inc(fin, 1)

            @block.scalar
            def _(act):
                act.wait_ge(csum, 1)
                act.activation(eacs[:], psE[:, 0:SH], ACT.Exp).then_inc(cexp, 1)
                act.activation(toend[:, 0:2, :].rearrange("p t h -> p (t h)"), psE[:, SH:3 * SH], ACT.Exp).then_inc(cexp, 1)
                act.activation(toend[0:TS, 2, :], psE[0:TS, 3 * SH:4 * SH], ACT.Exp).then_inc(cexp, 1)
                act.activation(toend[:, 3, :], psE[:, 4 * SH:5 * SH], ACT.Exp).then_inc(cexp, 1)
                for g in range(SG):
                    act.wait_ge(stsum, g + 1)
                    act.copy(st0[:, g * 512:(g + 1) * 512], psS[:]).then_inc(stkept, 1)
                for k, (t, g, q) in enumerate(steps):
                    n = TILES[t][1]
                    act.wait_ge(segd, k + 1)
                    if k >= 2:
                        act.wait_ge(yd, k - 1)
                    act.activation(dec[k % 2][0:n, :, 0:n], psA[k % 2][0:n, :].rearrange("p (r l) -> p r l", l=P)[:, :, 0:n], ACT.Exp).then_inc(decd, 1)
                for c in range(XC):
                    act.wait_ge(fin, c + 1)
                    act.copy(stout[:, c, :], (psS if c % 2 else psC)[:, 0:NST]).then_inc(fink, 1)

            @block.gpsimd
            def _(pool):
                for k, (t, g, q) in enumerate(steps):
                    n = TILES[t][1]
                    h = g * SR + 4 * q
                    if k >= 2:
                        pool.wait_ge(segd, k - 1)
                    pool.tensor_tensor(lm[k % 2][0:n, :, 0:n], up(t)[1][0:n, 0:n].unsqueeze(1).broadcast_to([n, 4, n]),
                                       m.dta[0:n, t, h:h + 4].unsqueeze(2).broadcast_to([n, 4, n]), ALU.mult).then_inc(lmd, 1)

            @block.vector
            def _(dve):
                for k, (t, g) in enumerate(groups):
                    t0, n = TILES[t]
                    dve.wait_ge(turned, k + 1)
                    if g < 4:
                        dve.tensor_tensor(m.xdt[0:n, t, g * 512:(g + 1) * 512].rearrange("p (h d) -> p h d", d=HD),
                                          psA[k % 2][0:n, :].rearrange("p (h d) -> p h d", d=HD),
                                          m.dt[0:n, t, g * SR:(g + 1) * SR].unsqueeze(2).broadcast_to([n, SR, HD]), ALU.mult).then_inc(kept, 1)
                    else:
                        dve.tensor_copy(bt[0:n, t, :], psA[k % 2][0:n, :]).then_inc(kept, 1)
                dve.wait_ge(kept, len(groups))
                dve.wait_ge(cexp, 4)

                def scaled(dst, t, e, g, n=P):
                    return dve.tensor_tensor(dst.rearrange("p (h d) -> p h d", d=HD),
                                             m.xdt[0:n, t, g * 512:(g + 1) * 512].rearrange("p (h d) -> p h d", d=HD),
                                             toend[0:n, e, g * SR:(g + 1) * SR].unsqueeze(2).broadcast_to([n, SR, HD]), ALU.mult)

                for g in range(SG):
                    scaled(xe[:, 0, g * 512:(g + 1) * 512], 0, 0, g).then_inc(xed, 1)

                def keep(t, g):
                    n, tg = TILES[t][1], t * SG + g
                    dve.wait_ge(yd, 2 * tg + 2)
                    dst = m.ytok[0:n, t, g * 512:(g + 1) * 512]
                    if t == 1:
                        dve.wait_ge(ytmp, g + 1)
                        dve.tensor_tensor(dst, psY[tg % 2][0:n, :], dst, ALU.add).then_inc(yk, 1)
                    else:
                        dve.tensor_copy(dst, psY[tg % 2][0:n, :]).then_inc(yk, 1)

                for t in range(3):
                    n = TILES[t][1]
                    for g in range(SG):
                        tg = t * SG + g
                        dve.wait_ge(cbs, tg + 1)
                        if tg >= 2:
                            dve.wait_ge(mtd, 2 * tg - 2)
                        dve.tensor_tensor(cbm[tg % 2][0:n, 0:n], psC[0:n, 0:n], up(t)[0][0:n, 0:n], ALU.mult).then_inc(cbk, 1)
                        if t == 1:
                            dve.wait_ge(yod, g + 1)
                            dve.tensor_tensor(m.ytok[:, t, g * 512:(g + 1) * 512].rearrange("p (h d) -> p h d", d=HD), psO[:].rearrange("p (h d) -> p h d", d=HD),
                                              eacs[:, g * SR:(g + 1) * SR].unsqueeze(2).broadcast_to([P, SR, HD]), ALU.mult).then_inc(ytmp, 1)
                        dve.wait_ge(cbk, tg + 1)
                        for q in range(2):
                            k = 2 * tg + q
                            dve.wait_ge(decd, k + 1)
                            v = dec[k % 2][0:n, :, 0:n]
                            dve.tensor_tensor(v, v, cbm[tg % 2][0:n, 0:n].unsqueeze(1).broadcast_to([n, 4, n]), ALU.mult).then_inc(mtd, 1)
                            if q == 0 and tg:
                                keep((tg - 1) // SG, (tg - 1) % SG)
                keep(2, SG - 1)
                for g in range(SG):
                    scaled(xe[:, 1, g * 512:(g + 1) * 512], 1, 1, g).then_inc(xed, 1)
                for g in range(SG):
                    scaled(xe[:, 2, g * 512:(g + 1) * 512], 0, 3, g).then_inc(xed, 1)
                for g in range(SG):
                    scaled(m.xes[:, g * 512:(g + 1) * 512], 2, 2, g, TS)

            @block.sync
            def _(sp):
                sp.wait_ge(fink, XC)
                sp.dma_start(a["ssm_prompt"].rearrange("n b (c h) p s -> (h p) (n b c) s", h=2), stout[:]).then_inc(fins, 16)
                sp.wait_ge(fins, 16)


def stage_state(nc, m, a):
    CCH = XC + SG
    with Stage(nc, "state") as s:
        dx = s.sb("dx", [TS, D_IN])
        ea = s.sb("ea", [P, XC, TS])
        bm = s.sb("bm", [TS, NSEQ, SG * NST])
        h0 = [s.sb(f"h0{i}", [P, XC, NST]) for i in range(2)]
        hT = s.sb("hT", [P, XC * P])
        hd = [s.sb(f"hd{i}", [P, XC, NST]) for i in range(2)]
        psE = [s.bank(f"psE{i}") for i in range(2)]
        psT = [s.bank(f"psT{i}") for i in range(2)]
        psO = s.bank("psO")
        psN = [s.bank(f"psN{i}") for i in range(2)]
        loaded = [s.sem(f"loaded{i}") for i in range(2)]
        spread = s.sem("dx_ready")
        esum = s.sem("ea_summed")
        eexp = s.sem("ea_ready")
        bms = s.sem("bm_ready")
        turned = s.sem("turned")
        kept = s.sem("kept", opened=True)
        yod = s.sem("yoff_made", opened=True)
        yk = s.sem("yoff_kept", opened=True)
        hds = s.sem("decayed", opened=True)
        newd = s.sem("update_made")
        newk = s.sem("state_ready", opened=True)
        stored = [s.sem(f"stored{i}", opened=True) for i in range(2)]
        cvf = m.xbc[:].rearrange("p c t -> p (c t)")
        bmf = bm[:].rearrange("p b n -> p (b n)")
        eaf = ea[:].rearrange("p c t -> p (c t)")
        src = a["state_ssm"].rearrange("n b (c h) p s -> (h p) (n b c) s", h=2)
        dst = a["ssm_sample"].rearrange("n b (c h) p s -> (h p) (n b c) s", h=2)
        with nc.Block() as block:
            @block.sync
            def _(sp):
                for i in range(NSEQ // 2):
                    for k in range(2):
                        if i:
                            sp.wait_ge(hds, OPEN + 2 * i + k - 1)
                            sp.wait_ge(turned, 8 * i + 4 * k - 4)
                        sp.dma_start(h0[k][:], src[:, (2 * i + k) * XC:(2 * i + k + 1) * XC, :]).then_inc(loaded[k], 16)
                    for k in range(2):
                        sp.wait_ge(newk, OPEN + 8 * i + 4 * k + 4)
                        sp.dma_start(dst[:, (2 * i + k) * XC:(2 * i + k + 1) * XC, :], hd[k][:]).then_inc(stored[k], 16)
                for k in range(2):
                    sp.wait_ge(stored[k], OPEN + 16 * (NSEQ // 2))

            @block.gpsimd
            def _(pool):
                pool.tensor_copy(dx[:].rearrange("p (h d) -> p h d", d=HD), m.dta[0:TS, 2, :].unsqueeze(2).broadcast_to([TS, SH, HD])).then_inc(spread, 1)
                pool.tensor_tensor(bm[:], m.btok[0:TS, 2, :].unsqueeze(1).broadcast_to([TS, NSEQ, SG * NST]),
                                   m.seq_s[:, 0:TS:SQ].unsqueeze(2).broadcast_to([TS, NSEQ, SG * NST]), ALU.mult).then_inc(bms, 1)
                pool.wait_ge(eexp, 4)
                with pool.Fori(0, NSEQ // 2) as i:
                    for k in range(2):
                        pool.wait_ge(loaded[k], i * 16 + 16)
                        pool.wait_ge(stored[k], OPEN + i * 16)
                        pool.tensor_tensor(hd[k][:], h0[k][:],
                                           ea[:, :, ds(i * 2 * SQ + (k * SQ + SQ - 1), 1)].broadcast_to([P, XC, NST]), ALU.mult).then_inc(hds, 1)

            @block.tensor
            def _(pe):
                pe.wait_ge(spread, 1)
                for c in range(XC):
                    if c % 4 == 0 and c >= 8:
                        pe.wait_ge(eexp, c // 4 - 1)
                    ins = pe.matmul(psE[(c // 4) % 2][:, (c % 4) * TS:(c % 4 + 1) * TS], dx[:, c * P:(c + 1) * P], m.upto_s[:], start=True, stop=True)
                    if c % 4 == 3:
                        ins.then_inc(esum, 1)
                pe.wait_ge(bms, 1)
                with pe.Fori(0, NSEQ // 2) as i:
                    for k in range(2):
                        pe.wait_ge(loaded[k], i * 16 + 16)
                        for g in range(4):
                            pe.wait_ge(kept, OPEN + i * 8 + max(4 * k + g - 1, 0)) if (k or g) else pe.wait_ge(kept, OPEN + i * 8)
                            for q in range(4):
                                ins = pe.transpose(psT[g % 2][:, q * P:(q + 1) * P], h0[k][:, 4 * g + q, :], m.ident[:])
                            ins.then_inc(turned, 1)
                        pe.wait_ge(kept, OPEN + i * 8 + 4 * k + 4)
                        pe.wait_ge(yk, OPEN + i * 2 + k)
                        for c in range(XC):
                            ins = pe.matmul(psO[:, c * SQ:(c + 1) * SQ], hT[:, c * P:(c + 1) * P],
                                            cvf[:, ds(i * 2 * SQ + ((CCH + c // 4) * T + TP + k * SQ), SQ)], start=True, stop=True)
                        ins.then_inc(yod, 1)
                        for g in range(4):
                            if g >= 2 or k:
                                pe.wait_ge(newk, OPEN + i * 8 + 4 * k + g - 1)
                            else:
                                pe.wait_ge(newk, OPEN + i * 8)
                            for q in range(4):
                                ins = pe.matmul(psN[g % 2][:, q * NST:(q + 1) * NST], m.xes[:, (4 * g + q) * P:(4 * g + q + 1) * P],
                                                bmf[:, ds(i * 2 * SG * NST + (k * SG * NST + g * NST), NST)], start=True, stop=True)
                            ins.then_inc(newd, 1)

            @block.scalar
            def _(act):
                for c in range(4):
                    act.wait_ge(esum, c + 1)
                    act.activation(ea[:, 4 * c:4 * c + 4, :].rearrange("p c t -> p (c t)"), psE[c % 2][:, 0:4 * TS], ACT.Exp).then_inc(eexp, 1)
                with act.Fori(0, NSEQ // 2) as i:
                    for k in range(2):
                        act.wait_ge(yod, OPEN + i * 2 + k)
                        for g in range(4):
                            act.wait_ge(turned, i * 8 + 4 * k + g + 1)
                            act.copy(hT[:, g * 512:(g + 1) * 512], psT[g % 2][:]).then_inc(kept, 1)

            @block.vector
            def _(dve):
                dve.wait_ge(eexp, 4)
                with dve.Fori(0, NSEQ // 2) as i:
                    for k in range(2):
                        dve.wait_ge(yod, OPEN + i * 2 + k + 1)
                        dve.tensor_tensor(m.yoff[:, :, ds(i * 2 * SQ + k * SQ, SQ)], psO[:, 0:XC * SQ].rearrange("p (c j) -> p c j", j=SQ),
                                          ea[:, :, ds(i * 2 * SQ + k * SQ, SQ)], ALU.mult).then_inc(yk, 1)
                        dve.wait_ge(hds, OPEN + i * 2 + k + 1)
                        for g in range(4):
                            dve.wait_ge(newd, i * 8 + 4 * k + g + 1)
                            v = hd[k][:, 4 * g:4 * g + 4, :]
                            dve.tensor_tensor(v, v, psN[g % 2][:].rearrange("p (c n) -> p c n", n=NST), ALU.add).then_inc(newk, 1)


def stage_gate(nc, m, a):
    y, z = m.yT2, m.proj
    with Stage(nc, "gate") as s:
        drow = s.sb("drow", [P, SH])
        dcol = s.sb("dcol", [P, XC])
        sq = s.sb("sq", [P, 4, T])
        var = s.sb("var", [P, SG, T])
        root = s.sb("root", [P, SG, T])
        inv = s.sb("inv", [P, SG, T])
        tmp = s.sb("tmp", [P, SG, T])
        psT = [s.bank(f"psT{i}") for i in range(2)]
        psS = [s.bank(f"psS{i}") for i in range(SG)]
        loaded = s.sem("loaded")
        turned = s.sem("turned")
        kept = s.sem("kept")
        zs = s.sem("z_gated")
        ysd = s.sem("y_ready")
        squared = s.sem("squared")
        summed = s.sem("summed")
        vard = s.sem("var_ready")
        rooted = s.sem("root_ready")
        vecd = Count(s.sem("dve_step"))
        with nc.Block() as block:
            @block.sync
            def _(sp):
                sp.dma_start(drow[:], a["ssd_d"].broadcast_to([P, SH])).then_inc(loaded, 16)

            @block.tensor
            def _(pe):
                for c in range(XC):
                    if c >= 2:
                        pe.wait_ge(kept, c - 1)
                    for t, (t0, n) in enumerate(TILES):
                        ins = pe.transpose(psT[c % 2][:, t0:t0 + n], m.ytok[0:n, t, c * P:(c + 1) * P], m.ident[0:n, 0:n])
                    ins.then_inc(turned, 1)
                for c in range(XC):
                    pe.wait_ge(squared, c + 1)
                    pe.matmul(psS[c // 4][:, 0:T], m.ones[:], sq[:, c % 4, :], start=(c % 4 == 0), stop=(c % 4 == 3)).then_inc(summed, 1)

            @block.scalar
            def _(act):
                act.activation(z[:, 0:XC, :], z[:, 0:XC, :], ACT.Silu).then_inc(zs, 1)
                for c in range(XC):
                    act.wait_ge(ysd, c + 1)
                    if c >= 4:
                        act.wait_ge(summed, c - 3)
                    act.activation(sq[:, c % 4, :], y[:, c, :], ACT.Square).then_inc(squared, 1)
                act.wait_ge(vard, SG)
                act.activation(root[:], var[:], ACT.Sqrt).then_inc(rooted, 1)

            @block.vector
            def _(dve):
                link = chained(dve, vecd)
                dve.wait_ge(loaded, 16)
                for h in range(2):
                    r = slice(64 * h, 64 * h + 64)
                    link(dve.tensor_copy(dcol[r, :], drow[r, h::2]))
                for c in range(XC):
                    dve.wait_ge(turned, c + 1)
                    ins = dve.scalar_tensor_tensor(out=y[:, c, :], in0=m.xbc[:, c, :], scalar=dcol[:, c:c + 1], in1=psT[c % 2][:, 0:T],
                                                   op0=ALU.mult, op1=ALU.add)
                    ins.then_inc(kept, 1)
                dve.wait_ge(kept, XC)
                link(dve.tensor_tensor(y[:, :, TP:T], y[:, :, TP:T], m.yoff[:], ALU.add))
                dve.wait_ge(zs, 1)
                for c in range(XC):
                    dve.tensor_tensor(y[:, c, :], y[:, c, :], z[:, c, :], ALU.mult).then_inc(ysd, 1)
                for g in range(SG):
                    dve.wait_ge(summed, 4 * g + 4)
                    dve.tensor_scalar(var[:, g, :], psS[g][:, 0:T], 1.0 / (D_IN // SG), EPS, ALU.mult, ALU.add).then_inc(vard, 1)
                dve.wait_ge(vard, SG)
                dve.wait_ge(rooted, 1)
                link(dve.reciprocal(inv[:], root[:]))
                link(dve.tensor_tensor(tmp[:], inv[:], inv[:], ALU.mult))
                link(dve.tensor_tensor(tmp[:], tmp[:], var[:], ALU.mult))
                link(dve.tensor_scalar(tmp[:], tmp[:], -0.5, 1.5, ALU.mult, ALU.add))
                link(dve.tensor_tensor(inv[:], inv[:], tmp[:], ALU.mult))
                dve.wait_ge(ysd, XC)
                dve.wait_ge(squared, XC)
                for c in range(XC):
                    dve.scalar_tensor_tensor(out=y[:, c, :], in0=y[:, c, :], scalar=m.vcol[:, 162 + c:163 + c], in1=inv[:, c // 4, :],
                                             op0=ALU.mult, op1=ALU.mult)


def stage_scores(nc, m, a, layer):
    q = m.proj
    with Stage(nc, f"scores{layer}") as s:
        krow = s.sb("krow", [P, 2, EH, P])
        kT = s.sb("kT", [P, 2 * EH, P])
        hdup = s.sb("hdup", [P, KC, P])
        qz = s.sb("qz", [P, 2 * EH, P])
        ps = [s.bank(f"ps{i}") for i in range(4)]
        loaded = s.sem("loaded")
        dup = s.sem("dup_ready")
        kturn = s.sem("k_turned")
        kkept = s.sem("k_kept")
        scored = s.sem("scored")
        skept = s.sem("scores_kept")
        cleared = s.sem("qz_cleared")
        with nc.Block() as block:
            @block.sync
            def _(sp):
                for j, k in enumerate(("peer_k1", "peer_k2")):
                    sp.dma_start(krow[:, j, :, :], a[k][layer].rearrange("h k d -> k h d")).then_inc(loaded, 16)

            @block.tensor
            def _(pe):
                u = 0
                pe.wait_ge(loaded, 32)
                for g in range(4):
                    for i in range(4):
                        hs = 4 * g + i
                        ins = pe.transpose(ps[g][:, i * P:(i + 1) * P], krow[:, hs % 2, hs // 2, :], m.ident[:])
                    ins.then_inc(kturn, 1)
                pe.wait_ge(dup, 3)
                for t in range(3):
                    for g in range(2):
                        pe.wait_ge(kkept, 2 * t + g + 1)
                        for i in range(4):
                            c = 4 * g + i
                            src = hdup[:, c, :] if t == 2 else m.hT[:, c, t * P:(t + 1) * P]
                            ins = pe.transpose(ps[(2 * t + g) % 4][:, i * P:(i + 1) * P], src, m.ident[:])
                        ins.then_inc(kturn, 1)
                pe.wait_ge(kkept, 10)
                n = 0
                for t in range(3):
                    for g in range(4 if t < 2 else 2):
                        if n >= 4:
                            pe.wait_ge(skept, n - 3)
                        for i in range(4):
                            hs = 4 * g + i
                            o = ps[n % 4][:, i * P:(i + 1) * P]
                            if t < 2:
                                ins = pe.matmul(o, q[:, hs, t * P:(t + 1) * P], kT[:, hs, :], start=True, stop=True)
                            else:
                                pe.matmul(o, qz[:, hs, :], kT[:, hs, :], start=True, stop=False)
                                ins = pe.matmul(o, qz[:, hs + EH, :], kT[:, hs + EH, :], start=False, stop=True)
                        ins.then_inc(scored, 1)
                        n += 1

            @block.scalar
            def _(act):
                for g in range(4):
                    act.wait_ge(kturn, g + 1)
                    act.copy(kT[:, 4 * g:4 * g + 4, :].rearrange("p c k -> p (c k)"), ps[g][:]).then_inc(kkept, 1)
                for t in range(3):
                    for g in range(2):
                        act.wait_ge(kturn, 5 + 2 * t + g)
                        act.copy(m.htok[:, t, g * 512:(g + 1) * 512], ps[(2 * t + g) % 4][:]).then_inc(kkept, 1)
                for n in range(10):
                    act.wait_ge(scored, n + 1)
                    act.copy(m.sc[:, n * 4 * NK:(n + 1) * 4 * NK], ps[n % 4][:]).then_inc(skept, 1)

            @block.vector
            def _(dve):
                dve.memset(qz[:], 0.0).then_inc(cleared, 1)
                dve.tensor_copy(hdup[:].rearrange("p c (r t) -> p c r t", r=2),
                                m.hT[:, :, TP:T].unsqueeze(2).broadcast_to([P, KC, 2, TS])).then_inc(dup, 1)
                dve.wait_ge(cleared, 1)
                dve.tensor_copy(qz[:, 0:EH, 0:TS], q[:, 0:EH, TP:T]).then_inc(dup, 1)
                dve.tensor_copy(qz[:, EH:2 * EH, TS:P], q[:, EH:2 * EH, TP:T]).then_inc(dup, 1)


class Choice:
    STEPS = 30

    def __init__(self, s, m, layer, passed):
        self.m, self.layer, self.passed = m, layer, passed
        self.sc = s.sb("sc", [P, 2, NK])
        self.sc2 = s.sb("sc2", [P, 2, NK])
        self.top = s.sb("top", [P, 2, TOPK])
        self.topi = s.sb("topi", [P, 2, TOPK], U32)
        self.topf = s.sb("topf", [P, 2, TOPK])
        self.cand = s.sb("cand", [P, TOPK * TOPK])
        self.cand2 = s.sb("cand2", [P, TOPK * TOPK])
        self.best = s.sb("best", [P, TOPK])
        self.gap = s.sb("gap", [P, TOPK])
        self.ex = s.sb("ex", [P, TOPK])
        self.pick = s.sb("pick", [P, TOPK], U32)
        self.part = s.sb("part", [P, 2, TOPK], U32)
        self.partf = s.sb("partf", [P, 2, TOPK])
        self.hot = s.sb("hot", [P, 2, TOPK * TOPK])
        self.found = s.sb("found", [P, 2, TOPK])
        self.num = s.sb("num", [P, TOPK])
        self.tot = s.sb("tot", [P, 1])
        self.taken = s.sem("scores_taken")
        self.step = s.sem("choice_step")
        self.less = s.sem("best_shifted")
        self.expd = s.sem("best_exp")
        self.chosen = s.sem("experts_chosen", opened=True)

    def take(self, act, j):
        act.wait_ge(self.chosen, OPEN + j)
        act.copy(self.sc[:].rearrange("p s k -> p (s k)"), self.m.sc[:, ds(j * 2 * NK, 2 * NK)]).then_inc(self.taken, 1)

    def exp(self, act, j):
        act.wait_ge(self.less, j + 1)
        act.activation(self.ex[:], self.gap[:], ACT.Exp).then_inc(self.expd, 1)

    def choose(self, dve, j):
        taken = value_of(dve, j + 1)
        apart(dve, self.passed)
        dve.wait_ge(self.taken, taken)
        steps = Steps(dve, self.step, j * self.STEPS, self.passed)
        sc, sc2, top, topi, cand, cand2, best, pick = self.sc, self.sc2, self.top, self.topi, self.cand, self.cand2, self.best, self.pick
        lo, hi = slice(0, 8), slice(8, 16)
        sides = range(2)
        steps.then(*[dve.max(top[:, g, lo], sc[:, g, :]) for g in sides])
        steps.then(*[dve.match_replace(sc2[:, g, :], top[:, g, lo], sc[:, g, :], LOWEST) for g in sides],
                   *[dve.max_index(topi[:, g, lo], top[:, g, lo], sc[:, g, :]) for g in sides])
        steps.then(*[dve.max(top[:, g, hi], sc2[:, g, :]) for g in sides])
        steps.then(*[dve.max_index(topi[:, g, hi], top[:, g, hi], sc2[:, g, :]) for g in sides],
                   dve.tensor_tensor(cand[:].rearrange("p (x y) -> p x y", y=TOPK),
                                     top[:, 0, :].unsqueeze(2).broadcast_to([P, TOPK, TOPK]),
                                     top[:, 1, :].unsqueeze(1).broadcast_to([P, TOPK, TOPK]), ALU.add))
        steps.then(dve.max(best[:, lo], cand[:]), dve.tensor_copy(self.topf[:], topi[:]))
        steps.then(dve.match_replace(cand2[:], best[:, lo], cand[:], LOWEST), dve.max_index(pick[:, lo], best[:, lo], cand[:]))
        steps.then(dve.max(best[:, hi], cand2[:]))
        steps.then(dve.max_index(pick[:, hi], best[:, hi], cand2[:]),
                   dve.tensor_scalar(self.gap[:], best[:], best[:, 0:1], None, ALU.subtract))
        dve.nop().then_inc(self.less, 1)
        steps.then(dve.tensor_scalar(self.part[:, 0, :], pick[:], 4, None, ALU.logical_shift_right),
                   dve.tensor_scalar(self.part[:, 1, :], pick[:], 15, None, ALU.bitwise_and))
        steps.then(dve.tensor_copy(self.partf[:], self.part[:]))
        hot = self.hot[:].rearrange("p s (k x) -> p s k x", x=TOPK)
        steps.then(*[dve.tensor_tensor(hot[:, g], self.partf[:, g, :].unsqueeze(2).broadcast_to([P, TOPK, TOPK]),
                                       self.m.iota16[:].unsqueeze(1).broadcast_to([P, TOPK, TOPK]), ALU.is_equal) for g in sides])
        steps.then(dve.tensor_tensor(hot, hot, self.topf[:].unsqueeze(2).broadcast_to([P, 2, TOPK, TOPK]), ALU.mult))
        steps.then(dve.tensor_reduce(self.found[:], hot, AX.X, ALU.add))
        steps.then(dve.scalar_tensor_tensor(out=self.num[:], in0=self.found[:, 0, :], scalar=float(NK), in1=self.found[:, 1, :],
                                            op0=ALU.mult, op1=ALU.add))
        expert = self.m.expert[:].rearrange("p t k -> p (t k)")[:, ds(j * TOPK, TOPK)]
        gate = self.m.gate[:].rearrange("p t k -> p (t k)")[:, ds(j * TOPK, TOPK)]
        steps.then(dve.tensor_scalar(expert, self.num[:], float(self.layer * NX), None, ALU.add))
        expd = value_of(dve, j + 1)
        apart(dve, self.passed)
        dve.wait_ge(self.expd, expd)
        steps.then(dve.tensor_reduce(self.tot[:], self.ex[:], AX.X, ALU.add))
        steps.then(dve.reciprocal(self.tot[:], self.tot[:]))
        steps.then(dve.tensor_scalar(gate, self.ex[:], self.tot[:, 0:1], None, ALU.mult))
        dve.nop().then_inc(self.chosen, 1)
        assert steps.n == self.STEPS, steps.n


def stage_experts(nc, m, a, layer):
    utab, vtab = (a[n].rearrange("l e d -> (l e) d") for n in ("peer_u", "peer_v"))
    g2 = m.mod[layer][:, 5 * KC:6 * KC, :]
    groups = (16, 16, 8)
    base = (0, 16, 32)
    turns = sum(groups) // 2
    with Stage(nc, f"exp{layer}") as s:
        ur = [s.sb(f"ur{k}", [P, D]) for k in range(GRP)]
        vr = [s.sb(f"vr{k}", [P, D]) for k in range(GRP)]
        ucol = s.sb("ucol", [P, GRP], U32)
        vcolx = s.sb("vcolx", [P, GRP], U32)
        dots = s.sb("dots", [P, GRP])
        act8 = s.sb("act8", [P, GRP])
        w8 = s.sb("w8", [P, GRP])
        diag = [s.sb(f"diag{k}", [P, P]) for k in range(GRP)]
        zero = s.sb("zero", [P, P])
        otok = s.sb("otok", [P, D])
        tmp = s.sb("tmp", [P, KC, TS])
        acc = [[s.bank(f"acc{i}{j}") for j in range(2)] for i in range(2)]
        psT = [s.bank(f"psT{i}") for i in range(2)]
        zeroed = s.sem("zero_ready")
        choice = Choice(s, m, layer, zeroed)
        ucoled = s.sem("ucol_ready")
        vcoled = s.sem("vcol_ready")
        uin = m.gathered[0:GRP]
        vin = m.gathered[GRP:2 * GRP]
        g0 = m.gathered_by
        m.gathered_by += 16 * sum(groups)
        dotted = s.sem("dotted", opened=True)
        acted = s.sem("gelu_ready", opened=True)
        weighed = s.sem("weights_ready", opened=True)
        diagd = s.sem("diag_ready", opened=True)
        mixed = s.sem("mixed", opened=True)
        summed = s.sem("tile_summed")
        okept = s.sem("tile_kept")
        oturned = s.sem("tile_turned")
        added = s.sem("tile_added")
        tmpd = s.sem("tmp_ready")
        gate = m.gate[:].rearrange("p t k -> p (t k)")
        with nc.Block() as block:
            @block.gpsimd
            def _(pool):
                experts = m.expert[:].rearrange("p t k -> p (t k)")

                def fetch(i, col, coled, land, table, rows, used):
                    past = value_of(pool, i * GRP + OPEN)
                    over, after = value_of(pool, i * 16 + g0), value_of(pool, i + 1)
                    apart(pool, zeroed)
                    for k in range(GRP):
                        pool.wait_ge(land[k], over)
                    pool.tensor_copy(col[:], experts[:, ds(i * GRP, GRP)]).then_inc(coled, 1)
                    apart(pool, zeroed)
                    pool.wait_ge(coled, after)
                    pool.wait_ge(used, past)
                    for k in range(GRP):
                        pool.indirect_dma_start(rows[k][:], None, table, bass.IndirectOffsetOnAxis(ap=col[:, k:k + 1], axis=0)).then_inc(land[k], 16)

                with pool.Fori(0, turns) as j:
                    chosen = value_of(pool, j + (OPEN + 1))
                    apart(pool, zeroed)
                    pool.wait_ge(choice.chosen, chosen)
                    for half in range(2):
                        fetch(j * 2 + half, ucol, ucoled, uin, utab, ur, dotted)
                        fetch(j * 2 + half, vcolx, vcoled, vin, vtab, vr, mixed)

            @block.tensor
            def _(pe):
                pe.wait_ge(zeroed, 1)
                for t in range(3):
                    b = t % 2
                    if t == 2:
                        pe.wait_ge(okept, 2)
                    for j in range(2):
                        pe.matmul(acc[b][j][:], zero[:], m.htok[:, 0, 0:512], start=True, stop=False, skip_group_check=True)
                    with pe.Fori(base[t], base[t] + groups[t]) as i:
                        for k in range(GRP):
                            pe.wait_ge(diagd, OPEN + i * GRP + (k + 1))
                            pe.wait_ge(vin[k], i * 16 + (g0 + 16))
                            pe.matmul(acc[b][0][:], diag[k][:], vr[k][:, 0:512], start=False, stop=False, skip_group_check=True)
                            pe.matmul(acc[b][1][:], diag[k][:], vr[k][:, 512:D], start=False, stop=False, skip_group_check=True).then_inc(mixed, 1)
                    for j in range(2):
                        pe.matmul(acc[b][j][:], zero[:], m.htok[:, 0, 0:512], start=False, stop=True, skip_group_check=True).then_inc(summed, 1)
                    pe.wait_ge(okept, 2 * t + 2)
                    pe.wait_ge(added, t)
                    for c in range(KC):
                        if t < 2:
                            ins = pe.transpose(psT[c // 4][:, (c % 4) * P:(c % 4 + 1) * P], otok[:, c * P:(c + 1) * P], m.ident[:])
                        else:
                            ins = pe.matmul(psT[0][:, c * TS:(c + 1) * TS], otok[:, c * P:(c + 1) * P], m.fold[:], start=True, stop=True)
                    ins.then_inc(oturned, 1)

            @block.scalar
            def _(act):

                def group(i):
                    act.wait_ge(dotted, OPEN + i * GRP + GRP)
                    act.wait_ge(weighed, OPEN + i)
                    act.activation(act8[:], dots[:], ACT.Gelu).then_inc(acted, 1)
                    act.wait_ge(weighed, OPEN + i + 1)
                    for k in range(GRP):
                        act.wait_ge(mixed, OPEN + i * GRP)
                        act.mul(diag[k][:], m.ident[:], w8[:, k:k + 1]).then_inc(diagd, 1)

                act.wait_ge(zeroed, 1)
                choice.take(act, 0)
                choice.exp(act, 0)
                for t in range(3):
                    with act.Fori(base[t] // 2, min(base[t] // 2 + groups[t] // 2, turns - 1)) as j:
                        choice.take(act, j + 1)
                        choice.exp(act, j + 1)
                        group(j * 2)
                        group(j * 2 + 1)
                    if t == 2:
                        group(2 * turns - 2)
                        group(2 * turns - 1)
                    for j in range(2):
                        act.wait_ge(summed, 2 * t + j + 1)
                        act.wait_ge(oturned, t)
                        act.copy(otok[:, j * 512:(j + 1) * 512], acc[t % 2][j][:]).then_inc(okept, 1)

            @block.vector
            def _(dve):
                dve.memset(zero[:], 0.0).then_inc(zeroed, 1)

                def group(i, t):
                    dve.wait_ge(acted, OPEN + i)
                    for k in range(GRP):
                        dve.wait_ge(uin[k], i * 16 + (g0 + 16))
                        dve.tensor_tensor_reduce(ur[k][:], ur[k][:], m.htok[:, t, :], 1.0, 0.0, ALU.mult, ALU.add,
                                                 dots[:, k:k + 1]).then_inc(dotted, 1)
                    dve.wait_ge(acted, OPEN + i + 1)
                    dve.wait_ge(diagd, OPEN + i * GRP)
                    dve.tensor_tensor(w8[:], act8[:], gate[:, ds(i * GRP, GRP)], ALU.mult).then_inc(weighed, 1)

                choice.choose(dve, 0)
                for t in range(3):
                    with dve.Fori(base[t] // 2, min(base[t] // 2 + groups[t] // 2, turns - 1)) as j:
                        choice.choose(dve, j + 1)
                        group(j * 2, t)
                        group(j * 2 + 1, t)
                    if t == 2:
                        group(2 * turns - 2, t)
                        group(2 * turns - 1, t)
                    dve.wait_ge(oturned, t + 1)
                    if t < 2:
                        for c in range(KC):
                            x = m.xT[:, c, t * P:(t + 1) * P]
                            ins = dve.scalar_tensor_tensor(out=x, in0=psT[c // 4][:, (c % 4) * P:(c % 4 + 1) * P], scalar=g2[:, c, 0:1],
                                                           in1=x, op0=ALU.mult, op1=ALU.add)
                        ins.then_inc(added, 1)
                    else:
                        dve.tensor_tensor(tmp[:].rearrange("p c (b j) -> p c b j", j=SQ),
                                          psT[0][:].rearrange("p (c b j) -> p c b j", c=KC, j=SQ),
                                          g2[:, :, 1:NCOND].unsqueeze(3).broadcast_to([P, KC, NSEQ, SQ]), ALU.mult).then_inc(tmpd, 1)
                        dve.wait_ge(tmpd, 1)
                        dve.tensor_tensor(m.xT[:, :, TP:T], m.xT[:, :, TP:T], tmp[:], ALU.add).then_inc(added, 1)


def stage_out(nc, m, a):
    with Stage(nc, "out") as s:
        rows = s.sb("rows", [P, 3, D])
        ps = [s.bank(f"ps{i}") for i in range(4)]
        turned = s.sem("turned")
        kept = s.sem("kept")
        stored = s.sem("stored")
        with nc.Block() as block:
            @block.tensor
            def _(pe):
                k = 0
                for t, (t0, n) in enumerate(TILES):
                    for g in range(2):
                        if k >= 4:
                            pe.wait_ge(kept, k - 3)
                        for q in range(4):
                            ins = pe.transpose(ps[k % 4][0:n, q * P:(q + 1) * P], m.hT[:, 4 * g + q, t0:t0 + n], m.ident[:])
                        ins.then_inc(turned, 1)
                        k += 1

            @block.scalar
            def _(act):
                for k in range(6):
                    t, g = k // 2, k % 2
                    n = TILES[t][1]
                    act.wait_ge(turned, k + 1)
                    act.copy(rows[0:n, t, g * 512:(g + 1) * 512], ps[k % 4][0:n, :]).then_inc(kept, 1)

            @block.sync
            def _(sp):
                yp = a["y_prompt"].rearrange("b t d -> (b t) d")
                for t, (t0, n) in enumerate(TILES):
                    sp.wait_ge(kept, 2 * t + 2)
                    dst = a["y_sample"].rearrange("b t d -> (b t) d") if t == 2 else yp[t0:t0 + n, :]
                    sp.dma_start(dst, rows[0:n, t, :]).then_inc(stored, 16)
                sp.wait_ge(stored, 48)


def peer(nc, m, a, layer):
    mod = m.mod[layer]
    stage_norm(nc, m, f"norm_ffn{layer}", mod[:, 4 * KC:5 * KC, :], mod[:, 3 * KC:4 * KC, :])
    stage_project(nc, m, f"peer_q{layer}", a["peer_wq"][layer], m.hT, m.proj[:], 8)
    stage_scores(nc, m, a, layer)
    stage_experts(nc, m, a, layer)


def build(nc, a, upto=99):
    m = Mem()
    with ExitStack() as ctx:
        def sb(c, name, shape, dt=F32):
            return c.enter_context(nc.sbuf_tensor(name, shape, dt))

        m.ident = sb(ctx, "ident", [P, P])
        m.ones = sb(ctx, "ones", [P, P])
        m.upto = sb(ctx, "upto", [P, P])
        m.after = sb(ctx, "after", [P, P])
        m.upto_s = sb(ctx, "upto_s", [TS, TS])
        m.after_s = sb(ctx, "after_s", [TS, TS])
        m.seq_s = sb(ctx, "seq_s", [TS, TS])
        m.far_p = sb(ctx, "far_p", [P, P])
        m.far_s = sb(ctx, "far_s", [96, SQ])
        m.headmask = sb(ctx, "headmask", [96, D_B])
        m.qsel = sb(ctx, "qsel", [96, SQ])
        m.fold = sb(ctx, "fold", [P, TS])
        m.iota16 = sb(ctx, "iota16", [P, TOPK])
        m.rowid = sb(ctx, "rowid", [P, 1])
        m.vcol = sb(ctx, "vcol", [P, 3 * P])
        m.cw = m.vcol[:, 256:256 + 96].rearrange("p (i c) -> p i c", c=CC)
        m.xT = sb(ctx, "xT", [P, KC, T])
        m.hT = sb(ctx, "hT", [P, KC, T])
        m.cT = sb(ctx, "cT", [P, KC, NCOND])
        m.mod = [sb(ctx, f"mod{l}", [P, 6 * KC, NCOND]) for l in range(2)]

        m.gathered_by = 0
        m.gathered = [nc.alloc_semaphore(f"gathered{i}") for i in range(16)]

        stage_setup(nc, m, a)
        stage_ada(nc, m, a, 0)
        mod = m.mod[0]
        stage_norm(nc, m, "norm_mix0", mod[:, KC:2 * KC, :], mod[:, 0:KC, :])
        with ExitStack() as c:
            m.proj = sb(c, "proj_ab", [P, 20, T])
            m.yT = sb(c, "y_ab", [P, KC, T])
            stage_project(nc, m, "ab_in", a["ab_w_in"][0], m.hT, m.proj[:], 10)
            stage_pool(nc, m, a)
            if upto >= 1:
                stage_attend_prompt(nc, m, a)
                stage_attend_sample(nc, m, a)
                stage_project(nc, m, "ab_out", a["ab_w_out"][0], m.yT, None, 4, residual=mod[:, 2 * KC:3 * KC, :])
        if upto >= 2:
            with ExitStack() as c:
                m.proj = sb(c, "peer_q0", [P, 2 * EH, T])
                m.htok = sb(c, "htok0", [P, 3, D])
                m.sc = sb(c, "scores0", [P, 40 * NK])
                m.expert = sb(c, "expert0", [P, 3, P], U32)
                m.gate = sb(c, "gate0", [P, 3, P])
                peer(nc, m, a, 0)
        mod = m.mod[1]
        if upto >= 3:
            stage_norm(nc, m, "norm_mix1", mod[:, KC:2 * KC, :], mod[:, 0:KC, :])
            with ExitStack() as c:
                m.dt = sb(c, "dt", [P, 3, SH])
                m.dta = sb(c, "dta", [P, 3, SH])
                m.proj = sb(c, "proj_ssd", [P, XC + CC, T])
                m.xbc = sb(c, "xbc", [P, CC, T])
                stage_project(nc, m, "ssd_in", a["ssd_w_in"][0], m.hT, m.proj[:], 20)
                stage_conv(nc, m, a)
                m.ytok = m.proj[:].rearrange("p c t -> p (c t)")[:, XC * T:XC * T + 3 * D_IN].rearrange("p (t n) -> p t n", t=3)
                with ExitStack() as c2:
                    m.btok = sb(c2, "btok", [P, 3, SG * NST])
                    m.xes = sb(c2, "xes", [TS, D_IN])
                    m.yoff = sb(c2, "yoff", [P, XC, TS])
                    with ExitStack() as c3:
                        m.xdt = sb(c3, "xdt", [P, 3, D_IN])
                        stage_scan(nc, m, a)
                    stage_state(nc, m, a)
                    m.yT2 = m.xbc_y = sb(c2, "y_ssd", [P, XC, T])
                    stage_gate(nc, m, a)
                    stage_project(nc, m, "ssd_out", a["ssd_w_out"][0], m.yT2, None, 4, kcn=XC, residual=mod[:, 2 * KC:3 * KC, :])
        if upto >= 4:
            with ExitStack() as c:
                m.proj = sb(c, "peer_q1", [P, 2 * EH, T])
                m.htok = sb(c, "htok1", [P, 3, D])
                m.sc = sb(c, "scores1", [P, 40 * NK])
                m.expert = sb(c, "expert1", [P, 3, P], U32)
                m.gate = sb(c, "gate1", [P, 3, P])
                peer(nc, m, a, 1)
        stage_norm(nc, m, "norm_out", m.vcol[:, 128:136], None)
        stage_out(nc, m, a)


INS = ["x_prompt", "x_sample", "cache_sb_k", "cache_sb_v", "state_pool", "state_conv", "state_ssm", "page_table",
       "c_prompt", "c_sample", "ada_w", "ada_b", "norm_mix_g", "norm_ffn_g", "norm_out_g", "ab_w_in", "ab_w_out",
       "pool_w", "pool_scale", "sb_bias", "ssd_w_in", "ssd_conv_w", "ssd_conv_b", "ssd_dt_bias", "ssd_a_log", "ssd_d",
       "ssd_norm_g", "ssd_w_out", "peer_wq", "peer_k1", "peer_k2", "peer_u", "peer_v"]
OUTS = [("y_prompt", (1, TP, D)), ("y_sample", (NSEQ, SQ, D)),
        ("k_prompt", (1, 1, TP, HB, HD)), ("v_prompt", (1, 1, TP, HB, HD)),
        ("k_sample", (1, NSEQ, SQ, HB, HD)), ("v_sample", (1, NSEQ, SQ, HB, HD)),
        ("pool_prompt", (1, 1, NBUF, D_A)), ("pool_sample", (1, NSEQ, NBUF, D_A)),
        ("conv_prompt", (1, 1, 3, CONV)), ("conv_sample", (1, NSEQ, 3, CONV)),
        ("ssm_prompt", (1, 1, SH, 64, NST)), ("ssm_sample", (1, NSEQ, SH, 64, NST))]


def kernel(**inputs):
    import numpy as np
    import concourse.bacc as bacc
    from concourse.bass_utils import run_bass_kernel_spmd

    nc = bacc.Bacc("TRN2", target_bir_lowering=False, num_devices=1)
    arrays, aps = {}, {}
    for name in INS:
        x = np.ascontiguousarray(inputs[name])
        arrays[f"in_{name}_dram"] = x
        aps[name] = nc.dram_tensor(f"in_{name}_dram", x.shape, mybir.dt.from_np(x.dtype), kind="ExternalInput").ap()
    for name, shape in OUTS:
        aps[name] = nc.dram_tensor(f"out_{name}_dram", shape, F32, kind="ExternalOutput").ap()
    build(nc, aps)
    r = run_bass_kernel_spmd(nc, [arrays], core_ids=[0])
    return tuple(r.results[0][f"out_{name}_dram"] for name, _ in OUTS)
```
